# Optimizing a Trainium2 kernel written in Bass

```python
import jax, jax.numpy as jnp
from jax import lax
import numpy as np

D_MODEL = 1024
BATCH = 1
SEQ = 512
DEPTH = 1

CHUNK = 64
Q_BLOCK = 128
EPS = 1e-6
N_MEM = 256
MLA_HEADS = 8
MLA_Q_RANK = 256
MLA_KV_RANK = 128
MLA_NOPE_DIM = 64
MLA_ROPE_DIM = 32
MLA_V_DIM = 64
MLA_QK_DIM = MLA_NOPE_DIM + MLA_ROPE_DIM
MLA_WIDTH = MLA_HEADS * MLA_V_DIM
ROPE_THETA = 10000.0
CONV_WIDTH = D_MODEL - MLA_WIDTH
CONV_KERNEL = 31
IN_SPLITS = [MLA_Q_RANK, MLA_Q_RANK + MLA_KV_RANK, MLA_Q_RANK + MLA_KV_RANK + MLA_ROPE_DIM]
IN_COLS = MLA_Q_RANK + MLA_KV_RANK + MLA_ROPE_DIM + 2 * CONV_WIDTH
MEM_HEADS = 4
MEM_HEAD_DIM = D_MODEL // MEM_HEADS
PEER_HEADS = 8
PEER_N_KEYS = 128
PEER_N_EXPERTS = PEER_N_KEYS * PEER_N_KEYS
PEER_KEY_DIM = 256
PEER_HALF_DIM = PEER_KEY_DIM // 2
PEER_TOPK = 16
PEER_TOKEN_BLOCK = 128

kernel_name = 'hybrid_mla_conformer_peer_block'

def rms_norm(x, g):
    xf = x.astype(jnp.float32)
    y = xf * lax.rsqrt(jnp.mean(xf * xf, axis=-1, keepdims=True) + EPS)
    return (y * g.astype(jnp.float32)).astype(x.dtype)

def layer_norm(x, g, b):
    xf = x.astype(jnp.float32)
    mu = jnp.mean(xf, axis=-1, keepdims=True)
    xc = xf - mu
    var = jnp.mean(xc * xc, axis=-1, keepdims=True)
    y = xc * lax.rsqrt(var + EPS) * g.astype(jnp.float32) + b.astype(jnp.float32)
    return y.astype(x.dtype)

def rope_tables(seq_len, dim):
    inv = 1.0 / (ROPE_THETA ** (jnp.arange(0, dim, 2, dtype=jnp.float32) / dim))
    ang = jnp.arange(seq_len, dtype=jnp.float32)[:, None] * inv[None, :]
    return jnp.cos(ang), jnp.sin(ang)

def apply_rope(x, cos, sin):
    x1, x2 = jnp.split(x, 2, axis=-1)
    c = cos.astype(x.dtype)
    s = sin.astype(x.dtype)
    return jnp.concatenate([x1 * c - x2 * s, x1 * s + x2 * c], axis=-1)

def chunk_causal_attention(q, k, v):
    B, S, H, Dqk = q.shape
    nb = S // Q_BLOCK
    scale = Dqk ** -0.5
    qb = q.reshape(B, nb, Q_BLOCK, H, Dqk).transpose(1, 0, 2, 3, 4)
    k_chunk = jnp.arange(S) // CHUNK

    def one_block(args):
        blk, q_blk = args
        s = jnp.einsum('bqhd,bkhd->bhqk', q_blk, k).astype(jnp.float32) * scale
        q_chunk = (blk * Q_BLOCK + jnp.arange(Q_BLOCK)) // CHUNK
        allowed = k_chunk[None, :] <= q_chunk[:, None]
        s = jnp.where(allowed, s, -1e30)
        p = jax.nn.softmax(s, axis=-1).astype(v.dtype)
        return jnp.einsum('bhqk,bkhd->bqhd', p, v)

    out = lax.map(one_block, (jnp.arange(nb), qb))
    return out.transpose(1, 0, 2, 3, 4).reshape(B, S, H, v.shape[-1])

def hybrid_mixer(xn, w_in, q_latent_g, w_q_up, kv_latent_g, w_kv_up,
                 conv_w, conv_b, conv_ln_g, conv_ln_b, w_mix_out):
    B, S, _ = xn.shape
    proj = xn @ w_in
    c_q, c_kv, k_r, conv_in = jnp.split(proj, IN_SPLITS, axis=-1)

    q = (rms_norm(c_q, q_latent_g) @ w_q_up).reshape(B, S, MLA_HEADS, MLA_QK_DIM)
    q_nope, q_rope = q[..., :MLA_NOPE_DIM], q[..., MLA_NOPE_DIM:]
    kv = (rms_norm(c_kv, kv_latent_g) @ w_kv_up).reshape(B, S, MLA_HEADS, MLA_NOPE_DIM + MLA_V_DIM)
    k_nope, v = kv[..., :MLA_NOPE_DIM], kv[..., MLA_NOPE_DIM:]
    cos, sin = rope_tables(S, MLA_ROPE_DIM)
    q_rope = apply_rope(q_rope, cos[:, None, :], sin[:, None, :])
    k_rope = apply_rope(k_r, cos, sin)
    q_full = jnp.concatenate([q_nope, q_rope], axis=-1)
    k_full = jnp.concatenate(
        [k_nope, jnp.broadcast_to(k_rope[:, :, None, :], (B, S, MLA_HEADS, MLA_ROPE_DIM))], axis=-1)
    attn = chunk_causal_attention(q_full, k_full, v).reshape(B, S, MLA_WIDTH)

    val, gate = jnp.split(conv_in, 2, axis=-1)
    u = val * jax.nn.sigmoid(gate)
    u = jnp.pad(u, ((0, 0), (CONV_KERNEL - 1, 0), (0, 0)))
    u = lax.conv_general_dilated(u, conv_w.astype(u.dtype), window_strides=(1,), padding='VALID',
                                 dimension_numbers=('NWC', 'WIO', 'NWC'),
                                 feature_group_count=CONV_WIDTH) + conv_b
    u = jax.nn.silu(layer_norm(u, conv_ln_g, conv_ln_b))

    return jnp.concatenate([attn, u], axis=-1) @ w_mix_out

def memory_cross_attention(hn, mem, mem_kv_norm_g, w_mem_q, w_mem_kv, w_mem_out):
    B, S, _ = hn.shape
    M = mem.shape[1]
    q = (hn @ w_mem_q).reshape(B, S, MEM_HEADS, MEM_HEAD_DIM)
    kv = rms_norm(mem, mem_kv_norm_g) @ w_mem_kv
    k, v = jnp.split(kv, 2, axis=-1)
    k = k.reshape(B, M, MEM_HEADS, MEM_HEAD_DIM)
    v = v.reshape(B, M, MEM_HEADS, MEM_HEAD_DIM)
    s = jnp.einsum('bshd,bmhd->bhsm', q, k).astype(jnp.float32) * (MEM_HEAD_DIM ** -0.5)
    p = jax.nn.softmax(s, axis=-1).astype(v.dtype)
    o = jnp.einsum('bhsm,bmhd->bshd', p, v).reshape(B, S, D_MODEL)
    return o @ w_mem_out

def peer_channel_mixer(hn, w_peer_query, peer_sub_keys, peer_u, peer_v):
    B, S, D = hn.shape
    q = (hn @ w_peer_query).reshape(B, S, PEER_HEADS, 2, PEER_HALF_DIM)
    sub_scores = jnp.einsum('bshpd,hpnd->bshpn', q, peer_sub_keys).astype(jnp.float32)
    top_s, top_i = lax.top_k(sub_scores, PEER_TOPK)
    cand_s = top_s[..., 0, :, None] + top_s[..., 1, None, :]
    cand_i = top_i[..., 0, :, None] * PEER_N_KEYS + top_i[..., 1, None, :]
    cand_s = cand_s.reshape(B, S, PEER_HEADS, PEER_TOPK * PEER_TOPK)
    cand_i = cand_i.reshape(B, S, PEER_HEADS, PEER_TOPK * PEER_TOPK)
    best_s, best_pos = lax.top_k(cand_s, PEER_TOPK)
    expert_idx = jnp.take_along_axis(cand_i, best_pos, axis=-1)
    gates = jax.nn.softmax(best_s, axis=-1)

    T = B * S
    nb = T // PEER_TOKEN_BLOCK
    xt = hn.reshape(nb, PEER_TOKEN_BLOCK, D)
    it = expert_idx.reshape(nb, PEER_TOKEN_BLOCK, PEER_HEADS, PEER_TOPK)
    gt = gates.reshape(nb, PEER_TOKEN_BLOCK, PEER_HEADS, PEER_TOPK)

    def one_block(args):
        xb, ib, gb = args
        u = peer_u[ib]
        a = jax.nn.gelu(jnp.einsum('thkd,td->thk', u, xb), approximate=False)
        w = (a.astype(jnp.float32) * gb).astype(xb.dtype)
        v = peer_v[ib]
        return jnp.einsum('thk,thkd->td', w, v)

    return lax.map(one_block, (xt, it, gt)).reshape(B, S, D)

def _normal(key, shape, scale):
    return jax.random.normal(key, shape, dtype=jnp.float32) * scale

def _gain(key, shape):
    return 1.0 + 0.01 * jax.random.normal(key, shape, dtype=jnp.float32)

def setup_inputs(seed: int = 0) -> dict:
    key = jax.random.key(seed)
    ks = jax.random.split(key, 24)
    L = DEPTH
    return {
        'x': _normal(ks[0], (BATCH, SEQ, D_MODEL), 1.0),
        'mem': _normal(ks[1], (BATCH, N_MEM, D_MODEL), 1.0),
        'norm_mix_g': _gain(ks[2], (L, D_MODEL)),
        'w_in': _normal(ks[3], (L, D_MODEL, IN_COLS), D_MODEL ** -0.5),
        'q_latent_g': _gain(ks[4], (L, MLA_Q_RANK)),
        'w_q_up': _normal(ks[5], (L, MLA_Q_RANK, MLA_HEADS * MLA_QK_DIM), MLA_Q_RANK ** -0.5),
        'kv_latent_g': _gain(ks[6], (L, MLA_KV_RANK)),
        'w_kv_up': _normal(ks[7], (L, MLA_KV_RANK, MLA_HEADS * (MLA_NOPE_DIM + MLA_V_DIM)), MLA_KV_RANK ** -0.5),
        'conv_w': _normal(ks[8], (L, CONV_KERNEL, 1, CONV_WIDTH), CONV_KERNEL ** -0.5),
        'conv_b': _normal(ks[9], (L, CONV_WIDTH), 0.01),
        'conv_ln_g': _gain(ks[10], (L, CONV_WIDTH)),
        'conv_ln_b': _normal(ks[11], (L, CONV_WIDTH), 0.01),
        'w_mix_out': _normal(ks[12], (L, D_MODEL, D_MODEL), D_MODEL ** -0.5),
        'norm_mem_g': _gain(ks[13], (L, D_MODEL)),
        'mem_kv_norm_g': _gain(ks[14], (L, D_MODEL)),
        'w_mem_q': _normal(ks[15], (L, D_MODEL, D_MODEL), D_MODEL ** -0.5),
        'w_mem_kv': _normal(ks[16], (L, D_MODEL, 2 * D_MODEL), D_MODEL ** -0.5),
        'w_mem_out': _normal(ks[17], (L, D_MODEL, D_MODEL), D_MODEL ** -0.5),
        'norm_ffn_g': _gain(ks[18], (L, D_MODEL)),
        'w_peer_query': _normal(ks[19], (L, D_MODEL, PEER_HEADS * PEER_KEY_DIM), D_MODEL ** -0.5),
        'peer_sub_keys': _normal(ks[20], (L, PEER_HEADS, 2, PEER_N_KEYS, PEER_HALF_DIM), PEER_HALF_DIM ** -0.5),
        'peer_u': _normal(ks[21], (L, PEER_N_EXPERTS, D_MODEL), D_MODEL ** -0.5),
        'peer_v': _normal(ks[22], (L, PEER_N_EXPERTS, D_MODEL), 0.5),
        'final_norm_g': _gain(ks[23], (D_MODEL,)),
    }

def reference(x, mem, norm_mix_g, w_in, q_latent_g, w_q_up, kv_latent_g, w_kv_up,
              conv_w, conv_b, conv_ln_g, conv_ln_b, w_mix_out,
              norm_mem_g, mem_kv_norm_g, w_mem_q, w_mem_kv, w_mem_out,
              norm_ffn_g, w_peer_query, peer_sub_keys, peer_u, peer_v, final_norm_g):
    h = x
    for l in range(DEPTH):
        h = h + hybrid_mixer(rms_norm(h, norm_mix_g[l]), w_in[l], q_latent_g[l], w_q_up[l],
                             kv_latent_g[l], w_kv_up[l], conv_w[l], conv_b[l],
                             conv_ln_g[l], conv_ln_b[l], w_mix_out[l])
        h = h + memory_cross_attention(rms_norm(h, norm_mem_g[l]), mem, mem_kv_norm_g[l],
                                       w_mem_q[l], w_mem_kv[l], w_mem_out[l])
        h = h + peer_channel_mixer(rms_norm(h, norm_ffn_g[l]), w_peer_query[l],
                                   peer_sub_keys[l], peer_u[l], peer_v[l])
    return rms_norm(h, final_norm_g)


_drawn_inputs = setup_inputs


def setup_inputs(seed=0):
    import zlib

    import numpy as np

    out = dict(_drawn_inputs(seed))
    spreads = {}
    factors = {'norm_mix_g': 3.247,
     'q_latent_g': 7.953,
     'kv_latent_g': 5.482,
     'conv_ln_g': 8.942,
     'conv_ln_b': 3.508,
     'norm_mem_g': 6.632,
     'mem_kv_norm_g': 5.357,
     'final_norm_g': 195.626,
     'conv_b': 5.415,
     'norm_ffn_g': 21.713}
    for name, (base, spread) in spreads.items():
        noise = np.random.default_rng([zlib.crc32(name.encode()), seed]).standard_normal(out[name].shape)
        drawn = base * np.exp(spread * noise) if base else spread * noise
        out[name] = __import__('jax').numpy.asarray(drawn.astype(out[name].dtype))
    for name, factor in factors.items():
        out[name] = (out[name] * factor).astype(out[name].dtype)
    return out
```

```python
import concourse.bass as bass
from concourse import mybir
from contextlib import ExitStack

P = 128
D = 1024
KT = D // P
SEQ = 512
TILES = SEQ // P
EPS = 1e-6
N_MEM = 256
MEM_TILES = N_MEM // P
HEADS, NOPE, ROPE, VDIM = 8, 64, 32, 64
QK = NOPE + ROPE
HALF = ROPE // 2
Q_RANK, KV_RANK = 256, 128
LATENT = Q_RANK + KV_RANK + ROPE
CONV, TAPS = 512, 31
CT = CONV // P
HIST = TAPS - 1
MEM_HEADS, MEM_DIM = 4, 256
PEER_HEADS, KEYS, TOPK = 8, 128, 16
SETS = 2 * PEER_HEADS
SLOTS = PEER_HEADS * TOPK
RING = 8
GROUPS = SLOTS // RING
WRING = 7
LOWEST = -3.0e38

BY_PE = (0, 1, 3, 4, 6)
BY_DVE = (2, 5, 7)

W_TILE = ([("w_in", k, 0, LATENT) for k in range(KT)] + [("w_in", k, LATENT, 1024) for k in range(KT)]
          + [("w_mix_out", k, 0, 1024) for k in range(KT)] + [("w_mem_q", k, 0, 1024) for k in range(KT)]
          + [("w_mem_out", k, 0, 1024) for k in range(KT)]
          + [("w_peer_query", k, 1024 * n, 1024) for n in range(2) for k in range(KT)])
W_MEMORY = [("w_mem_kv", k, 1024 * n, 1024) for n in range(2) for k in range(KT)]
PER_TILE = len(W_TILE)
assert PER_TILE % WRING == 0

T_MEMORY = 4
T_LATENT, T_CONV, T_Q, T_K, T_P, T_ATTN = 0, 1, 2, 4, 6, 14
T_HMEM, T_QMEM, T_PMEM, T_OMEM, T_HFFN, T_QPEER, T_TILE = 16, 18, 20, 22, 24, 26, 30

PLAN = [("do", "inputs"), ("U", 0, 1), ("do", "project"), ("U", 1, 2), ("do", "latents"), ("do", "conv_input"),
        ("U", 3, 1), ("do", "queries_keys"), ("U", 4, 1)]
for _h in range(HEADS):
    PLAN += [("do", ("head", _h)), ("U", 5 + _h, 1)]
PLAN += [("do", "attended"), ("do", "conv_norm"), ("U", 13, 1), ("do", "mix_out"), ("U", 14, 2), ("do", "mem_norm"),
         ("V", 0, 1), ("do", "mem_query"), ("V", 1, 1), ("do", "mem_scores"), ("do", "mem_values"), ("V", 2, 1),
         ("do", "mem_out"), ("V", 3, 1), ("do", "peer_norm"), ("V", 4, 1), ("do", ("peer_query", 0)), ("V", 5, 1),
         ("do", ("peer_query", 1)), ("V", 6, 1), ("do", "sub_scores")]
for _q in range(4):
    PLAN += [("do", ("sub_topk", _q)), ("V", 7 + _q, 1)]
PLAN += [("do", "candidates"), ("V", 11, 1), ("do", ("best", 0)), ("do", ("best", 1)), ("V", 12, 1),
         ("do", "gates"), ("V", 13, 1), ("do", "indices"), ("V", 14, 1), ("do", "publish"), ("V", 15, 1)]


def of_tile(t, per_tile, n):
    return t * per_tile + n


def build(nc, dram, out):
    f32, i32, u32 = mybir.dt.float32, mybir.dt.int32, mybir.dt.uint32
    ALU, ACT, AX = mybir.AluOpType, mybir.ActivationFunctionType, mybir.AxisListType
    MLA_SCALE, MEM_SCALE = QK ** -0.5, MEM_DIM ** -0.5

    ctx = ExitStack()
    with ctx:
        def sb(name, shape, dt=f32):
            return ctx.enter_context(nc.sbuf_tensor(name, shape, dt))

        def sem(name):
            return ctx.enter_context(nc.semaphore(name))

        ring = sb("ring", [P, RING, D])
        wring = sb("wring", [P, WRING, 1024])
        key_cache = sb("key_cache", [P, HEADS, SEQ])
        value_cache = sb("value_cache", [P, TILES, HEADS * VDIM])
        mem_kT = sb("mem_kT", [P, KT, N_MEM])
        mem_v = sb("mem_v", [P, MEM_TILES, D])
        sub_keysT = sb("sub_keysT", [P, SETS, KEYS])
        w_q_up = sb("w_q_up", [P, 2, HEADS * QK])
        w_kv_up = sb("w_kv_up", [P, HEADS * (NOPE + VDIM)])
        ffn_g = sb("ffn_g", [P, D])
        final_g = sb("final_g", [P, D])
        latent_g = sb("latent_g", [P, Q_RANK + KV_RANK])
        mix_gT = sb("mix_gT", [P, KT])
        mem_gT = sb("mem_gT", [P, KT])
        memkv_gT = sb("memkv_gT", [P, KT])
        conv_wT = sb("conv_wT", [P, CT, TAPS])
        conv_p = sb("conv_p", [P, 3, CT])
        ident = sb("ident", [P, P])
        mean_w = sb("mean_w", [P, P])
        rope = sb("rope", [P, 2, HALF])
        iota = sb("iota", [P, TOPK])
        eps = sb("eps", [P, 1])
        mask = sb("mask", [P, SEQ])
        h = sb("h", [P, D])
        hn = sb("hn", [P, D])
        row_a = sb("row_a", [P, D])
        row_b = sb("row_b", [P, D])
        ta = sb("ta", [P, KT, P])
        tb = sb("tb", [P, KT, P])
        arena = sb("arena", [P, 6144])
        lat_row = sb("lat_row", [P, Q_RANK + KV_RANK])
        lat_t = sb("lat_t", [P, 3, P])
        u_t = sb("u_t", [P, CT, HIST + P])
        conv_acc = sb("conv_acc", [P, CT, P])
        y_acc = sb("y_acc", [P, D])
        y_row = sb("y_row", [P, D])
        diag = sb("diag", [P, len(BY_PE), P])
        small = sb("small", [P, 64])
        a_group = sb("a_group", [P, RING])
        a_all = sb("a_all", [P, SLOTS])
        gelu_a = sb("gelu_a", [P, SLOTS])
        gate = sb("gate", [P, SLOTS])
        weight = sb("weight", [P, SLOTS])
        idx = sb("idx", [P, SLOTS], i32)
        idx_group = sb("idx_group", [P, 2, RING], i32)
        top_v = sb("top_v", [P, SETS, TOPK])
        top_i = sb("top_i", [P, SETS, TOPK], u32)
        best_v = sb("best_v", [P, PEER_HEADS, TOPK])
        best_p = sb("best_p", [P, PEER_HEADS, TOPK], u32)

        def region(first, size):
            return arena[:, first:first + size]

        qk = region(0, 864).rearrange("p (h d) -> p h d", d=QK)
        kfull = region(864, 768).rearrange("p (h d) -> p h d", d=QK)
        q_t = region(1632, 1024).rearrange("p (h t) -> p h t", t=P)
        probs = region(2656, 1024).rearrange("p (b k) -> p b k", k=SEQ)
        probs_t = region(3680, 1024).rearrange("p (b j t) -> p b j t", b=2, t=P)
        sig = region(4704, 512)
        u_row = region(5216, 512)
        qp_t = region(0, 2048).rearrange("p (s t) -> p s t", t=P)
        onehot = region(0, 2048).rearrange("p (h k a) -> p h k a", h=8, k=16)
        scores = region(2048, 2048).rearrange("p (s n) -> p s n", n=KEYS)
        top_f = region(2048, 256).rearrange("p (s k) -> p s k", k=TOPK)
        pos_f = region(2304, 256).rearrange("p (c s) -> p c s", c=2)
        pos_u = region(2560, 256).bitcast(u32).rearrange("p (c s) -> p c s", c=2)
        picked = region(2816, 256).rearrange("p (c s) -> p c s", c=2)
        cand = region(4096, 2048).rearrange("p (h a b) -> p h a b", h=8, a=16)
        cand_h = region(4096, 2048).rearrange("p (h c) -> p h c", h=8)
        peer_row = region(4096, 1024)
        memn_t = region(0, 2048).rearrange("p (k m) -> p k m", m=N_MEM)
        mem_k_row = region(2048, 2048).rearrange("p (m d) -> p m d", d=D)
        ss, root, rinv = small[:, 0:4], small[:, 4:8], small[:, 8:12]
        mx, nmx, lsum, linv = small[:, 16:24], small[:, 24:32], small[:, 32:40], small[:, 40:48]
        f_ss, f_root, f_rinv = small[:, 48:49], small[:, 49:50], small[:, 50:51]
        m_ss, m_root, m_rinv = small[:, 52:54], small[:, 54:56], small[:, 56:58]
        rmix = small[:, 58:59]
        kv2 = small[:, 60:62]
        conv_root = row_b[:, 0:P]
        conv_x = row_b[:, 512:1024].rearrange("p (c t) -> p c t", t=P)

        acc = ctx.enter_context(nc.psum_tensor("acc", [P, D], f32))
        g = ctx.enter_context(nc.psum_tensor("g", [P, 4, 512], f32))
        tp = ctx.enter_context(nc.psum_tensor("tp", [P, 2, 512], f32))
        g01 = g[:, 0:2, :].rearrange("p b n -> p (b n)")
        g23 = g[:, 2:4, :].rearrange("p b n -> p (b n)")
        g12 = g[:, 1:3, :].rearrange("p b n -> p (b n)")

        loaded = sem("constants_loaded")
        input_landed = sem("input_landed")
        w_landed = [sem(f"weights_landed_{s}") for s in range(WRING)]
        w_used = sem("weights_used")
        landed = [sem(f"rows_landed_{r}") for r in range(RING)]
        granted = sem("pool_granted")
        dve_granted = sem("dve_granted")
        act_granted = sem("act_granted")
        idx_staged = sem("indices_staged")
        idx_ready = sem("indices_ready")
        u_used = sem("u_rows_used")
        v_used_pe = sem("v_rows_used_by_pe")
        v_used_dve = sem("v_rows_used_by_dve")
        a_copied = sem("a_copied")
        gelu_ready = sem("gelu_ready")
        weight_ready = sem("weight_ready")
        diag_ready = sem("diag_ready")
        y_ready = sem("y_ready")
        y_root_ready = sem("y_root_ready")
        y_normed = sem("y_normed")
        stored = sem("y_row_free")
        h_taken = sem("h_taken")
        filled = sem("transposed_bank_filled")
        drained = sem("transposed_bank_drained")
        dve_step = sem("dve_step")
        act_step = sem("act_step")
        zeroed = sem("caches_zeroed")
        memT_scaled = sem("memory_scaled")
        mem_root = sem("memory_root")
        mem_rinv_ready = sem("memory_rinv_ready")
        mem_saved = sem("memory_saved")
        x_scaled = sem("x_scaled")
        root_ready = sem("root_ready")
        rmix_ready = sem("input_rinv_ready")
        k_rope_copied = sem("k_rope_copied")
        lat_normed = sem("latents_normed")
        sig_ready = sem("sigmoid_ready")
        u_ready = sem("conv_row_ready")
        up_ready = sem("up_ready")
        up_saved = sem("up_saved")
        roped = sem("roped")
        s_ready = sem("attention_scores_ready")
        s_masked = sem("attention_scores_masked")
        p_ready = sem("attention_probs_ready")
        pv_done = sem("attention_values_done")
        attn_ready = sem("attention_row_ready")
        hist_read = sem("conv_history_saved")
        conv_done = sem("conv_done")
        stat_ready = sem("conv_stat_ready")
        centred = sem("conv_centred")
        squared = sem("conv_squared")
        conv_rooted = sem("conv_rooted")
        conv_normed = sem("conv_normed")
        cat_ready = sem("conv_output_ready")
        h_mixed = sem("h_mixed")
        h_row = sem("memory_input_row_ready")
        mq_saved = sem("memory_query_saved")
        ms_ready = sem("memory_scores_ready")
        ms_max = sem("memory_scores_max")
        mp_ready = sem("memory_probs_ready")
        mo_ready = sem("memory_values_ready")
        mo_row = sem("memory_row_ready")
        h_remembered = sem("h_remembered")
        hn_ready = sem("expert_input_ready")
        pq_saved = sem("peer_query_saved")
        sub_ready = sem("sub_scores_ready")
        sub_saved = sem("sub_scores_saved")
        best_shifted = sem("best_shifted")
        best_exp = sem("best_exp")

        block = ctx.enter_context(nc.Block())

        def hold(eng, tick, s, value):
            eng.wait_ge(s, value)
            if not isinstance(value, int):
                eng.sem_inc(tick, 1)

        def chunk_number(t, n):
            return len(W_MEMORY) + PER_TILE * t + n

        def place(n):
            return (len(W_MEMORY) + n) % WRING

        def landed_value(t, n):
            return 16 * (PER_TILE // WRING) * t + 16 * ((len(W_MEMORY) + n) // WRING + 1)

        @block.sync
        def _(sp):
            consts = [(memn_t, dram["memT"]), (memkv_gT[:, :], dram["memkv_gT"]),
                      (row_a[:, :], dram["mem"][0:P, :]), (row_b[:, :], dram["mem"][P:2 * P, :]),
                      (ident[:, :], dram["ident"]), (mix_gT[:, :], dram["mix_gT"]), (mem_gT[:, :], dram["mem_gT"]),
                      (latent_g[:, 0:Q_RANK], dram["q_latent_g"].to_broadcast([P, Q_RANK])),
                      (latent_g[:, Q_RANK:], dram["kv_latent_g"].to_broadcast([P, KV_RANK])),
                      (conv_wT[:, :, :], dram["conv_wT"]), (conv_p[:, :, :], dram["conv_p"]),
                      (iota[:, :], dram["iota"].to_broadcast([P, TOPK])),
                      (w_q_up[:, :, :], dram["w_q_up"].rearrange("(k p) n -> p k n", p=P)),
                      (w_kv_up[:, :], dram["w_kv_up"]),
                      (ffn_g[:, :], dram["norm_ffn_g"].to_broadcast([P, D])),
                      (final_g[:, :], dram["final_norm_g"].to_broadcast([P, D])),
                      (sub_keysT[:, :, :], dram["sub_keysT"])]
            for dst, src in consts:
                sp.dma_start(dst, src).then_inc(loaded, 16)
            assert len(consts) == 17

            def weight_dma(spec, slot):
                name, k, col, cols = spec
                sp.dma_start(wring[:, slot, 0:cols], dram[name][k * P:(k + 1) * P, col:col + cols]) \
                  .then_inc(w_landed[slot], 16)

            def inputs(t):
                sp.dma_start(h[:, :], dram["x"][bass.ds(t * P, P), :]).then_inc(input_landed, 16)
                sp.dma_start(ta[:, :, :], dram["xT"][bass.ds(t * P, P), :, :]).then_inc(input_landed, 16)
                sp.dma_start(mask[:, :], dram["mask"][bass.ds(t * P, P), :]).then_inc(input_landed, 16)
                sp.dma_start(rope[:, :, :], dram["rope"][bass.ds(t * P, P), :, :]).then_inc(input_landed, 16)

            def tile_weights(t):
                for n, spec in enumerate(W_TILE):
                    sp.wait_ge(w_used, chunk_number(t, n) - WRING + 1)
                    weight_dma(spec, place(n))

            for m, spec in enumerate(W_MEMORY):
                if m >= WRING:
                    sp.wait_ge(w_used, m - WRING + 1)
                weight_dma(spec, m % WRING)
                if m == 4:
                    inputs(0)
            tile_weights(0)
            with sp.Fori(1, TILES) as t:
                sp.wait_ge(h_taken, t)
                sp.wait_ge(idx_ready, t)
                inputs(t)
                tile_weights(t)
            sp.wait_ge(stored, 16 * (TILES + 1))

        @block.gpsimd
        def _(pool):
            pool.memset(key_cache[:, :, :], 0.0).then_inc(zeroed, 1)
            pool.memset(value_cache[:, :, :], 0.0).then_inc(zeroed, 1)
            pool.memset(u_t[:, :, :], 0.0).then_inc(zeroed, 1)
            pool.memset(mean_w[:, :], 1.0 / CONV).then_inc(zeroed, 1)
            pool.memset(eps[:, :], EPS).then_inc(zeroed, 1)

            def stage(t, group, turn):
                pool.tensor_copy(idx_group[:, turn, :], idx[:, bass.ds((group % GROUPS if isinstance(group, int) else group) * RING, RING)]) \
                    .then_inc(idx_staged, 1)

            def fetch(table, r, turn):
                pool.indirect_dma_start(ring[:, r, :], None, dram[table],
                                        bass.IndirectOffsetOnAxis(ap=idx_group[:, turn, r:r + 1], axis=0)) \
                    .then_inc(landed[r], 16)

            def u_group(t, group, turn, first=False):
                stage(t, group, turn)
                hold(pool, granted, idx_staged, of_tile(t, 2 * GROUPS, group + 1))
                for r in range(RING):
                    if first:
                        if not isinstance(t, int) or t:
                            if r in BY_PE:
                                hold(pool, granted, v_used_pe,
                                     of_tile(t, GROUPS * len(BY_PE), BY_PE.index(r) + 1 - len(BY_PE)))
                            else:
                                hold(pool, granted, v_used_dve,
                                     of_tile(t, GROUPS * len(BY_DVE), BY_DVE.index(r) + 1 - len(BY_DVE)))
                    else:
                        hold(pool, granted, u_used, of_tile(t, SLOTS, (group - 1) * RING + r + 1))
                    fetch("peer_u", r, turn)

            def v_group(t, group, turn, first=False):
                stage(t, group, turn)
                hold(pool, granted, idx_staged, of_tile(t, 2 * GROUPS, GROUPS + group + 1))
                for r in range(RING):
                    if first:
                        hold(pool, granted, u_used, of_tile(t, SLOTS, SLOTS - RING + r + 1))
                    elif r in BY_PE:
                        hold(pool, granted, v_used_pe,
                             of_tile(t, GROUPS * len(BY_PE), (group - 1) * len(BY_PE) + BY_PE.index(r) + 1))
                    else:
                        hold(pool, granted, v_used_dve,
                             of_tile(t, GROUPS * len(BY_DVE), (group - 1) * len(BY_DVE) + BY_DVE.index(r) + 1))
                    fetch("peer_v", r, turn)

            def after_first(t):
                u_group(t, 1, 1)
                with pool.Fori(1, GROUPS // 2) as j:
                    u_group(t, j * 2, 0)
                    u_group(t, j * 2 + 1, 1)
                v_group(t, 0, 0, first=True)
                v_group(t, 1, 1)
                with pool.Fori(1, GROUPS // 2) as j:
                    v_group(t, j * 2, 0)
                    v_group(t, j * 2 + 1, 1)

            pool.wait_ge(idx_ready, 1)
            u_group(0, 0, 0, first=True)
            with pool.Fori(0, TILES - 1) as t:
                after_first(t)
                hold(pool, granted, idx_ready, t + 2)
                u_group(t + 1, 0, 0, first=True)
            after_first(TILES - 1)

        @block.scalar
        def _(act):
            ACT_STEPS = 4
            done = [0]

            def settle(t, ins):
                done[0] += 1
                ins.then_inc(act_step, 1)
                act.wait_ge(act_step, of_tile(t, ACT_STEPS, done[0] + 1))

            def drain(t, n, dst, rows=P, blocks=4, base=T_MEMORY):
                act.wait_ge(filled, of_tile(t, T_TILE, base + n + 1))
                act.activation(dst, tp[0:rows, n % 2, 0:blocks * P].rearrange("p (b t) -> p b t", t=P), ACT.Copy) \
                   .then_inc(drained, 1)

            act.wait_ge(loaded, 16 * 17)
            act.wait_ge(zeroed, 5)
            act.activation(mem_k_row[:, 0, :], row_a[:, :], ACT.Square, accum_out=m_ss[:, 0:1])
            act.activation(mem_k_row[:, 1, :], row_b[:, :], ACT.Square, accum_out=m_ss[:, 1:2]).then_inc(act_step, 1)
            act.wait_ge(act_step, 1)
            act.activation(m_root[:, :], m_ss[:, :], ACT.Sqrt, scale=1.0 / D, bias=eps[:, 0:1]).then_inc(mem_root, 1)
            act.wait_ge(mem_rinv_ready, 1)
            act.wait_ge(w_used, KT)
            for m in range(MEM_TILES):
                last = act.activation(mem_k_row[:, m, :], (g01, g23)[m], ACT.Copy, scale=m_rinv[:, m:m + 1])
                last.then_inc(mem_saved, 1)
            for n in range(4):
                act.wait_ge(filled, n + 1)
                act.activation(mem_kT[:, 4 * (n % 2):4 * (n % 2) + 4, (n // 2) * P:(n // 2 + 1) * P],
                               tp[:, n % 2, :].rearrange("p (b t) -> p b t", t=P), ACT.Copy).then_inc(drained, 1)
            act.wait_ge(w_used, 2 * KT)
            for m in range(MEM_TILES):
                act.activation(mem_v[:, m, :], (g01, g23)[m], ACT.Copy, scale=m_rinv[:, m:m + 1]).then_inc(mem_saved, 1)

            def inputs(t):
                act.wait_ge(input_landed, of_tile(t, 64, 64))
                settle(t, act.activation(row_a[:, :], h[:, :], ACT.Square, accum_out=ss[:, 0:1]))
                act.activation(root[:, 0:1], ss[:, 0:1], ACT.Sqrt, scale=1.0 / D, bias=eps[:, 0:1]) \
                   .then_inc(root_ready, 1)

            def project(t):
                pass

            def latents(t):
                act.wait_ge(rmix_ready, of_tile(t, 1, 1))
                act.wait_ge(w_used, chunk_number(t, KT))
                act.activation(qk[:, HEADS, NOPE:QK], g[:, 0, Q_RANK + KV_RANK:LATENT], ACT.Copy, scale=rmix) \
                   .then_inc(k_rope_copied, 1)
                act.activation(lat_row[:, 0:Q_RANK], g[:, 0, 0:Q_RANK], ACT.Square, scale=rmix, accum_out=ss[:, 1:2])
                settle(t, act.activation(lat_row[:, Q_RANK:], g[:, 0, Q_RANK:Q_RANK + KV_RANK], ACT.Square,
                                         scale=rmix, accum_out=ss[:, 2:3]))
                act.activation(root[:, 1:2], ss[:, 1:2], ACT.Sqrt, scale=1.0 / Q_RANK, bias=eps[:, 0:1])
                act.activation(root[:, 2:3], ss[:, 2:3], ACT.Sqrt, scale=1.0 / KV_RANK, bias=eps[:, 0:1]) \
                   .then_inc(root_ready, 1)

            def conv_input(t):
                act.wait_ge(w_used, chunk_number(t, 2 * KT))
                act.activation(sig, g[:, 2, :], ACT.Sigmoid, scale=rmix).then_inc(sig_ready, 1)
                drain(t, T_LATENT, lat_t[:, :, :], blocks=3)
                drain(t, T_CONV, u_t[:, :, HIST:])

            def queries_keys(t):
                act.wait_ge(up_ready, of_tile(t, 2, 1))
                act.activation(qk[:, 0:5, :], g[:, 3, 0:5 * QK].rearrange("p (h d) -> p h d", d=QK), ACT.Copy)
                act.activation(qk[:, 5:8, :], g[:, 0, 0:3 * QK].rearrange("p (h d) -> p h d", d=QK), ACT.Copy) \
                   .then_inc(up_saved, 1)
                act.wait_ge(up_ready, of_tile(t, 2, 2))
                kv = g12.rearrange("p (h d) -> p h d", d=NOPE + VDIM)
                act.activation(kfull[:, :, 0:NOPE], kv[:, :, 0:NOPE], ACT.Copy).then_inc(up_saved, 1)
                act.activation(value_cache[:, bass.ds(t, 1), :].rearrange("p a (h d) -> p (a h) d", d=VDIM),
                               kv[:, :, NOPE:], ACT.Copy).then_inc(up_saved, 1)
                for n in range(2):
                    drain(t, T_Q + n, q_t[0:QK, 4 * n:4 * n + 4, :], rows=QK)
                for n in range(2):
                    hold(act, act_granted, filled, of_tile(t, T_TILE, T_MEMORY + T_K + n + 1))
                    act.activation(key_cache[0:QK, 4 * n:4 * n + 4, bass.ds(t * P, P)],
                                   tp[0:QK, n, :].rearrange("p (b t) -> p b t", t=P), ACT.Copy).then_inc(drained, 1)

            def head(t, n):
                act.wait_ge(s_masked, of_tile(t, 2 * HEADS, 2 * n + 2))
                act.activation(probs[:, n % 2, :], probs[:, n % 2, :], ACT.Exp, scale=MLA_SCALE,
                               bias=nmx[:, n:n + 1], accum_out=lsum[:, n:n + 1]).then_inc(p_ready, 1)
                if n >= 2:
                    act.wait_ge(pv_done, of_tile(t, HEADS, n - 1))
                drain(t, T_P + n, probs_t[:, n % 2, :, :])

            def attended(t):
                drain(t, T_ATTN, ta[:, 0:2, :], blocks=2)
                drain(t, T_ATTN + 1, ta[:, 2:4, :], blocks=2)

            def conv_norm(t):
                act.wait_ge(centred, of_tile(t, 1, 1))
                act.activation(conv_acc[:, :, :], conv_x, ACT.Square).then_inc(squared, 1)
                act.wait_ge(stat_ready, of_tile(t, 2, 2))
                act.activation(conv_root, g[:, 3, P:2 * P], ACT.Sqrt, bias=eps[:, 0:1]).then_inc(conv_rooted, 1)
                act.wait_ge(conv_normed, of_tile(t, 1, 1))
                for c in range(CT):
                    last = act.activation(ta[:, 4 + c, :], conv_x[:, c, :], ACT.Silu, scale=conv_p[:, 1, c:c + 1],
                                          bias=conv_p[:, 2, c:c + 1])
                last.then_inc(cat_ready, 1)

            def norm_root(t, column):
                settle(t, act.activation(row_a[:, :], h[:, :], ACT.Square, accum_out=ss[:, column:column + 1]))
                act.activation(root[:, column:column + 1], ss[:, column:column + 1], ACT.Sqrt, scale=1.0 / D,
                               bias=eps[:, 0:1]).then_inc(root_ready, 1)

            def mix_out(t):
                pass

            def mem_norm(t):
                act.wait_ge(h_mixed, of_tile(t, 1, 1))
                norm_root(t, 3)
                for n in range(2):
                    act.wait_ge(filled, of_tile(t, T_TILE, T_MEMORY + T_HMEM + n + 1))
                    for b in range(4):
                        last = act.activation(ta[:, 4 * n + b, :], tp[:, n, b * P:(b + 1) * P], ACT.Copy,
                                              scale=mem_gT[:, 4 * n + b:4 * n + b + 1])
                    last.then_inc(drained, 1)

            def mem_query(t):
                act.wait_ge(w_used, chunk_number(t, 4 * KT))
                act.activation(row_b[:, :], g23, ACT.Copy).then_inc(mq_saved, 1)
                for n in range(2):
                    drain(t, T_QMEM + n, tb[:, 4 * n:4 * n + 4, :])

            def mem_scores(t):
                act.wait_ge(ms_max, of_tile(t, 2, 2))
                for n in range(MEM_HEADS):
                    last = act.activation(row_b[:, n * N_MEM:(n + 1) * N_MEM], g01[:, n * N_MEM:(n + 1) * N_MEM],
                                          ACT.Exp, scale=MEM_SCALE, bias=nmx[:, n:n + 1],
                                          accum_out=lsum[:, n:n + 1])
                last.then_inc(mp_ready, 1)
                for n in range(2):
                    drain(t, T_PMEM + n, tb[:, 4 * n:4 * n + 4, :])

            def mem_values(t):
                for n in range(2):
                    drain(t, T_OMEM + n, ta[:, 4 * n:4 * n + 4, :])

            def mem_out(t):
                pass

            def peer_norm(t):
                act.wait_ge(h_remembered, of_tile(t, 1, 1))
                norm_root(t, 3)
                for n in range(2):
                    drain(t, T_HFFN + n, ta[:, 4 * n:4 * n + 4, :])

            def peer_query(t, half):
                act.wait_ge(w_used, chunk_number(t, (6 + half) * KT))
                act.activation((row_b[:, :], peer_row)[half], (g23, g01)[half], ACT.Copy).then_inc(pq_saved, 1)
                for n in range(2):
                    drain(t, T_QPEER + 2 * half + n, qp_t[:, 8 * half + 4 * n:8 * half + 4 * n + 4, :])

            def sub_scores(t):
                for n in range(4):
                    act.wait_ge(sub_ready, of_tile(t, 4, n + 1))
                    act.activation(scores[:, 4 * n:4 * n + 4, :], g[:, n, :].rearrange("p (s n) -> p s n", n=KEYS),
                                   ACT.Copy).then_inc(sub_saved, 1)

            def sub_topk(t, q):
                pass

            def gates(t):
                act.wait_ge(best_shifted, of_tile(t, 1, 1))
                act.activation(gate[:, :], gate[:, :], ACT.Exp).then_inc(best_exp, 1)

            def nothing(t, *_):
                pass

            def gelu(t):
                act.wait_ge(a_copied, of_tile(t, GROUPS, GROUPS))
                act.activation(gelu_a[:, :], a_all[:, :], ACT.Gelu).then_inc(gelu_ready, 1)
                act.wait_ge(weight_ready, of_tile(t, 1, 1))

            def v_group(t, group, first):
                for j, r in enumerate(BY_PE):
                    if not first:
                        hold(act, act_granted, v_used_pe, of_tile(t, GROUPS * len(BY_PE), j + 1 - len(BY_PE)) + group * len(BY_PE))
                    act.activation(diag[:, j, :], ident[:, :], ACT.Copy,
                                   scale=weight[:, bass.ds(group * RING + r, 1)]).then_inc(diag_ready, 1)

            def rows(t, kind, first, count):
                if kind == "U":
                    if first + count == GROUPS:
                        gelu(t)
                    return
                if first == 0:
                    act.wait_ge(y_ready, t + 1)
                for n in range(first, first + count):
                    if count > 2 and n == 1:
                        with act.Fori(1, first + count) as group:
                            v_group(t, group, False)
                        break
                    v_group(t, n, n == 0)

            def finish(t):
                act.wait_ge(y_ready, t + 2)
                act.activation(row_a[:, :], y_row[:, :], ACT.Square, accum_out=f_ss).then_inc(y_root_ready, 1)
                act.wait_ge(y_root_ready, of_tile(t, 2, 1))
                act.activation(f_root, f_ss, ACT.Sqrt, scale=1.0 / D, bias=eps[:, 0:1]).then_inc(y_root_ready, 1)
                hold(act, act_granted, y_normed, of_tile(t, 2, 2))
                act.dma_start(out[bass.ds(t * P, P), :], y_row[:, :]).then_inc(stored, 16)

            stages = dict(inputs=inputs, project=project, latents=latents, conv_input=conv_input,
                          queries_keys=queries_keys, head=head, attended=attended, conv_norm=conv_norm,
                          mix_out=mix_out, mem_norm=mem_norm, mem_query=mem_query, mem_scores=mem_scores,
                          mem_values=mem_values, mem_out=mem_out, peer_norm=peer_norm, peer_query=peer_query,
                          sub_scores=sub_scores, sub_topk=sub_topk, candidates=nothing, best=nothing, gates=gates,
                          indices=nothing, publish=nothing)

            def front(t, step):
                name, *args = (step,) if isinstance(step, str) else step
                stages[name](t, *args)

            for step in PLAN:
                if step[0] == "do":
                    front(0, step[1])
            assert done[0] == ACT_STEPS, done
            with act.Fori(0, TILES - 1) as t:
                done[0] = 0
                for step in PLAN:
                    if step[0] == "do":
                        front(t + 1, step[1])
                    else:
                        rows(t, *step)
                finish(t)
            rows(TILES - 1, "U", 0, GROUPS)
            rows(TILES - 1, "V", 0, GROUPS)
            finish(TILES - 1)

        @block.vector
        def _(dve):
            DVE_STEPS = 249
            BASE = 1
            done = [0]

            def step_of(t, n):
                return of_tile(t, DVE_STEPS, BASE + n)

            def note(ins):
                done[0] += 1
                ins.then_inc(dve_step, 1)
                return done[0]

            def settle(t, n=None):
                dve.wait_ge(dve_step, step_of(t, done[0] if n is None else n))

            def settle_held(t, n=None):
                hold(dve, dve_granted, dve_step, step_of(t, done[0] if n is None else n))

            dve.wait_ge(loaded, 16 * 17)
            dve.wait_ge(zeroed, 5)
            dve.tensor_tensor(memn_t, memn_t, memkv_gT[:, :].unsqueeze(2).to_broadcast([P, KT, N_MEM]), ALU.mult) \
               .then_inc(memT_scaled, 1)
            dve.wait_ge(mem_root, 1)
            dve.reciprocal(m_rinv[:, :], m_root[:, :]).then_inc(mem_rinv_ready, 1)
            dve.memset(a_group[:, :], 0.0).then_inc(dve_step, 1)
            dve.sem_inc(y_ready, 1)
            dve.sem_inc(stored, 16)
            dve.wait_ge(dve_step, 1)

            def inputs(t):
                dve.wait_ge(input_landed, of_tile(t, 64, 64))
                dve.tensor_tensor(ta[:, :, :], ta[:, :, :], mix_gT[:, :].unsqueeze(2).to_broadcast([P, KT, P]),
                                  ALU.mult).then_inc(x_scaled, 1)
                dve.wait_ge(root_ready, of_tile(t, 4, 1))
                dve.reciprocal(rmix, root[:, 0:1]).then_inc(rmix_ready, 1)

            def latents(t):
                dve.wait_ge(rmix_ready, of_tile(t, 1, 1))
                dve.wait_ge(root_ready, of_tile(t, 4, 2))
                note(dve.reciprocal(rinv[:, 1:3], root[:, 1:3]))
                settle(t)
                note(dve.tensor_scalar(kv2, rinv[:, 1:3], rmix, None, ALU.mult))
                settle(t)
                dve.scalar_tensor_tensor(lat_row[:, 0:Q_RANK], g[:, 0, 0:Q_RANK], kv2[:, 0:1], latent_g[:, 0:Q_RANK],
                                         ALU.mult, ALU.mult)
                dve.scalar_tensor_tensor(lat_row[:, Q_RANK:], g[:, 0, Q_RANK:Q_RANK + KV_RANK], kv2[:, 1:2],
                                         latent_g[:, Q_RANK:], ALU.mult, ALU.mult).then_inc(lat_normed, 1)

            def conv_input(t):
                dve.wait_ge(sig_ready, of_tile(t, 1, 1))
                dve.scalar_tensor_tensor(u_row, g[:, 1, :], rmix, sig, ALU.mult, ALU.mult).then_inc(u_ready, 1)

            def queries_keys(t):
                dve.wait_ge(up_saved, of_tile(t, 3, 1))
                dve.wait_ge(k_rope_copied, of_tile(t, 1, 1))
                n9 = [P, HEADS + 1, HALF]
                cos, sin = (rope[:, c:c + 1, :].to_broadcast(n9) for c in range(2))
                x1, x2 = qk[:, :, NOPE:NOPE + HALF], qk[:, :, NOPE + HALF:QK]
                w = (HEADS + 1) * HALF
                t1, t2, t3, t4 = (row_b[:, c * w:(c + 1) * w].rearrange("p (h d) -> p h d", d=HALF) for c in range(4))
                dve.tensor_tensor(t1, x1, cos, ALU.mult)
                dve.tensor_tensor(t2, x2, sin, ALU.mult)
                dve.tensor_tensor(t3, x1, sin, ALU.mult)
                note(dve.tensor_tensor(t4, x2, cos, ALU.mult))
                settle(t)
                dve.tensor_tensor(x1, t1, t2, ALU.subtract)
                dve.tensor_tensor(x2, t3, t4, ALU.add).then_inc(roped, 1)
                dve.wait_ge(roped, of_tile(t, 2, 1))
                dve.tensor_copy(kfull[:, :, NOPE:QK], qk[:, HEADS:HEADS + 1, NOPE:QK].to_broadcast([P, HEADS, ROPE])) \
                   .then_inc(roped, 1)

            def tap(t, k, n):
                dynamic = not isinstance(k, int)
                for c in range(CT):
                    dve.wait_ge(dve_step, step_of(t, n - CT + c + 1))
                    ins = dve.scalar_tensor_tensor(
                        conv_acc[:, c, :], u_t[:, c, bass.ds(k, P)],
                        conv_wT[:, c, bass.ds(k, 1)], conv_acc[:, c, :], ALU.mult, ALU.add)
                    ins.then_inc(dve_step, 1)

            def head(t, n):
                dve.wait_ge(s_ready, of_tile(t, HEADS, n + 1))
                if n >= 2:
                    dve.wait_ge(filled, of_tile(t, T_TILE, T_MEMORY + T_P + n - 1))
                dve.tensor_tensor(probs[:, n % 2, :], g[:, n % 2, :], mask[:, :], ALU.add).then_inc(s_masked, 1)
                dve.wait_ge(s_masked, of_tile(t, 2 * HEADS, 2 * n + 1))
                note(dve.tensor_reduce(mx[:, n:n + 1], probs[:, n % 2, :], AX.X, ALU.max))
                settle(t)
                dve.tensor_scalar(nmx[:, n:n + 1], mx[:, n:n + 1], -MLA_SCALE, None, ALU.mult).then_inc(s_masked, 1)
                if n == 0:
                    for c in range(CT):
                        dve.wait_ge(drained, of_tile(t, T_TILE, T_MEMORY + T_CONV + 1))
                        note(dve.tensor_scalar(conv_acc[:, c, :], u_t[:, c, 0:P], conv_wT[:, c, 0:1],
                                               conv_p[:, 0, c:c + 1], ALU.mult, ALU.add))
                first, taps = 1 + 4 * n, min(4, TAPS - 1 - 4 * n)
                if n:
                    settle_held(t)
                before = done[0]
                with dve.Fori(0, taps) as k:
                    tap(t, k + first, k * CT + before)
                done[0] += taps * CT

            def attended(t):
                dve.wait_ge(p_ready, of_tile(t, HEADS, HEADS))
                note(dve.reciprocal(linv, lsum))
                settle(t)
                dve.wait_ge(pv_done, of_tile(t, HEADS, HEADS))
                dve.tensor_tensor(row_b[:, 0:512].rearrange("p (h d) -> p h d", d=VDIM),
                                  g[:, 2, :].rearrange("p (h d) -> p h d", d=VDIM),
                                  linv.unsqueeze(2).to_broadcast([P, HEADS, VDIM]), ALU.mult).then_inc(attn_ready, 1)
                dve.tensor_copy(u_t[:, :, 0:HIST], u_t[:, :, P:P + HIST]).then_inc(hist_read, 1)

            def conv_norm(t):
                all4 = [P, CT, P]
                dve.wait_ge(stat_ready, of_tile(t, 2, 1))
                dve.wait_ge(dve_step, step_of(t, done[0]))
                dve.tensor_tensor(conv_x, conv_acc[:, :, :], g[:, 3:4, 0:P].to_broadcast(all4), ALU.subtract) \
                   .then_inc(centred, 1)
                dve.wait_ge(conv_rooted, of_tile(t, 1, 1))
                note(dve.reciprocal(conv_root, conv_root))
                settle(t)
                dve.tensor_tensor(conv_x, conv_x, row_b[:, 0:P].unsqueeze(1).to_broadcast(all4), ALU.mult) \
                   .then_inc(conv_normed, 1)

            def mix_out(t):
                dve.wait_ge(w_used, chunk_number(t, 3 * KT))
                dve.tensor_tensor(h[:, :], h[:, :], g01, ALU.add).then_inc(h_mixed, 1)

            def mem_norm(t):
                dve.wait_ge(root_ready, of_tile(t, 4, 3))
                note(dve.reciprocal(rinv[:, 3:4], root[:, 3:4]))
                settle(t)
                dve.tensor_scalar(row_a[:, :], h[:, :], rinv[:, 3:4], None, ALU.mult).then_inc(h_row, 1)

            def mem_scores(t):
                dve.wait_ge(ms_ready, of_tile(t, 1, 1))
                dve.tensor_reduce(mx[:, 0:4], g01.rearrange("p (h m) -> p h m", m=N_MEM), AX.X, ALU.max) \
                   .then_inc(ms_max, 1)
                dve.wait_ge(ms_max, of_tile(t, 2, 1))
                dve.tensor_scalar(nmx[:, 0:4], mx[:, 0:4], -MEM_SCALE, None, ALU.mult).then_inc(ms_max, 1)

            def mem_values(t):
                dve.wait_ge(mp_ready, of_tile(t, 1, 1))
                note(dve.reciprocal(linv[:, 0:4], lsum[:, 0:4]))
                settle(t)
                dve.wait_ge(mo_ready, of_tile(t, 1, 1))
                dve.tensor_tensor(row_a[:, :].rearrange("p (h d) -> p h d", d=MEM_DIM),
                                  g23.rearrange("p (h d) -> p h d", d=MEM_DIM),
                                  linv[:, 0:4].unsqueeze(2).to_broadcast([P, MEM_HEADS, MEM_DIM]), ALU.mult) \
                   .then_inc(mo_row, 1)

            def mem_out(t):
                dve.wait_ge(w_used, chunk_number(t, 5 * KT))
                dve.tensor_tensor(h[:, :], h[:, :], g01, ALU.add).then_inc(h_remembered, 1)

            def peer_norm(t):
                dve.wait_ge(root_ready, of_tile(t, 4, 4))
                note(dve.reciprocal(rinv[:, 3:4], root[:, 3:4]))
                settle(t)
                dve.scalar_tensor_tensor(hn[:, :], h[:, :], rinv[:, 3:4], ffn_g[:, :], ALU.mult, ALU.mult) \
                   .then_inc(hn_ready, 1)

            def best_16(t, values, indices, source, many):
                for s in many:
                    note(dve.max(values[:, s, 0:8], source[:, s, :]))
                settle_held(t)
                for s in many:
                    dve.max_index(indices[:, s, 0:8], values[:, s, 0:8], source[:, s, :])
                    note(dve.match_replace(source[:, s, :], values[:, s, 0:8], source[:, s, :], LOWEST))
                settle_held(t)
                for s in many:
                    note(dve.max(values[:, s, 8:16], source[:, s, :]))
                settle_held(t)
                for s in many:
                    note(dve.max_index(indices[:, s, 8:16], values[:, s, 8:16], source[:, s, :]))

            def sub_topk(t, q):
                hold(dve, dve_granted, sub_saved, of_tile(t, 4, q + 1))
                best_16(t, top_v, top_i, scores, range(4 * q, 4 * q + 4))

            def candidates(t):
                settle(t)
                n4 = [P, PEER_HEADS, TOPK, TOPK]
                halves = top_v[:, :, :].rearrange("p (h c) k -> p c h k", c=2)
                note(dve.tensor_tensor(cand, halves[:, 0, :, :].unsqueeze(3).to_broadcast(n4),
                                       halves[:, 1, :, :].unsqueeze(2).to_broadcast(n4), ALU.add))
                note(dve.tensor_copy(top_f, top_i[:, :, :]))
                settle_held(t)

            def best(t, half):
                best_16(t, best_v, best_p, cand_h, range(4 * half, 4 * half + 4))

            def gates(t):
                settle(t)
                n3 = [P, PEER_HEADS, TOPK]
                gate3 = gate[:, :].rearrange("p (h k) -> p h k", k=TOPK)
                dve.tensor_tensor(gate3, best_v[:, :, :], best_v[:, :, 0:1].to_broadcast(n3), ALU.subtract) \
                   .then_inc(best_shifted, 1)
                flat = best_p[:, :, :].rearrange("p h k -> p (h k)")
                dve.tensor_scalar(pos_u[:, 0, :], flat, 4, None, ALU.logical_shift_right)
                note(dve.tensor_scalar(pos_u[:, 1, :], flat, 15, None, ALU.bitwise_and))
                settle(t)
                note(dve.tensor_copy(pos_f, pos_u))
                dve.wait_ge(best_exp, of_tile(t, 1, 1))
                note(dve.tensor_reduce(mx, gate3, AX.X, ALU.add))
                settle(t)
                note(dve.reciprocal(linv, mx))
                settle(t)
                note(dve.tensor_tensor(gate3, gate3, linv.unsqueeze(2).to_broadcast(n3), ALU.mult))

            def indices(t):
                n4 = [P, PEER_HEADS, TOPK, TOPK]
                tops = top_f.rearrange("p (h c) k -> p c h k", c=2)
                places = iota[:, :].unsqueeze(1).unsqueeze(1).to_broadcast(n4)
                for c in range(2):
                    pos = pos_f[:, c, :].rearrange("p (h k) -> p h k", k=TOPK).unsqueeze(3).to_broadcast(n4)
                    settle(t)
                    note(dve.tensor_tensor(onehot, pos, places, ALU.is_equal))
                    settle(t)
                    note(dve.tensor_tensor(onehot, onehot, tops[:, c, :, :].unsqueeze(2).to_broadcast(n4), ALU.mult))
                    settle(t)
                    note(dve.tensor_reduce(picked[:, c, :].rearrange("p (h k) -> p h k", k=TOPK), onehot, AX.X, ALU.add))

            def publish(t):
                settle(t)
                if not isinstance(t, int) or t:
                    dve.wait_ge(idx_staged, of_tile(t, 2 * GROUPS, 0))
                dve.scalar_tensor_tensor(idx[:, :], picked[:, 0, :], float(KEYS), picked[:, 1, :],
                                         ALU.mult, ALU.add).then_inc(idx_ready, 1)

            def nothing(t, *_):
                pass

            def start(t):
                dve.wait_ge(h_remembered, of_tile(t, 1, 1))
                hold(dve, dve_granted, hn_ready, of_tile(t, 1, 1))
                dve.tensor_copy(y_acc[:, :], h[:, :]).then_inc(h_taken, 1)

            def u_group(t, group):
                for r in range(RING):
                    dve.wait_ge(landed[r], (of_tile(t, 2 * GROUPS, 1) + group) * 16)
                    dve.tensor_tensor_reduce(out=ring[:, r, :], in0=ring[:, r, :], in1=hn[:, :], scale=1.0, scalar=0.0,
                                             op0=ALU.mult, op1=ALU.add, accum_out=a_group[:, r:r + 1]) \
                       .then_inc(u_used, 1)
                hold(dve, dve_granted, u_used, of_tile(t, SLOTS, RING) + group * RING)
                dve.tensor_copy(a_all[:, bass.ds(group * RING, RING)], a_group[:, :]).then_inc(a_copied, 1)
                hold(dve, dve_granted, a_copied, of_tile(t, GROUPS, 1) + group)

            def weights(t):
                dve.wait_ge(gelu_ready, of_tile(t, 1, 1))
                dve.tensor_tensor(weight[:, :], gelu_a[:, :], gate[:, :], ALU.mult).then_inc(weight_ready, 1)
                dve.wait_ge(weight_ready, of_tile(t, 1, 1))
                dve.wait_ge(h_taken, of_tile(t, 1, 1))

            def v_group(t, group):
                for j, r in enumerate(BY_DVE):
                    dve.wait_ge(landed[r], (of_tile(t, 2 * GROUPS, GROUPS + 1) + group) * 16)
                    dve.scalar_tensor_tensor(y_acc[:, :], ring[:, r, :], weight[:, bass.ds(group * RING + r, 1)],
                                             y_acc[:, :], ALU.mult, ALU.add).then_inc(v_used_dve, 1)
                    hold(dve, dve_granted, v_used_dve,
                         of_tile(t, GROUPS * len(BY_DVE), j + 1) + group * len(BY_DVE))

            def rows(t, kind, first, count):
                body = u_group if kind == "U" else v_group
                if count == 1:
                    body(t, first)
                else:
                    with dve.Fori(first, first + count) as group:
                        body(t, group)
                if kind == "U" and first + count == GROUPS:
                    weights(t)

            def finish(t):
                dve.wait_ge(v_used_pe, of_tile(t, GROUPS * len(BY_PE), GROUPS * len(BY_PE)))
                dve.wait_ge(stored, of_tile(t, 16, 16))
                dve.tensor_tensor(y_row[:, :], acc[:, :], y_acc[:, :], ALU.add).then_inc(y_ready, 1)
                dve.wait_ge(y_root_ready, of_tile(t, 2, 2))
                dve.reciprocal(f_rinv, f_root).then_inc(y_normed, 1)
                dve.wait_ge(y_normed, of_tile(t, 2, 1))
                dve.scalar_tensor_tensor(y_row[:, :], y_row[:, :], f_rinv, final_g[:, :], ALU.mult, ALU.mult) \
                   .then_inc(y_normed, 1)

            stages = dict(inputs=inputs, project=nothing, latents=latents, conv_input=conv_input,
                          queries_keys=queries_keys, head=head, attended=attended, conv_norm=conv_norm,
                          mix_out=mix_out, mem_norm=mem_norm, mem_query=nothing, mem_scores=mem_scores,
                          mem_values=mem_values, mem_out=mem_out, peer_norm=peer_norm, peer_query=nothing,
                          sub_scores=nothing, sub_topk=sub_topk, candidates=candidates, best=best, gates=gates,
                          indices=indices, publish=publish)

            def front(t, step):
                name, *args = (step,) if isinstance(step, str) else step
                stages[name](t, *args)

            for step in PLAN:
                if step[0] == "do":
                    front(0, step[1])
            assert done[0] == DVE_STEPS, done
            with dve.Fori(0, TILES - 1) as t:
                done[0] = 0
                start(t)
                for step in PLAN:
                    if step[0] == "do":
                        front(t + 1, step[1])
                    else:
                        rows(t, *step)
                finish(t)
            start(TILES - 1)
            rows(TILES - 1, "U", 0, GROUPS)
            rows(TILES - 1, "V", 0, GROUPS)
            finish(TILES - 1)

        @block.tensor
        def _(pe):
            def fill(t, n, blocks, rows=P, base=T_MEMORY):
                seq = base + n
                if seq >= 2 or not isinstance(t, int):
                    pe.wait_ge(drained, of_tile(t, T_TILE, seq - 1))
                for b, src in enumerate(blocks):
                    last = pe.transpose(tp[0:rows, n % 2, b * P:(b + 1) * P], src, ident[:, :])
                last.then_inc(filled, 1)

            def is_drained(t, n, base=T_MEMORY):
                pe.wait_ge(drained, of_tile(t, T_TILE, base + n + 1))

            def use(t, n, lhs, outs):
                pe.wait_ge(w_landed[place(n)], landed_value(t, n))
                for o, col, cols, start, stop in outs:
                    last = pe.matmul(o, lhs, wring[:, place(n), col:col + cols], start=start, stop=stop)
                last.then_inc(w_used, 1)
                return last

            def gemm(t, first, lhs_of, banks):
                for k in range(KT):
                    use(t, first + k, lhs_of(k), [(banks[n], 512 * n, 512, k == 0, k == KT - 1) for n in range(2)])

            pe.wait_ge(loaded, 16 * 17)
            pe.wait_ge(memT_scaled, 1)
            for n in range(2):
                if n:
                    pe.wait_ge(mem_saved, 2)
                for k in range(KT):
                    c = n * KT + k
                    pe.wait_ge(w_landed[c % WRING], 16 * (c // WRING + 1))
                    for m in range(MEM_TILES):
                        for b in range(2):
                            last = pe.matmul(g[:, 2 * m + b, :], memn_t[:, k, m * P:(m + 1) * P],
                                             wring[:, c % WRING, b * 512:(b + 1) * 512], start=k == 0, stop=k == KT - 1)
                    last.then_inc(w_used, 1)
                if n == 0:
                    pe.wait_ge(mem_saved, 2)
                    for q in range(4):
                        fill(0, q, [mem_k_row[:, q // 2, (4 * (q % 2) + b) * P:(4 * (q % 2) + b + 1) * P]
                                    for b in range(4)], base=0)

            def inputs(t):
                pass

            def project(t):
                pe.wait_ge(x_scaled, of_tile(t, 1, 1))
                if isinstance(t, int) and t == 0:
                    pe.wait_ge(mem_saved, 4)
                else:
                    pe.wait_ge(sub_saved, of_tile(t, 4, 0))
                for k in range(KT):
                    last = use(t, k, ta[:, k, :], [(g[:, 0, 0:LATENT], 0, LATENT, k == 0, k == KT - 1)])
                for k in range(KT):
                    use(t, KT + k, ta[:, k, :], [(g[:, 1, :], 0, 512, k == 0, k == KT - 1),
                                                 (g[:, 2, :], 512, 512, k == 0, k == KT - 1)])

            def latents(t):
                pe.wait_ge(lat_normed, of_tile(t, 1, 1))
                fill(t, T_LATENT, [lat_row[:, b * P:(b + 1) * P] for b in range(3)])

            def conv_input(t):
                pe.wait_ge(u_ready, of_tile(t, 1, 1))
                if not isinstance(t, int):
                    pe.wait_ge(hist_read, t)
                fill(t, T_CONV, [u_row[:, b * P:(b + 1) * P] for b in range(4)])

            def queries_keys(t):
                is_drained(t, T_LATENT)
                pe.wait_ge(k_rope_copied, of_tile(t, 1, 1))
                for k in range(2):
                    pe.matmul(g[:, 3, 0:5 * QK], lat_t[:, k, :], w_q_up[:, k, 0:5 * QK], start=k == 0, stop=k == 1)
                    last = pe.matmul(g[:, 0, 0:3 * QK], lat_t[:, k, :], w_q_up[:, k, 5 * QK:], start=k == 0, stop=k == 1)
                last.then_inc(up_ready, 1)
                for b in range(2):
                    last = pe.matmul(g[:, 1 + b, :], lat_t[:, 2, :], w_kv_up[:, b * 512:(b + 1) * 512], start=True, stop=True)
                last.then_inc(up_ready, 1)
                pe.wait_ge(roped, of_tile(t, 2, 1))
                for n in range(2):
                    fill(t, T_Q + n, [qk[:, 4 * n + b, :] for b in range(4)], rows=QK)
                pe.wait_ge(roped, of_tile(t, 2, 2))
                pe.wait_ge(up_saved, of_tile(t, 3, 3))
                for n in range(2):
                    fill(t, T_K + n, [kfull[:, 4 * n + b, :] for b in range(4)], rows=QK)

            def scores_of(t, n):
                if n == 0:
                    is_drained(t, T_K + 1)
                else:
                    if n >= 2:
                        pe.wait_ge(s_masked, of_tile(t, 2 * HEADS, 2 * (n - 2) + 1))
                pe.matmul(g[:, n % 2, :], q_t[0:QK, n, :], key_cache[0:QK, n, :], start=True, stop=True) \
                  .then_inc(s_ready, 1)

            def values_of(t, n):
                is_drained(t, T_P + n)
                for j in range(TILES):
                    last = pe.matmul(g[:, 2, n * VDIM:(n + 1) * VDIM], probs_t[:, n % 2, j, :],
                                     value_cache[:, j, n * VDIM:(n + 1) * VDIM], start=j == 0, stop=j == TILES - 1)
                last.then_inc(pv_done, 1)

            def head(t, n):
                if n == 0:
                    scores_of(t, 0)
                if n + 1 < HEADS:
                    scores_of(t, n + 1)
                pe.wait_ge(p_ready, of_tile(t, HEADS, n + 1))
                fill(t, T_P + n, [probs[:, n % 2, j * P:(j + 1) * P] for j in range(TILES)])
                if n:
                    values_of(t, n - 1)

            def attended(t):
                values_of(t, HEADS - 1)
                pe.wait_ge(attn_ready, of_tile(t, 1, 1))
                for n in range(2):
                    fill(t, T_ATTN + n, [row_b[:, (2 * n + b) * P:(2 * n + b + 1) * P] for b in range(2)])

            def conv_norm(t):
                pe.wait_ge(hist_read, of_tile(t, 1, 1))
                for c in range(CT):
                    last = pe.matmul(g[:, 3, 0:P], mean_w[:, :], conv_acc[:, c, :], start=c == 0, stop=c == CT - 1)
                last.then_inc(stat_ready, 1)
                pe.wait_ge(squared, of_tile(t, 1, 1))
                for c in range(CT):
                    last = pe.matmul(g[:, 3, P:2 * P], mean_w[:, :], conv_acc[:, c, :], start=c == 0, stop=c == CT - 1)
                last.then_inc(stat_ready, 1)

            def mix_out(t):
                is_drained(t, T_ATTN + 1)
                pe.wait_ge(cat_ready, of_tile(t, 1, 1))
                gemm(t, 2 * KT, lambda k: ta[:, k, :], (g[:, 0, :], g[:, 1, :]))

            def mem_norm(t):
                pe.wait_ge(h_row, of_tile(t, 1, 1))
                for n in range(2):
                    fill(t, T_HMEM + n, [row_a[:, (4 * n + b) * P:(4 * n + b + 1) * P] for b in range(4)])

            def mem_query(t):
                is_drained(t, T_HMEM + 1)
                gemm(t, 3 * KT, lambda k: ta[:, k, :], (g[:, 2, :], g[:, 3, :]))
                pe.wait_ge(mq_saved, of_tile(t, 1, 1))
                for n in range(2):
                    fill(t, T_QMEM + n, [row_b[:, (4 * n + b) * P:(4 * n + b + 1) * P] for b in range(4)])

            def mem_scores(t):
                is_drained(t, T_QMEM + 1)
                for n in range(MEM_HEADS):
                    for k in range(2):
                        last = pe.matmul(g[:, n // 2, (n % 2) * N_MEM:(n % 2 + 1) * N_MEM], tb[:, 2 * n + k, :],
                                         mem_kT[:, 2 * n + k, :], start=k == 0, stop=k == 1)
                last.then_inc(ms_ready, 1)
                pe.wait_ge(mp_ready, of_tile(t, 1, 1))
                for n in range(2):
                    fill(t, T_PMEM + n, [row_b[:, (4 * n + b) * P:(4 * n + b + 1) * P] for b in range(4)])

            def mem_values(t):
                is_drained(t, T_PMEM + 1)
                for n in range(MEM_HEADS):
                    for m in range(MEM_TILES):
                        last = pe.matmul(g[:, 2 + n // 2, (n % 2) * MEM_DIM:(n % 2 + 1) * MEM_DIM], tb[:, 2 * n + m, :],
                                         mem_v[:, m, n * MEM_DIM:(n + 1) * MEM_DIM], start=m == 0, stop=m == 1)
                last.then_inc(mo_ready, 1)
                pe.wait_ge(mo_row, of_tile(t, 1, 1))
                for n in range(2):
                    fill(t, T_OMEM + n, [row_a[:, (4 * n + b) * P:(4 * n + b + 1) * P] for b in range(4)])

            def mem_out(t):
                is_drained(t, T_OMEM + 1)
                gemm(t, 4 * KT, lambda k: ta[:, k, :], (g[:, 0, :], g[:, 1, :]))

            def peer_norm(t):
                pe.wait_ge(hn_ready, of_tile(t, 1, 1))
                for n in range(2):
                    fill(t, T_HFFN + n, [hn[:, (4 * n + b) * P:(4 * n + b + 1) * P] for b in range(4)])

            def peer_query(t, half):
                is_drained(t, T_HFFN + 1)
                gemm(t, (5 + half) * KT, lambda k: ta[:, k, :], ((g[:, 2, :], g[:, 3, :]), (g[:, 0, :], g[:, 1, :]))[half])
                pe.wait_ge(pq_saved, of_tile(t, 2, half + 1))
                src = (row_b[:, :], peer_row)[half]
                for n in range(2):
                    fill(t, T_QPEER + 2 * half + n, [src[:, (4 * n + b) * P:(4 * n + b + 1) * P] for b in range(4)])

            def sub_scores(t):
                is_drained(t, T_QPEER + 3)
                for n in range(4):
                    for b in range(4):
                        last = pe.matmul(g[:, n, b * P:(b + 1) * P], qp_t[:, 4 * n + b, :], sub_keysT[:, 4 * n + b, :],
                                         start=True, stop=True)
                    last.then_inc(sub_ready, 1)

            def nothing(t, *_):
                pass

            def v_group(t, group, first=False, last=False):
                for j, r in enumerate(BY_PE):
                    pe.wait_ge(landed[r], (of_tile(t, 2 * GROUPS, GROUPS + 1) + group) * 16)
                    pe.wait_ge(diag_ready, of_tile(t, GROUPS * len(BY_PE), j + 1) + group * len(BY_PE))
                    for n in range(2):
                        ins = pe.matmul(acc[:, n * 512:(n + 1) * 512], diag[:, j, :], ring[:, r, n * 512:(n + 1) * 512],
                                        start=first and j == 0, stop=last and j == len(BY_PE) - 1)
                    ins.then_inc(v_used_pe, 1)

            def rows(t, kind, first, count):
                if kind == "U":
                    return
                if first == 0:
                    pe.wait_ge(y_ready, t + 1)
                n = first
                while n < first + count:
                    if 0 < n < GROUPS - 1 and count > 2:
                        with pe.Fori(1, GROUPS - 1) as group:
                            v_group(t, group)
                        n = GROUPS - 1
                        continue
                    v_group(t, n, n == 0, n == GROUPS - 1)
                    n += 1

            stages = dict(inputs=inputs, project=project, latents=latents, conv_input=conv_input,
                          queries_keys=queries_keys, head=head, attended=attended, conv_norm=conv_norm,
                          mix_out=mix_out, mem_norm=mem_norm, mem_query=mem_query, mem_scores=mem_scores,
                          mem_values=mem_values, mem_out=mem_out, peer_norm=peer_norm, peer_query=peer_query,
                          sub_scores=sub_scores, sub_topk=nothing, candidates=nothing, best=nothing, gates=nothing,
                          indices=nothing, publish=nothing)

            def front(t, step):
                name, *args = (step,) if isinstance(step, str) else step
                stages[name](t, *args)

            for step in PLAN:
                if step[0] == "do":
                    front(0, step[1])
            with pe.Fori(0, TILES - 1) as t:
                for step in PLAN:
                    if step[0] == "do":
                        front(t + 1, step[1])
                    else:
                        rows(t, *step)
            rows(TILES - 1, "V", 0, GROUPS)


def kernel(**inputs):
    import numpy as np
    import concourse.bacc as bacc
    from concourse import mybir as mb
    from concourse.bass_utils import run_bass_kernel_spmd

    def columns(v):
        return np.ascontiguousarray(np.asarray(v).reshape(-1, P).T)

    a = {k: np.asarray(v) for k, v in inputs.items()}
    x = a["x"][0]
    arrays = {
        "x": x,
        "xT": np.ascontiguousarray(x.reshape(TILES, P, KT, P).transpose(0, 3, 2, 1)).reshape(TILES * P, KT, P),
        "mem": a["mem"][0],
        "memT": np.ascontiguousarray(a["mem"][0].reshape(N_MEM, KT, P).transpose(2, 1, 0)),
        "mix_gT": columns(a["norm_mix_g"][0]), "mem_gT": columns(a["norm_mem_g"][0]),
        "memkv_gT": columns(a["mem_kv_norm_g"][0]),
        "q_latent_g": a["q_latent_g"], "kv_latent_g": a["kv_latent_g"],
        "norm_ffn_g": a["norm_ffn_g"], "final_norm_g": a["final_norm_g"].reshape(1, D),
        "conv_wT": np.ascontiguousarray(a["conv_w"][0, :, 0, :].reshape(TAPS, CT, P).transpose(2, 1, 0)),
        "conv_p": np.ascontiguousarray(np.stack([a[n][0].reshape(CT, P).T for n in ("conv_b", "conv_ln_g", "conv_ln_b")], 1)),
        "w_in": a["w_in"][0], "w_q_up": a["w_q_up"][0], "w_kv_up": a["w_kv_up"][0], "w_mix_out": a["w_mix_out"][0],
        "w_mem_q": a["w_mem_q"][0], "w_mem_kv": a["w_mem_kv"][0], "w_mem_out": a["w_mem_out"][0],
        "w_peer_query": a["w_peer_query"][0],
        "sub_keysT": np.ascontiguousarray(a["peer_sub_keys"][0].transpose(3, 0, 1, 2)).reshape(P, SETS, KEYS),
        "peer_u": a["peer_u"][0], "peer_v": a["peer_v"][0],
    }
    arrays["ident"] = np.eye(P, dtype=np.float32)
    arrays["iota"] = np.arange(TOPK, dtype=np.float32).reshape(1, TOPK)
    inv = (1.0 / (np.float32(10000.0) ** (np.arange(0, ROPE, 2, dtype=np.float32) / np.float32(ROPE)))).astype(np.float32)
    ang = np.arange(SEQ, dtype=np.float32)[:, None] * inv[None, :]
    arrays["rope"] = np.stack([np.cos(ang), np.sin(ang)], 1).astype(np.float32)
    chunk = np.arange(SEQ) // 64
    arrays["mask"] = np.where(chunk[None, :] <= chunk[:, None], 0.0, -1e30).astype(np.float32)

    nc = bacc.Bacc("TRN2", target_bir_lowering=False, num_devices=1)
    arrays = {n: np.ascontiguousarray(v) for n, v in arrays.items()}
    dram = {n: nc.dram_tensor("in_" + n, v.shape, mb.dt.from_np(v.dtype), kind="ExternalInput").ap()
            for n, v in arrays.items()}
    out = nc.dram_tensor("out", (SEQ, D), mb.dt.float32, kind="ExternalOutput").ap()
    build(nc, dram, out)
    r = run_bass_kernel_spmd(nc, [{"in_" + n: v for n, v in arrays.items()}], core_ids=[0])
    return r.results[0]["out"].reshape(1, SEQ, D)
```

```python
import concourse.bass as bass
from concourse import mybir
from contextlib import ExitStack

P = 128
D = 1024
KT = D // P
SEQ = 512
TILES = SEQ // P
EPS = 1e-6
N_MEM = 256
MEM_TILES = N_MEM // P
HEADS, NOPE, ROPE, VDIM = 8, 64, 32, 64
QK = NOPE + ROPE
HALF = ROPE // 2
Q_RANK, KV_RANK = 256, 128
LATENT = Q_RANK + KV_RANK + ROPE
CONV, TAPS = 512, 31
CT = CONV // P
HIST = TAPS - 1
MEM_HEADS, MEM_DIM = 4, 256
PEER_HEADS, KEYS, TOPK = 8, 128, 16
SETS = 2 * PEER_HEADS
SLOTS = PEER_HEADS * TOPK
RING = 8
GROUPS = SLOTS // RING
WRING = 7
LOWEST = -3.0e38

BY_PE = (0, 1, 2, 3, 4)
BY_DVE = (5, 6, 7)

W_TILE = ([("w_in", k, 0, LATENT) for k in range(KT)] + [("w_in", k, LATENT, 1024) for k in range(KT)]
          + [("w_mix_out", k, 0, 1024) for k in range(KT)] + [("w_mem_q", k, 0, 1024) for k in range(KT)]
          + [("w_mem_out", k, 0, 1024) for k in range(KT)]
          + [("w_peer_query", k, 1024 * n, 1024) for n in range(2) for k in range(KT)])
W_MEMORY = [("w_mem_kv", k, 1024 * n, 1024) for n in range(2) for k in range(KT)]
PER_TILE = len(W_TILE)
W_BEFORE_MEMORY = 2 * KT
assert PER_TILE % WRING == 0

T_LATENT, T_CONV, T_Q, T_K, T_P, T_ATTN = 0, 1, 2, 4, 6, 14
T_HMEM, T_QMEM, T_PMEM, T_OMEM, T_HFFN, T_QPEER, T_TILE = 16, 18, 20, 22, 24, 26, 30
T_MEMORY = 4

HALF_GROUPS = GROUPS // 2
U, V = ("u rows",), ("v rows",)


def later(*steps):
    return [("next tile",) + s for s in steps]


def choice(half):
    return [("peer_query", half), ("sub_scores", half), ("sub_topk", half, 0), ("sub_topk", half, 1),
            ("candidates", half), ("best", half), ("gates", half), ("indices", half, 0), ("indices", half, 1)]


HEADS_STEPS = [("head", n) for n in range(HEADS)]
CONV_TAPS = 5
CONV_STEPS = [("conv", n) for n in range((TAPS - 1) // CONV_TAPS)]
FIRST = ([("inputs",), ("project",), ("latents",), ("conv_input",), ("queries_keys",)] + HEADS_STEPS
         + [("attended",), ("memory", 0)] + CONV_STEPS + [("memory", 1), ("conv_norm",), ("mix_out",), ("mem_norm",),
            ("mem_query",), ("mem_scores",), ("mem_values",), ("mem_out",), ("peer_norm",)] + choice(0)
         + [("publish", 0), ("next_input",)])
LATE = ([("peer_query", 1), U, ("sub_scores", 1), V, ("sub_topk", 1, 0), U, ("sub_topk", 1, 1), V,
         ("candidates", 1), U, ("best", 1), V, ("gates", 1)] + later(("inputs",), ("project",))
        + [("indices", 1, 0), U, ("indices", 1, 1), V] + later(("latents",), ("conv_input",))
        + [U, V] + later(("queries_keys",)) + [U] + later(("head", 0), ("head", 1)) + [V] + later(("conv", 0))
        + [U] + later(("head", 2), ("head", 3)) + [V] + later(("conv", 1)) + [U, ("publish", 1)]
        + later(("head", 4), ("head", 5)) + [V])
EARLY = [("conv", 2), U, ("head", 6), ("head", 7), ("attended",), V, ("conv", 3), U, ("conv", 4), V, ("conv", 5),
         U, ("conv_norm",), V, ("mix_out",), U, ("mem_norm",), V, ("mem_query",), U, ("mem_scores",), ("mem_values",),
         V, ("mem_out",), U, ("peer_norm",), V, ("peer_query", 0), U, ("sub_scores", 0), ("sub_topk", 0, 0),
         ("sub_topk", 0, 1), V, ("candidates", 0), ("best", 0), ("gates", 0), ("indices", 0, 0), U,
         ("indices", 0, 1), ("publish", 0), ("next_input",), V]
LATE_LAST = [s for s in LATE if s[0] != "next tile"]
assert all(steps.count(U) == steps.count(V) == HALF_GROUPS for steps in (EARLY, LATE))


def of_tile(t, per_tile, n):
    return t * per_tile + n


def build(nc, dram, out):
    f32, i32, u32 = mybir.dt.float32, mybir.dt.int32, mybir.dt.uint32
    ALU, ACT, AX = mybir.AluOpType, mybir.ActivationFunctionType, mybir.AxisListType
    MLA_SCALE, MEM_SCALE = QK ** -0.5, MEM_DIM ** -0.5

    ctx = ExitStack()
    with ctx:
        def sb(name, shape, dt=f32):
            return ctx.enter_context(nc.sbuf_tensor(name, shape, dt))

        def sem(name):
            return ctx.enter_context(nc.semaphore(name))

        ring = sb("ring", [P, RING, D])
        wring = sb("wring", [P, WRING, 1024])
        key_cache = sb("key_cache", [P, HEADS, SEQ])
        value_cache = sb("value_cache", [P, TILES, HEADS * VDIM])
        mem_kT = sb("mem_kT", [P, KT, N_MEM])
        mem_v = sb("mem_v", [P, MEM_TILES, D])
        sub_keysT = sb("sub_keysT", [P, SETS, KEYS])
        w_q_up = sb("w_q_up", [P, 2, HEADS * QK])
        w_kv_up = sb("w_kv_up", [P, HEADS * (NOPE + VDIM)])
        ffn_g = sb("ffn_g", [P, D])
        final_g = sb("final_g", [P, D])
        latent_g = sb("latent_g", [P, Q_RANK + KV_RANK])
        mix_gT = sb("mix_gT", [P, KT])
        mem_gT = sb("mem_gT", [P, KT])
        memkv_gT = sb("memkv_gT", [P, KT])
        conv_wT = sb("conv_wT", [P, CT, TAPS])
        conv_p = sb("conv_p", [P, 3, CT])
        ident = sb("ident", [P, P])
        mean_w = sb("mean_w", [P, P])
        rope = sb("rope", [P, 2, HALF])
        iota = sb("iota", [P, TOPK])
        eps = sb("eps", [P, 1])
        mask = sb("mask", [P, SEQ])
        h = sb("h", [P, D])
        hn = sb("hn", [P, D])
        row_a = sb("row_a", [P, D])
        row_b = sb("row_b", [P, D])
        ta = sb("ta", [P, KT, P])
        tb = sb("tb", [P, KT, P])
        arena = sb("arena", [P, 5728])
        lat_row = sb("lat_row", [P, Q_RANK + KV_RANK])
        lat_t = sb("lat_t", [P, 3, P])
        u_t = sb("u_t", [P, CT, HIST + P])
        conv_acc = sb("conv_acc", [P, CT, P])
        h_kept = sb("h_kept", [P, D])
        y_acc = sb("y_acc", [P, D])
        y_row = sb("y_row", [P, D])
        diag = sb("diag", [P, len(BY_PE), P])
        small = sb("small", [P, 64])
        a_group = sb("a_group", [P, RING])
        a_all = sb("a_all", [P, SLOTS])
        gelu_a = sb("gelu_a", [P, SLOTS])
        gate = sb("gate", [P, SLOTS])
        weight = sb("weight", [P, SLOTS])
        idx = sb("idx", [P, SLOTS], i32)
        idx_group = sb("idx_group", [P, 2, RING], i32)
        top_v = sb("top_v", [P, SETS // 2, TOPK])
        top_i = sb("top_i", [P, SETS // 2, TOPK], u32)
        best_v = sb("best_v", [P, PEER_HEADS // 2, TOPK])
        picked = sb("picked", [P, 2, SLOTS // 2])
        best_p = sb("best_p", [P, PEER_HEADS // 2, TOPK], u32)

        def region(first, size):
            return arena[:, first:first + size]

        qk = region(0, 864).rearrange("p (h d) -> p h d", d=QK)
        kfull = region(864, 768).rearrange("p (h d) -> p h d", d=QK)
        q_t = region(1632, 1024).rearrange("p (h t) -> p h t", t=P)
        probs = region(2656, 1024).rearrange("p (b k) -> p b k", k=SEQ)
        probs_t = region(3680, 1024).rearrange("p (b j t) -> p b j t", b=2, t=P)
        sig = region(4704, 512)
        u_row = region(5216, 512)
        N_SET = SETS // 2
        N_HEAD = PEER_HEADS // 2
        qp_t = region(0, 1024).rearrange("p (s t) -> p s t", t=P)
        onehot = region(0, 1024).rearrange("p (h k a) -> p h k a", h=N_HEAD, k=TOPK)
        scores = region(1024, 1024).rearrange("p (s n) -> p s n", n=KEYS)
        cand = region(2048, 1024).rearrange("p (h a b) -> p h a b", h=N_HEAD, a=TOPK)
        cand_h = region(2048, 1024).rearrange("p (h c) -> p h c", h=N_HEAD)
        top_f = region(3072, 128).rearrange("p (s k) -> p s k", k=TOPK)
        pos_f = region(3200, 128).rearrange("p (c s) -> p c s", c=2)
        pos_u = region(3328, 128).bitcast(u32).rearrange("p (c s) -> p c s", c=2)
        memn_t = ring[:, 0:2, :].rearrange("p a (k m) -> p (a k) m", m=N_MEM)
        mem_k_row = ring[:, 2:4, :]
        mem_row = ring[:, 4:6, :]
        mem_junk = ring[:, 6:8, :]
        ss, root, rinv = small[:, 0:4], small[:, 4:8], small[:, 8:12]
        mx, nmx, lsum, linv = small[:, 16:24], small[:, 24:32], small[:, 32:40], small[:, 40:48]
        f_ss, f_root, f_rinv = small[:, 48:49], small[:, 49:50], small[:, 50:51]
        m_ss, m_root, m_rinv = small[:, 52:54], small[:, 54:56], small[:, 56:58]
        rmix = small[:, 58:59]
        kv2 = small[:, 60:62]
        conv_root = row_b[:, 0:P]
        conv_x = row_b[:, 512:1024].rearrange("p (c t) -> p c t", t=P)

        acc = ctx.enter_context(nc.psum_tensor("acc", [P, D], f32))
        g = ctx.enter_context(nc.psum_tensor("g", [P, 4, 512], f32))
        tp = ctx.enter_context(nc.psum_tensor("tp", [P, 2, 512], f32))
        g01 = g[:, 0:2, :].rearrange("p b n -> p (b n)")
        g23 = g[:, 2:4, :].rearrange("p b n -> p (b n)")
        g12 = g[:, 1:3, :].rearrange("p b n -> p (b n)")

        loaded = {n: sem("loaded_" + n) for n in ("input", "mixer", "memory", "experts")}
        input_landed = sem("input_landed")
        w_landed = [sem(f"weights_landed_{s}") for s in range(WRING)]
        w_used = sem("weights_used")
        landed = [sem(f"rows_landed_{r}") for r in range(RING)]
        granted = sem("pool_granted")
        dve_granted = sem("dve_granted")
        act_granted = sem("act_granted")
        idx_staged = sem("indices_staged")
        idx_ready = sem("indices_ready")
        u_used = sem("u_rows_used")
        v_used_pe = sem("v_rows_used_by_pe")
        v_used_dve = sem("v_rows_used_by_dve")
        a_copied = sem("a_copied")
        gelu_ready = sem("gelu_ready")
        weight_ready = sem("weight_ready")
        diag_ready = sem("diag_ready")
        y_ready = sem("y_ready")
        y_root_ready = sem("y_root_ready")
        y_normed = sem("y_normed")
        stored = sem("y_row_free")
        h_taken = sem("h_taken")
        filled = sem("transposed_bank_filled")
        drained = sem("transposed_bank_drained")
        dve_step = sem("dve_step")
        act_step = sem("act_step")
        zeroed = sem("caches_zeroed")
        hn_taken = sem("expert_input_taken")
        memT_scaled = sem("memory_scaled")
        mem_root = sem("memory_root")
        mem_rinv_ready = sem("memory_rinv_ready")
        mem_saved = sem("memory_saved")
        x_scaled = sem("x_scaled")
        root_ready = sem("root_ready")
        rmix_ready = sem("input_rinv_ready")
        k_rope_copied = sem("k_rope_copied")
        lat_normed = sem("latents_normed")
        sig_ready = sem("sigmoid_ready")
        u_ready = sem("conv_row_ready")
        up_ready = sem("up_ready")
        up_saved = sem("up_saved")
        roped = sem("roped")
        s_ready = sem("attention_scores_ready")
        s_masked = sem("attention_scores_masked")
        p_ready = sem("attention_probs_ready")
        pv_done = sem("attention_values_done")
        attn_ready = sem("attention_row_ready")
        hist_read = sem("conv_history_saved")
        conv_done = sem("conv_done")
        stat_ready = sem("conv_stat_ready")
        centred = sem("conv_centred")
        squared = sem("conv_squared")
        conv_rooted = sem("conv_rooted")
        conv_normed = sem("conv_normed")
        cat_ready = sem("conv_output_ready")
        h_mixed = sem("h_mixed")
        h_row = sem("memory_input_row_ready")
        mq_saved = sem("memory_query_saved")
        ms_ready = sem("memory_scores_ready")
        ms_max = sem("memory_scores_max")
        mp_ready = sem("memory_probs_ready")
        mo_ready = sem("memory_values_ready")
        mo_row = sem("memory_row_ready")
        h_remembered = sem("h_remembered")
        hn_ready = sem("expert_input_ready")
        pq_saved = sem("peer_query_saved")
        sub_ready = sem("sub_scores_ready")
        sub_saved = sem("sub_scores_saved")
        best_shifted = sem("best_shifted")
        best_exp = sem("best_exp")
        picked_ready = sem("picked_ready")

        block = ctx.enter_context(nc.Block())

        def hold(eng, tick, s, value):
            eng.wait_ge(s, value)
            if not isinstance(value, int):
                eng.sem_inc(tick, 1)

        def first_of(t):
            return isinstance(t, int) and t == 0

        def chunk_number(t, n):
            if first_of(t) and n < W_BEFORE_MEMORY:
                return n
            return len(W_MEMORY) + PER_TILE * t + n

        def used_after(t, n):
            return chunk_number(t, n - 1) + 1

        def place(t, n):
            return (n if first_of(t) and n < W_BEFORE_MEMORY else len(W_MEMORY) + n) % WRING

        def landed_value(t, n):
            if first_of(t):
                return 16 * (chunk_number(t, n) // WRING + 1)
            return 16 * (PER_TILE // WRING) * t + 16 * ((len(W_MEMORY) + n) // WRING + 1)

        def bank_number(t, n):
            return n if first_of(t) and n < T_HMEM else of_tile(t, T_TILE, T_MEMORY + n)

        def u_sequence(t, g):
            return of_tile(t, 2 * GROUPS, 1 - HALF_GROUPS) + g * 2

        def u_sequence_start(g):
            return 1 + g

        def v_sequence(t, g, last_tile=False):
            if last_tile:
                return of_tile(t, 2 * GROUPS, HALF_GROUPS + 1 + HALF_GROUPS) + g
            return of_tile(t, 2 * GROUPS, HALF_GROUPS + 2) + g * 2

        def v_count(t, g, by, n):
            return of_tile(t, GROUPS * len(by), len(by) + n) + g * len(by)

        @block.sync
        def _(sp):
            def constants(name, pairs):
                for dst, src in pairs:
                    sp.dma_start(dst, src).then_inc(loaded[name], 16)

            def weight_dma(spec, slot):
                name, k, col, cols = spec
                sp.dma_start(wring[:, slot, 0:cols], dram[name][k * P:(k + 1) * P, col:col + cols]) \
                  .then_inc(w_landed[slot], 16)

            def inputs(t):
                sp.dma_start(h[:, :], dram["x"][bass.ds(t * P, P), :]).then_inc(input_landed, 16)
                sp.dma_start(ta[:, :, :], dram["xT"][bass.ds(t * P, P), :, :]).then_inc(input_landed, 16)
                sp.dma_start(mask[:, :], dram["mask"][bass.ds(t * P, P), :]).then_inc(input_landed, 16)
                sp.dma_start(rope[:, :, :], dram["rope"][bass.ds(t * P, P), :, :]).then_inc(input_landed, 16)

            def tile_weights(t, first, end):
                for n in range(first, end):
                    if not first_of(t) or n >= WRING:
                        sp.wait_ge(w_used, chunk_number(t, n) - WRING + 1)
                    weight_dma(W_TILE[n], place(t, n))

            constants("input", [(mix_gT[:, :], dram["mix_gT"])])
            inputs(0)
            tile_weights(0, 0, WRING)
            constants("mixer", [
                (ident[:, :], dram["ident"]),
                (latent_g[:, 0:Q_RANK], dram["q_latent_g"].to_broadcast([P, Q_RANK])),
                (latent_g[:, Q_RANK:], dram["kv_latent_g"].to_broadcast([P, KV_RANK])),
                (w_q_up[:, :, :], dram["w_q_up"].rearrange("(k p) n -> p k n", p=P)),
                (w_kv_up[:, :], dram["w_kv_up"]),
                (conv_wT[:, :, :], dram["conv_wT"]), (conv_p[:, :, :], dram["conv_p"])])
            tile_weights(0, WRING, W_BEFORE_MEMORY)
            constants("memory", [
                (memkv_gT[:, :], dram["memkv_gT"]), (mem_gT[:, :], dram["mem_gT"]), (memn_t, dram["memT"]),
                (mem_row, dram["mem"].rearrange("(m p) d -> p m d", p=P))])
            for m, spec in enumerate(W_MEMORY):
                sp.wait_ge(w_used, W_BEFORE_MEMORY + m - WRING + 1)
                weight_dma(spec, (W_BEFORE_MEMORY + m) % WRING)
            constants("experts", [
                (iota[:, :], dram["iota"].to_broadcast([P, TOPK])),
                (ffn_g[:, :], dram["norm_ffn_g"].to_broadcast([P, D])),
                (final_g[:, :], dram["final_norm_g"].to_broadcast([P, D])),
                (sub_keysT[:, :, :], dram["sub_keysT"])])
            tile_weights(0, W_BEFORE_MEMORY, PER_TILE)
            with sp.Fori(1, TILES) as t:
                sp.wait_ge(h_taken, t)
                sp.wait_ge(w_used, chunk_number(t, 0))
                inputs(t)
                tile_weights(t, 0, PER_TILE)
            sp.wait_ge(stored, 16 * (TILES + 1))

        @block.gpsimd
        def _(pool):
            pool.memset(key_cache[:, :, :], 0.0).then_inc(zeroed, 1)
            pool.memset(value_cache[:, :, :], 0.0).then_inc(zeroed, 1)
            pool.memset(u_t[:, :, :], 0.0).then_inc(zeroed, 1)
            pool.memset(mean_w[:, :], 1.0 / CONV).then_inc(zeroed, 1)
            pool.memset(eps[:, :], EPS).then_inc(zeroed, 1)

            def stage(group, turn, sequence):
                pool.tensor_copy(idx_group[:, turn, :], idx[:, bass.ds(group * RING, RING)]).then_inc(idx_staged, 1)
                hold(pool, granted, idx_staged, sequence)

            def fetch(table, r, turn):
                pool.indirect_dma_start(ring[:, r, :], None, dram[table],
                                        bass.IndirectOffsetOnAxis(ap=idx_group[:, turn, r:r + 1], axis=0)) \
                    .then_inc(landed[r], 16)

            def v_place_free(t, group, r):
                by, used = (BY_PE, v_used_pe) if r in BY_PE else (BY_DVE, v_used_dve)
                hold(pool, granted, used, v_count(t, group, by, by.index(r) + 1))

            def u_place_free(t, group, r):
                hold(pool, granted, u_used, of_tile(t, SLOTS, r + 1) + group * RING)

            def u_group(t, group, turn, v_before):
                stage(group, turn, u_sequence(t, group))
                for r in range(RING):
                    v_place_free(*v_before, r)
                    fetch("peer_u", r, turn)

            def v_group(t, group, turn, u_before):
                stage(group, turn, v_sequence(t, group))
                for r in range(RING):
                    u_place_free(*u_before, r)
                    fetch("peer_v", r, turn)

            def first_half(t):
                u_place_free(t, HALF_GROUPS - 1, RING - 1)
                u_group(t, HALF_GROUPS, 0, (t, -1))
                v_group(t, 0, 1, (t, HALF_GROUPS))
                with pool.Fori(1, HALF_GROUPS) as s:
                    u_group(t, s + HALF_GROUPS, 0, (t, s - 1))
                    v_group(t, s, 1, (t, s + HALF_GROUPS))

            hold(pool, granted, idx_ready, 1)
            for s in range(HALF_GROUPS):
                stage(s, s % 2, u_sequence_start(s))
                for r in range(RING):
                    if s:
                        u_place_free(0, s - 1, r)
                    fetch("peer_u", r, s % 2)
            with pool.Fori(0, TILES - 1) as t:
                hold(pool, granted, idx_ready, of_tile(t, 2, 2))
                first_half(t)
                hold(pool, granted, idx_ready, of_tile(t, 2, 3))
                with pool.Fori(0, HALF_GROUPS) as s:
                    u_group(t + 1, s, 0, (t, s + HALF_GROUPS - 1))
                    v_group(t, s + HALF_GROUPS, 1, (t + 1, s))
            hold(pool, granted, idx_ready, 2 * TILES)
            first_half(TILES - 1)
            with pool.Fori(0, HALF_GROUPS // 2) as j:
                for turn in range(2):
                    g8 = j * 2 + HALF_GROUPS + turn
                    stage(g8, turn, v_sequence(TILES - 1, g8, last_tile=True))
                    for r in range(RING):
                        v_place_free(TILES - 1, g8 - 1, r)
                        fetch("peer_v", r, turn)

        @block.scalar
        def _(act):
            ACT_STEPS = 4
            done = [0, 0]
            at = [0]

            def own(t, n):
                return n + (n > 2) if first_of(t) else of_tile(t, ACT_STEPS, n + 1)

            def settle(t, ins):
                assert not at[0] or done[0] == ACT_STEPS
                done[at[0]] += 1
                ins.then_inc(act_step, 1)
                act.wait_ge(act_step, own(t, done[at[0]]))

            def next_tile():
                assert done[0] == ACT_STEPS, done
                done[0], done[1] = done[1], 0

            def drain(t, n, dst, rows=P, blocks=4):
                act.wait_ge(filled, bank_number(t, n) + 1)
                act.activation(dst, tp[0:rows, n % 2, 0:blocks * P].rearrange("p (b t) -> p b t", t=P), ACT.Copy) \
                   .then_inc(drained, 1)

            act.wait_ge(zeroed, 5)

            def memory(t, half):
                if half == 0:
                    act.wait_ge(loaded["memory"], 64)
                    for m in range(MEM_TILES):
                        last = act.activation(mem_junk[:, m, :], mem_row[:, m, :], ACT.Square, accum_out=m_ss[:, m:m + 1])
                    last.then_inc(act_step, 1)
                    act.wait_ge(act_step, 3)
                    act.activation(m_root[:, :], m_ss[:, :], ACT.Sqrt, scale=1.0 / D, bias=eps[:, 0:1]) \
                       .then_inc(mem_root, 1)
                    act.wait_ge(mem_rinv_ready, 1)
                act.wait_ge(w_used, W_BEFORE_MEMORY + (half + 1) * KT)
                rows = mem_k_row if half == 0 else mem_v
                for m in range(MEM_TILES):
                    act.activation(rows[:, m, :], (g01, g23)[m], ACT.Copy, scale=m_rinv[:, m:m + 1]) \
                       .then_inc(mem_saved, 1)
                if half == 0:
                    for n in range(4):
                        act.wait_ge(filled, T_HMEM + n + 1)
                        act.activation(mem_kT[:, 4 * (n % 2):4 * (n % 2) + 4, (n // 2) * P:(n // 2 + 1) * P],
                                       tp[:, n % 2, :].rearrange("p (b t) -> p b t", t=P), ACT.Copy).then_inc(drained, 1)

            def inputs(t):
                act.wait_ge(input_landed, of_tile(t, 64, 64))
                settle(t, act.activation(row_a[:, :], h[:, :], ACT.Square, accum_out=ss[:, 0:1]))
                act.activation(root[:, 0:1], ss[:, 0:1], ACT.Sqrt, scale=1.0 / D, bias=eps[:, 0:1]) \
                   .then_inc(root_ready, 1)

            def latents(t):
                act.wait_ge(rmix_ready, of_tile(t, 1, 1))
                if not first_of(t):
                    act.wait_ge(picked_ready, of_tile(t, 4, 0))
                act.wait_ge(w_used, used_after(t, KT))
                act.activation(qk[:, HEADS, NOPE:QK], g[:, 0, Q_RANK + KV_RANK:LATENT], ACT.Copy, scale=rmix) \
                   .then_inc(k_rope_copied, 1)
                act.activation(lat_row[:, 0:Q_RANK], g[:, 0, 0:Q_RANK], ACT.Square, scale=rmix, accum_out=ss[:, 1:2])
                settle(t, act.activation(lat_row[:, Q_RANK:], g[:, 0, Q_RANK:Q_RANK + KV_RANK], ACT.Square,
                                         scale=rmix, accum_out=ss[:, 2:3]))
                act.activation(root[:, 1:2], ss[:, 1:2], ACT.Sqrt, scale=1.0 / Q_RANK, bias=eps[:, 0:1])
                act.activation(root[:, 2:3], ss[:, 2:3], ACT.Sqrt, scale=1.0 / KV_RANK, bias=eps[:, 0:1]) \
                   .then_inc(root_ready, 1)

            def conv_input(t):
                act.wait_ge(w_used, used_after(t, 2 * KT))
                act.activation(sig, g[:, 2, :], ACT.Sigmoid, scale=rmix).then_inc(sig_ready, 1)
                drain(t, T_LATENT, lat_t[:, :, :], blocks=3)
                drain(t, T_CONV, u_t[:, :, HIST:])

            def queries_keys(t):
                act.wait_ge(up_ready, of_tile(t, 2, 1))
                act.activation(qk[:, 0:5, :], g[:, 3, 0:5 * QK].rearrange("p (h d) -> p h d", d=QK), ACT.Copy)
                act.activation(qk[:, 5:8, :], g[:, 0, 0:3 * QK].rearrange("p (h d) -> p h d", d=QK), ACT.Copy) \
                   .then_inc(up_saved, 1)
                act.wait_ge(up_ready, of_tile(t, 2, 2))
                kv = g12.rearrange("p (h d) -> p h d", d=NOPE + VDIM)
                act.activation(kfull[:, :, 0:NOPE], kv[:, :, 0:NOPE], ACT.Copy).then_inc(up_saved, 1)
                act.activation(value_cache[:, bass.ds(t, 1), :].rearrange("p a (h d) -> p (a h) d", d=VDIM),
                               kv[:, :, NOPE:], ACT.Copy).then_inc(up_saved, 1)
                for n in range(2):
                    drain(t, T_Q + n, q_t[0:QK, 4 * n:4 * n + 4, :], rows=QK)
                for n in range(2):
                    hold(act, act_granted, filled, bank_number(t, T_K + n) + 1)
                    act.activation(key_cache[0:QK, 4 * n:4 * n + 4, bass.ds(t * P, P)],
                                   tp[0:QK, n, :].rearrange("p (b t) -> p b t", t=P), ACT.Copy).then_inc(drained, 1)

            def head(t, n):
                act.wait_ge(s_masked, of_tile(t, 2 * HEADS, 2 * n + 2))
                act.activation(probs[:, n % 2, :], probs[:, n % 2, :], ACT.Exp, scale=MLA_SCALE,
                               bias=nmx[:, n:n + 1], accum_out=lsum[:, n:n + 1]).then_inc(p_ready, 1)
                if n >= 2:
                    act.wait_ge(pv_done, of_tile(t, HEADS, n - 1))
                drain(t, T_P + n, probs_t[:, n % 2, :, :])

            def attended(t):
                drain(t, T_ATTN, ta[:, 0:2, :], blocks=2)
                drain(t, T_ATTN + 1, ta[:, 2:4, :], blocks=2)

            def conv_norm(t):
                act.wait_ge(centred, of_tile(t, 1, 1))
                act.activation(conv_acc[:, :, :], conv_x, ACT.Square).then_inc(squared, 1)
                act.wait_ge(stat_ready, of_tile(t, 2, 2))
                act.activation(conv_root, g[:, 3, P:2 * P], ACT.Sqrt, bias=eps[:, 0:1]).then_inc(conv_rooted, 1)
                act.wait_ge(conv_normed, of_tile(t, 1, 1))
                for c in range(CT):
                    last = act.activation(ta[:, 4 + c, :], conv_x[:, c, :], ACT.Silu, scale=conv_p[:, 1, c:c + 1],
                                          bias=conv_p[:, 2, c:c + 1])
                last.then_inc(cat_ready, 1)

            def norm_root(t, column):
                settle(t, act.activation(row_a[:, :], h[:, :], ACT.Square, accum_out=ss[:, column:column + 1]))
                act.activation(root[:, column:column + 1], ss[:, column:column + 1], ACT.Sqrt, scale=1.0 / D,
                               bias=eps[:, 0:1]).then_inc(root_ready, 1)

            def mem_norm(t):
                act.wait_ge(h_mixed, of_tile(t, 1, 1))
                norm_root(t, 3)
                for n in range(2):
                    act.wait_ge(filled, bank_number(t, T_HMEM + n) + 1)
                    for b in range(4):
                        last = act.activation(ta[:, 4 * n + b, :], tp[:, n, b * P:(b + 1) * P], ACT.Copy,
                                              scale=mem_gT[:, 4 * n + b:4 * n + b + 1])
                    last.then_inc(drained, 1)

            def mem_query(t):
                act.wait_ge(w_used, used_after(t, 4 * KT))
                act.activation(row_b[:, :], g23, ACT.Copy).then_inc(mq_saved, 1)
                for n in range(2):
                    drain(t, T_QMEM + n, tb[:, 4 * n:4 * n + 4, :])

            def mem_scores(t):
                act.wait_ge(ms_max, of_tile(t, 2, 2))
                for n in range(MEM_HEADS):
                    last = act.activation(row_b[:, n * N_MEM:(n + 1) * N_MEM], g01[:, n * N_MEM:(n + 1) * N_MEM],
                                          ACT.Exp, scale=MEM_SCALE, bias=nmx[:, n:n + 1],
                                          accum_out=lsum[:, n:n + 1])
                last.then_inc(mp_ready, 1)
                for n in range(2):
                    drain(t, T_PMEM + n, tb[:, 4 * n:4 * n + 4, :])

            def mem_values(t):
                for n in range(2):
                    drain(t, T_OMEM + n, ta[:, 4 * n:4 * n + 4, :])

            def peer_norm(t):
                act.wait_ge(h_remembered, of_tile(t, 1, 1))
                norm_root(t, 3)
                for n in range(2):
                    drain(t, T_HFFN + n, ta[:, 4 * n:4 * n + 4, :])

            def peer_query(t, half):
                act.wait_ge(w_used, used_after(t, (6 + half) * KT))
                act.activation(row_b[:, :], g23, ACT.Copy).then_inc(pq_saved, 1)
                if half:
                    act.wait_ge(picked_ready, of_tile(t, 4, 2))
                for n in range(2):
                    drain(t, T_QPEER + 2 * half + n, qp_t[:, 4 * n:4 * n + 4, :])

            def sub_scores(t, half):
                for n in range(2):
                    act.wait_ge(sub_ready, of_tile(t, 4, 2 * half + n + 1))
                    act.activation(scores[:, 4 * n:4 * n + 4, :], g[:, n, :].rearrange("p (s n) -> p s n", n=KEYS),
                                   ACT.Copy).then_inc(sub_saved, 1)

            def gates(t, half):
                act.wait_ge(best_shifted, of_tile(t, 2, half + 1))
                part = gate[:, half * SLOTS // 2:(half + 1) * SLOTS // 2]
                act.activation(part, part, ACT.Exp).then_inc(best_exp, 1)

            def gelu(t, half):
                act.wait_ge(a_copied, of_tile(t, GROUPS, (half + 1) * HALF_GROUPS))
                part = slice(half * SLOTS // 2, (half + 1) * SLOTS // 2)
                act.activation(gelu_a[:, part], a_all[:, part], ACT.Gelu).then_inc(gelu_ready, 1)
                act.wait_ge(weight_ready, of_tile(t, 2, half + 1))

            def v_group(t, group):
                for j, r in enumerate(BY_PE):
                    hold(act, act_granted, v_used_pe, v_count(t, group - 1, BY_PE, j + 1))
                    act.activation(diag[:, j, :], ident[:, :], ACT.Copy,
                                   scale=weight[:, bass.ds(group * RING + r, 1)]).then_inc(diag_ready, 1)

            def finish(t):
                act.wait_ge(y_ready, t + 2)
                act.activation(row_a[:, :], y_row[:, :], ACT.Square, accum_out=f_ss).then_inc(y_root_ready, 1)
                act.wait_ge(y_root_ready, of_tile(t, 2, 1))
                act.activation(f_root, f_ss, ACT.Sqrt, scale=1.0 / D, bias=eps[:, 0:1]).then_inc(y_root_ready, 1)
                hold(act, act_granted, y_normed, of_tile(t, 2, 2))
                act.dma_start(out[bass.ds(t * P, P), :], y_row[:, :]).then_inc(stored, 16)

            stages = dict(inputs=inputs, latents=latents, conv_input=conv_input, queries_keys=queries_keys, head=head,
                          memory=memory, attended=attended, conv_norm=conv_norm, mem_norm=mem_norm,
                          mem_query=mem_query, mem_scores=mem_scores, mem_values=mem_values, peer_norm=peer_norm,
                          peer_query=peer_query, sub_scores=sub_scores, gates=gates)

            def run(t, steps, u=None, v=None):
                groups = {"u rows": u, "v rows": v}
                passed = dict.fromkeys(groups, 0)
                for name, *args in steps:
                    at[0] = name == "next tile"
                    if name in groups:
                        if groups[name]:
                            groups[name](passed[name])
                        passed[name] += 1
                    elif at[0] and args[0] in stages:
                        stages[args[0]](t + 1, *args[1:])
                    elif name in stages:
                        stages[name](t, *args)

            def tile(t, late):
                run(t + 1, EARLY, v=lambda k: v_group(t, k))
                gelu(t, 1)
                run(t + 1, late, v=lambda k: v_group(t, HALF_GROUPS + k))
                gelu(t + 1, 0)
                finish(t)
                next_tile()

            run(0, FIRST)
            run(0, LATE)
            next_tile()
            gelu(0, 0)
            with act.Fori(0, TILES - 2) as t:
                tile(t, LATE)
            tile(TILES - 2, LATE_LAST)
            with act.Fori(0, HALF_GROUPS) as group:
                v_group(TILES - 1, group)
            gelu(TILES - 1, 1)
            with act.Fori(HALF_GROUPS, GROUPS) as group:
                v_group(TILES - 1, group)
            finish(TILES - 1)

        @block.vector
        def _(dve):
            DVE_STEPS = 165
            BASE = 1
            done = [0, 0]
            at = [0]

            def step_of(t, n):
                return of_tile(t, DVE_STEPS, BASE + n)

            def note(ins):
                assert not at[0] or done[0] == DVE_STEPS, done
                done[at[0]] += 1
                ins.then_inc(dve_step, 1)

            def next_tile():
                assert done[0] == DVE_STEPS, done
                done[0], done[1] = done[1], 0

            def settle(t):
                dve.wait_ge(dve_step, step_of(t, done[at[0]]))

            def settle_held(t):
                hold(dve, dve_granted, dve_step, step_of(t, done[at[0]]))

            dve.wait_ge(zeroed, 5)
            dve.memset(a_group[:, :], 0.0).then_inc(dve_step, 1)
            dve.sem_inc(y_ready, 1)
            dve.sem_inc(stored, 16)
            dve.sem_inc(v_used_pe, len(BY_PE))
            dve.sem_inc(v_used_dve, len(BY_DVE))
            dve.wait_ge(dve_step, 1)
            dve.wait_ge(loaded["input"], 16)

            def memory(t, half):
                if half == 0:
                    dve.wait_ge(loaded["memory"], 64)
                    dve.tensor_tensor(memn_t, memn_t, memkv_gT[:, :].unsqueeze(2).to_broadcast([P, KT, N_MEM]),
                                      ALU.mult).then_inc(memT_scaled, 1)
                    dve.wait_ge(mem_root, 1)
                    dve.reciprocal(m_rinv[:, :], m_root[:, :]).then_inc(mem_rinv_ready, 1)

            def inputs(t):
                dve.wait_ge(input_landed, of_tile(t, 64, 64))
                dve.tensor_tensor(ta[:, :, :], ta[:, :, :], mix_gT[:, :].unsqueeze(2).to_broadcast([P, KT, P]),
                                  ALU.mult).then_inc(x_scaled, 1)
                dve.wait_ge(root_ready, of_tile(t, 4, 1))
                dve.reciprocal(rmix, root[:, 0:1]).then_inc(rmix_ready, 1)

            def latents(t):
                if first_of(t):
                    dve.wait_ge(loaded["mixer"], 16 * 7)
                dve.wait_ge(rmix_ready, of_tile(t, 1, 1))
                dve.wait_ge(root_ready, of_tile(t, 4, 2))
                note(dve.reciprocal(rinv[:, 1:3], root[:, 1:3]))
                settle(t)
                note(dve.tensor_scalar(kv2, rinv[:, 1:3], rmix, None, ALU.mult))
                settle(t)
                dve.scalar_tensor_tensor(lat_row[:, 0:Q_RANK], g[:, 0, 0:Q_RANK], kv2[:, 0:1], latent_g[:, 0:Q_RANK],
                                         ALU.mult, ALU.mult)
                dve.scalar_tensor_tensor(lat_row[:, Q_RANK:], g[:, 0, Q_RANK:Q_RANK + KV_RANK], kv2[:, 1:2],
                                         latent_g[:, Q_RANK:], ALU.mult, ALU.mult).then_inc(lat_normed, 1)

            def conv_input(t):
                dve.wait_ge(sig_ready, of_tile(t, 1, 1))
                dve.scalar_tensor_tensor(u_row, g[:, 1, :], rmix, sig, ALU.mult, ALU.mult).then_inc(u_ready, 1)

            def queries_keys(t):
                dve.wait_ge(up_saved, of_tile(t, 3, 1))
                dve.wait_ge(k_rope_copied, of_tile(t, 1, 1))
                n9 = [P, HEADS + 1, HALF]
                cos, sin = (rope[:, c:c + 1, :].to_broadcast(n9) for c in range(2))
                x1, x2 = qk[:, :, NOPE:NOPE + HALF], qk[:, :, NOPE + HALF:QK]
                w = (HEADS + 1) * HALF
                t1, t2, t3, t4 = (row_b[:, c * w:(c + 1) * w].rearrange("p (h d) -> p h d", d=HALF) for c in range(4))
                dve.tensor_tensor(t1, x1, cos, ALU.mult)
                dve.tensor_tensor(t2, x2, sin, ALU.mult)
                dve.tensor_tensor(t3, x1, sin, ALU.mult)
                note(dve.tensor_tensor(t4, x2, cos, ALU.mult))
                settle(t)
                dve.tensor_tensor(x1, t1, t2, ALU.subtract)
                dve.tensor_tensor(x2, t3, t4, ALU.add).then_inc(roped, 1)
                dve.wait_ge(roped, of_tile(t, 2, 1))
                dve.tensor_copy(kfull[:, :, NOPE:QK], qk[:, HEADS:HEADS + 1, NOPE:QK].to_broadcast([P, HEADS, ROPE])) \
                   .then_inc(roped, 1)

            def head(t, n):
                dve.wait_ge(s_ready, of_tile(t, HEADS, n + 1))
                if n >= 2:
                    dve.wait_ge(filled, bank_number(t, T_P + n - 2) + 1)
                dve.tensor_tensor(probs[:, n % 2, :], g[:, n % 2, :], mask[:, :], ALU.add).then_inc(s_masked, 1)
                dve.wait_ge(s_masked, of_tile(t, 2 * HEADS, 2 * n + 1))
                note(dve.tensor_reduce(mx[:, n:n + 1], probs[:, n % 2, :], AX.X, ALU.max))
                settle(t)
                dve.tensor_scalar(nmx[:, n:n + 1], mx[:, n:n + 1], -MLA_SCALE, None, ALU.mult).then_inc(s_masked, 1)

            def conv(t, n):
                if n == 0:
                    dve.wait_ge(drained, bank_number(t, T_CONV) + 1)
                    for c in range(CT):
                        ins = dve.tensor_scalar(conv_acc[:, c, :], u_t[:, c, 0:P], conv_wT[:, c, 0:1],
                                                conv_p[:, 0, c:c + 1], ALU.mult, ALU.add)
                    note(ins)
                for k in range(1 + CONV_TAPS * n, 1 + CONV_TAPS * (n + 1)):
                    settle(t)
                    for c in range(CT):
                        ins = dve.scalar_tensor_tensor(conv_acc[:, c, :], u_t[:, c, k:k + P], conv_wT[:, c, k:k + 1],
                                                       conv_acc[:, c, :], ALU.mult, ALU.add)
                    note(ins)
                if n == len(CONV_STEPS) - 1:
                    dve.tensor_copy(u_t[:, :, 0:HIST], u_t[:, :, P:P + HIST]).then_inc(hist_read, 1)

            def attended(t):
                dve.wait_ge(p_ready, of_tile(t, HEADS, HEADS))
                note(dve.reciprocal(linv, lsum))
                settle(t)
                dve.wait_ge(pv_done, of_tile(t, HEADS, HEADS))
                dve.tensor_tensor(row_b[:, 0:512].rearrange("p (h d) -> p h d", d=VDIM),
                                  g[:, 2, :].rearrange("p (h d) -> p h d", d=VDIM),
                                  linv.unsqueeze(2).to_broadcast([P, HEADS, VDIM]), ALU.mult).then_inc(attn_ready, 1)

            def conv_norm(t):
                all4 = [P, CT, P]
                dve.wait_ge(stat_ready, of_tile(t, 2, 1))
                settle(t)
                dve.tensor_tensor(conv_x, conv_acc[:, :, :], g[:, 3:4, 0:P].to_broadcast(all4), ALU.subtract) \
                   .then_inc(centred, 1)
                dve.wait_ge(conv_rooted, of_tile(t, 1, 1))
                note(dve.reciprocal(conv_root, conv_root))
                settle(t)
                dve.tensor_tensor(conv_x, conv_x, row_b[:, 0:P].unsqueeze(1).to_broadcast(all4), ALU.mult) \
                   .then_inc(conv_normed, 1)

            def mix_out(t):
                dve.wait_ge(w_used, used_after(t, 3 * KT))
                dve.tensor_tensor(h[:, :], h[:, :], g01, ALU.add).then_inc(h_mixed, 1)

            def mem_norm(t):
                dve.wait_ge(root_ready, of_tile(t, 4, 3))
                note(dve.reciprocal(rinv[:, 3:4], root[:, 3:4]))
                settle(t)
                dve.tensor_scalar(row_a[:, :], h[:, :], rinv[:, 3:4], None, ALU.mult).then_inc(h_row, 1)

            def mem_scores(t):
                dve.wait_ge(ms_ready, of_tile(t, 1, 1))
                dve.tensor_reduce(mx[:, 0:4], g01.rearrange("p (h m) -> p h m", m=N_MEM), AX.X, ALU.max) \
                   .then_inc(ms_max, 1)
                dve.wait_ge(ms_max, of_tile(t, 2, 1))
                dve.tensor_scalar(nmx[:, 0:4], mx[:, 0:4], -MEM_SCALE, None, ALU.mult).then_inc(ms_max, 1)

            def mem_values(t):
                dve.wait_ge(mp_ready, of_tile(t, 1, 1))
                note(dve.reciprocal(linv[:, 0:4], lsum[:, 0:4]))
                settle(t)
                dve.wait_ge(mo_ready, of_tile(t, 1, 1))
                dve.tensor_tensor(row_a[:, :].rearrange("p (h d) -> p h d", d=MEM_DIM),
                                  g23.rearrange("p (h d) -> p h d", d=MEM_DIM),
                                  linv[:, 0:4].unsqueeze(2).to_broadcast([P, MEM_HEADS, MEM_DIM]), ALU.mult) \
                   .then_inc(mo_row, 1)

            def mem_out(t):
                dve.wait_ge(w_used, used_after(t, 5 * KT))
                dve.tensor_tensor(h[:, :], h[:, :], g01, ALU.add).then_inc(h_remembered, 1)

            def peer_norm(t):
                if first_of(t):
                    dve.wait_ge(loaded["experts"], 64)
                dve.wait_ge(root_ready, of_tile(t, 4, 4))
                note(dve.reciprocal(rinv[:, 3:4], root[:, 3:4]))
                settle(t)
                dve.scalar_tensor_tensor(row_a[:, :], h[:, :], rinv[:, 3:4], ffn_g[:, :], ALU.mult, ALU.mult) \
                   .then_inc(hn_ready, 1)
                dve.tensor_copy(h_kept[:, :], h[:, :]).then_inc(h_taken, 1)

            def next_input(t):
                dve.wait_ge(hn_ready, of_tile(t, 1, 1))
                dve.tensor_copy(hn[:, :], row_a[:, :]).then_inc(hn_taken, 1)
                hold(dve, dve_granted, hn_taken, of_tile(t, 1, 1))

            def best_16(t, values, indices, source, many):
                for s in many:
                    note(dve.max(values[:, s, 0:8], source[:, s, :]))
                settle_held(t)
                for s in many:
                    dve.max_index(indices[:, s, 0:8], values[:, s, 0:8], source[:, s, :])
                    note(dve.match_replace(source[:, s, :], values[:, s, 0:8], source[:, s, :], LOWEST))
                settle_held(t)
                for s in many:
                    note(dve.max(values[:, s, 8:16], source[:, s, :]))
                settle_held(t)
                for s in many:
                    note(dve.max_index(indices[:, s, 8:16], values[:, s, 8:16], source[:, s, :]))

            def sub_topk(t, half, q):
                hold(dve, dve_granted, sub_saved, of_tile(t, 4, 2 * half + q + 1))
                best_16(t, top_v, top_i, scores, range(4 * q, 4 * q + 4))

            def candidates(t, half):
                settle(t)
                n4 = [P, N_HEAD, TOPK, TOPK]
                halves = top_v[:, :, :].rearrange("p (h c) k -> p c h k", c=2)
                note(dve.tensor_tensor(cand, halves[:, 0, :, :].unsqueeze(3).to_broadcast(n4),
                                       halves[:, 1, :, :].unsqueeze(2).to_broadcast(n4), ALU.add))
                note(dve.tensor_copy(top_f, top_i[:, :, :]))
                settle_held(t)

            def best(t, half):
                best_16(t, best_v, best_p, cand_h, range(N_HEAD))

            def gates(t, half):
                settle(t)
                n3 = [P, N_HEAD, TOPK]
                gate3 = gate[:, half * SLOTS // 2:(half + 1) * SLOTS // 2].rearrange("p (h k) -> p h k", k=TOPK)
                dve.tensor_tensor(gate3, best_v[:, :, :], best_v[:, :, 0:1].to_broadcast(n3), ALU.subtract) \
                   .then_inc(best_shifted, 1)
                flat = best_p[:, :, :].rearrange("p h k -> p (h k)")
                dve.tensor_scalar(pos_u[:, 0, :], flat, 4, None, ALU.logical_shift_right)
                note(dve.tensor_scalar(pos_u[:, 1, :], flat, 15, None, ALU.bitwise_and))
                settle(t)
                note(dve.tensor_copy(pos_f, pos_u))
                dve.wait_ge(best_exp, of_tile(t, 2, half + 1))
                note(dve.tensor_reduce(mx[:, 0:N_HEAD], gate3, AX.X, ALU.add))
                settle(t)
                note(dve.reciprocal(linv[:, 0:N_HEAD], mx[:, 0:N_HEAD]))
                settle(t)
                note(dve.tensor_tensor(gate3, gate3, linv[:, 0:N_HEAD].unsqueeze(2).to_broadcast(n3), ALU.mult))

            def indices(t, half, c):
                n4 = [P, N_HEAD, TOPK, TOPK]
                tops = top_f.rearrange("p (h c) k -> p c h k", c=2)
                places = iota[:, :].unsqueeze(1).unsqueeze(1).to_broadcast(n4)
                pos = pos_f[:, c, :].rearrange("p (h k) -> p h k", k=TOPK).unsqueeze(3).to_broadcast(n4)
                settle(t)
                if c:
                    dve.wait_ge(picked_ready, of_tile(t, 4, 2 * half + 1))
                note(dve.tensor_tensor(onehot, pos, places, ALU.is_equal))
                settle(t)
                note(dve.tensor_tensor(onehot, onehot, tops[:, c, :, :].unsqueeze(2).to_broadcast(n4), ALU.mult))
                settle(t)
                dve.tensor_reduce(picked[:, c, :].rearrange("p (h k) -> p h k", k=TOPK), onehot, AX.X, ALU.add) \
                   .then_inc(picked_ready, 1)

            def publish(t, half):
                dve.wait_ge(picked_ready, of_tile(t, 4, 2 * half + 2))
                if not first_of(t):
                    dve.wait_ge(idx_staged, v_sequence(t - 1, (half + 1) * HALF_GROUPS - 1))
                dve.scalar_tensor_tensor(idx[:, half * SLOTS // 2:(half + 1) * SLOTS // 2], picked[:, 0, :], float(KEYS),
                                         picked[:, 1, :], ALU.mult, ALU.add).then_inc(idx_ready, 1)

            def u_group(t, group, sequence=None):
                for r in range(RING):
                    dve.wait_ge(landed[r], (u_sequence(t, group) if sequence is None else sequence) * 16)
                    dve.tensor_tensor_reduce(out=ring[:, r, :], in0=ring[:, r, :], in1=hn[:, :], scale=1.0, scalar=0.0,
                                             op0=ALU.mult, op1=ALU.add, accum_out=a_group[:, r:r + 1]) \
                       .then_inc(u_used, 1)
                hold(dve, dve_granted, u_used, of_tile(t, SLOTS, RING) + group * RING)
                dve.tensor_copy(a_all[:, bass.ds(group * RING, RING)], a_group[:, :]).then_inc(a_copied, 1)
                hold(dve, dve_granted, a_copied, of_tile(t, GROUPS, 1) + group)

            def weights(t, half):
                dve.wait_ge(gelu_ready, of_tile(t, 2, half + 1))
                part = slice(half * SLOTS // 2, (half + 1) * SLOTS // 2)
                dve.tensor_tensor(weight[:, part], gelu_a[:, part], gate[:, part], ALU.mult).then_inc(weight_ready, 1)
                hold(dve, dve_granted, weight_ready, of_tile(t, 2, half + 1))

            def v_group(t, group, first=False, last_tile=False):
                for j, r in enumerate(BY_DVE):
                    dve.wait_ge(landed[r], v_sequence(t, group, last_tile) * 16)
                    before = h_kept if first and j == 0 else y_acc
                    if first and j == 0:
                        dve.wait_ge(h_taken, of_tile(t, 1, 1))
                    dve.scalar_tensor_tensor(y_acc[:, :], ring[:, r, :], weight[:, bass.ds(group * RING + r, 1)],
                                             before[:, :], ALU.mult, ALU.add).then_inc(v_used_dve, 1)
                    hold(dve, dve_granted, v_used_dve, v_count(t, group, BY_DVE, j + 1))

            def finish(t):
                dve.wait_ge(v_used_pe, v_count(t, GROUPS, BY_PE, 0))
                dve.wait_ge(stored, of_tile(t, 16, 16))
                dve.tensor_tensor(y_row[:, :], acc[:, :], y_acc[:, :], ALU.add).then_inc(y_ready, 1)
                dve.wait_ge(y_root_ready, of_tile(t, 2, 2))
                dve.reciprocal(f_rinv, f_root).then_inc(y_normed, 1)
                dve.wait_ge(y_normed, of_tile(t, 2, 1))
                dve.scalar_tensor_tensor(y_row[:, :], y_row[:, :], f_rinv, final_g[:, :], ALU.mult, ALU.mult) \
                   .then_inc(y_normed, 1)

            stages = dict(inputs=inputs, latents=latents, conv_input=conv_input, queries_keys=queries_keys, head=head,
                          memory=memory, conv=conv, attended=attended, conv_norm=conv_norm, mix_out=mix_out,
                          mem_norm=mem_norm, mem_scores=mem_scores, mem_values=mem_values, mem_out=mem_out,
                          peer_norm=peer_norm, next_input=next_input, sub_topk=sub_topk, candidates=candidates,
                          best=best, gates=gates, indices=indices, publish=publish)

            def run(t, steps, u=None, v=None):
                groups = {"u rows": u, "v rows": v}
                passed = dict.fromkeys(groups, 0)
                for name, *args in steps:
                    at[0] = name == "next tile"
                    if name in groups:
                        if groups[name]:
                            groups[name](passed[name])
                        passed[name] += 1
                    elif at[0] and args[0] in stages:
                        stages[args[0]](t + 1, *args[1:])
                    elif name in stages:
                        stages[name](t, *args)

            def tile(t, late):
                run(t + 1, EARLY, u=lambda k: u_group(t, k + HALF_GROUPS), v=lambda k: v_group(t, k, first=k == 0))
                weights(t, 1)
                run(t + 1, late, u=lambda k: u_group(t + 1, k), v=lambda k: v_group(t, k + HALF_GROUPS))
                weights(t + 1, 0)
                finish(t)
                next_tile()

            run(0, FIRST)
            run(0, LATE, u=lambda k: u_group(0, k, u_sequence_start(k)))
            next_tile()
            weights(0, 0)
            with dve.Fori(0, TILES - 2) as t:
                tile(t, LATE)
            tile(TILES - 2, LATE_LAST)
            u_group(TILES - 1, HALF_GROUPS)
            v_group(TILES - 1, 0, first=True)
            with dve.Fori(1, HALF_GROUPS) as k:
                u_group(TILES - 1, k + HALF_GROUPS)
                v_group(TILES - 1, k)
            weights(TILES - 1, 1)
            with dve.Fori(HALF_GROUPS, GROUPS) as group:
                v_group(TILES - 1, group, last_tile=True)
            finish(TILES - 1)

        @block.tensor
        def _(pe):
            def fill(t, n, blocks, rows=P, number=None):
                number = bank_number(t, n) if number is None else number
                if not isinstance(number, int) or number >= 2:
                    pe.wait_ge(drained, number - 1)
                for b, src in enumerate(blocks):
                    last = pe.transpose(tp[0:rows, n % 2, b * P:(b + 1) * P], src, ident[:, :])
                last.then_inc(filled, 1)

            def is_drained(t, n):
                pe.wait_ge(drained, bank_number(t, n) + 1)

            def use(t, n, lhs, outs):
                pe.wait_ge(w_landed[place(t, n)], landed_value(t, n))
                for o, col, cols, start, stop in outs:
                    last = pe.matmul(o, lhs, wring[:, place(t, n), col:col + cols], start=start, stop=stop)
                last.then_inc(w_used, 1)

            def gemm(t, first, lhs_of, banks):
                for k in range(KT):
                    use(t, first + k, lhs_of(k), [(banks[n], 512 * n, 512, k == 0, k == KT - 1) for n in range(2)])

            pe.wait_ge(zeroed, 5)

            def memory(t, half):
                if half == 0:
                    pe.wait_ge(memT_scaled, 1)
                    pe.wait_ge(attn_ready, 1)
                else:
                    pe.wait_ge(mem_saved, 2)
                for k in range(KT):
                    c = W_BEFORE_MEMORY + half * KT + k
                    pe.wait_ge(w_landed[c % WRING], 16 * (c // WRING + 1))
                    for m in range(MEM_TILES):
                        for b in range(2):
                            last = pe.matmul(g[:, 2 * m + b, :], memn_t[:, k, m * P:(m + 1) * P],
                                             wring[:, c % WRING, b * 512:(b + 1) * 512], start=k == 0, stop=k == KT - 1)
                    last.then_inc(w_used, 1)
                if half == 0:
                    pe.wait_ge(mem_saved, 2)
                    for q in range(4):
                        fill(0, q, [mem_k_row[:, q // 2, (4 * (q % 2) + b) * P:(4 * (q % 2) + b + 1) * P]
                                    for b in range(4)], number=T_HMEM + q)

            def project(t):
                pe.wait_ge(x_scaled, of_tile(t, 1, 1))
                if not first_of(t):
                    pe.wait_ge(sub_saved, of_tile(t, 4, 0))
                for k in range(KT):
                    use(t, k, ta[:, k, :], [(g[:, 0, 0:LATENT], 0, LATENT, k == 0, k == KT - 1)])
                for k in range(KT):
                    use(t, KT + k, ta[:, k, :], [(g[:, 1, :], 0, 512, k == 0, k == KT - 1),
                                                 (g[:, 2, :], 512, 512, k == 0, k == KT - 1)])

            def latents(t):
                pe.wait_ge(lat_normed, of_tile(t, 1, 1))
                if first_of(t):
                    pe.wait_ge(loaded["mixer"], 16 * 7)
                fill(t, T_LATENT, [lat_row[:, b * P:(b + 1) * P] for b in range(3)])

            def conv_input(t):
                pe.wait_ge(u_ready, of_tile(t, 1, 1))
                if not isinstance(t, int):
                    pe.wait_ge(hist_read, t)
                fill(t, T_CONV, [u_row[:, b * P:(b + 1) * P] for b in range(4)])

            def queries_keys(t):
                is_drained(t, T_LATENT)
                pe.wait_ge(k_rope_copied, of_tile(t, 1, 1))
                for k in range(2):
                    pe.matmul(g[:, 3, 0:5 * QK], lat_t[:, k, :], w_q_up[:, k, 0:5 * QK], start=k == 0, stop=k == 1)
                    last = pe.matmul(g[:, 0, 0:3 * QK], lat_t[:, k, :], w_q_up[:, k, 5 * QK:], start=k == 0, stop=k == 1)
                last.then_inc(up_ready, 1)
                for b in range(2):
                    last = pe.matmul(g[:, 1 + b, :], lat_t[:, 2, :], w_kv_up[:, b * 512:(b + 1) * 512], start=True, stop=True)
                last.then_inc(up_ready, 1)
                pe.wait_ge(roped, of_tile(t, 2, 1))
                for n in range(2):
                    fill(t, T_Q + n, [qk[:, 4 * n + b, :] for b in range(4)], rows=QK)
                pe.wait_ge(roped, of_tile(t, 2, 2))
                pe.wait_ge(up_saved, of_tile(t, 3, 3))
                for n in range(2):
                    fill(t, T_K + n, [kfull[:, 4 * n + b, :] for b in range(4)], rows=QK)

            def scores_of(t, n):
                if n == 0:
                    is_drained(t, T_K + 1)
                else:
                    if n >= 2:
                        pe.wait_ge(s_masked, of_tile(t, 2 * HEADS, 2 * (n - 2) + 1))
                pe.matmul(g[:, n % 2, :], q_t[0:QK, n, :], key_cache[0:QK, n, :], start=True, stop=True) \
                  .then_inc(s_ready, 1)

            def values_of(t, n):
                is_drained(t, T_P + n)
                for j in range(TILES):
                    last = pe.matmul(g[:, 2, n * VDIM:(n + 1) * VDIM], probs_t[:, n % 2, j, :],
                                     value_cache[:, j, n * VDIM:(n + 1) * VDIM], start=j == 0, stop=j == TILES - 1)
                last.then_inc(pv_done, 1)

            def head(t, n):
                if n == 0:
                    scores_of(t, 0)
                if n + 1 < HEADS:
                    scores_of(t, n + 1)
                pe.wait_ge(p_ready, of_tile(t, HEADS, n + 1))
                fill(t, T_P + n, [probs[:, n % 2, j * P:(j + 1) * P] for j in range(TILES)])
                if n:
                    values_of(t, n - 1)
                if n == HEADS - 1:
                    values_of(t, n)

            def attended(t):
                pe.wait_ge(attn_ready, of_tile(t, 1, 1))
                for n in range(2):
                    fill(t, T_ATTN + n, [row_b[:, (2 * n + b) * P:(2 * n + b + 1) * P] for b in range(2)])

            def conv_norm(t):
                pe.wait_ge(hist_read, of_tile(t, 1, 1))
                if first_of(t):
                    pe.wait_ge(mem_saved, 2 * MEM_TILES)
                for c in range(CT):
                    last = pe.matmul(g[:, 3, 0:P], mean_w[:, :], conv_acc[:, c, :], start=c == 0, stop=c == CT - 1)
                last.then_inc(stat_ready, 1)
                pe.wait_ge(squared, of_tile(t, 1, 1))
                for c in range(CT):
                    last = pe.matmul(g[:, 3, P:2 * P], mean_w[:, :], conv_acc[:, c, :], start=c == 0, stop=c == CT - 1)
                last.then_inc(stat_ready, 1)

            def mix_out(t):
                is_drained(t, T_ATTN + 1)
                pe.wait_ge(cat_ready, of_tile(t, 1, 1))
                gemm(t, 2 * KT, lambda k: ta[:, k, :], (g[:, 0, :], g[:, 1, :]))

            def mem_norm(t):
                pe.wait_ge(h_row, of_tile(t, 1, 1))
                for n in range(2):
                    fill(t, T_HMEM + n, [row_a[:, (4 * n + b) * P:(4 * n + b + 1) * P] for b in range(4)])

            def mem_query(t):
                is_drained(t, T_HMEM + 1)
                gemm(t, 3 * KT, lambda k: ta[:, k, :], (g[:, 2, :], g[:, 3, :]))
                pe.wait_ge(mq_saved, of_tile(t, 1, 1))
                for n in range(2):
                    fill(t, T_QMEM + n, [row_b[:, (4 * n + b) * P:(4 * n + b + 1) * P] for b in range(4)])

            def mem_scores(t):
                is_drained(t, T_QMEM + 1)
                for n in range(MEM_HEADS):
                    for k in range(2):
                        last = pe.matmul(g[:, n // 2, (n % 2) * N_MEM:(n % 2 + 1) * N_MEM], tb[:, 2 * n + k, :],
                                         mem_kT[:, 2 * n + k, :], start=k == 0, stop=k == 1)
                last.then_inc(ms_ready, 1)
                pe.wait_ge(mp_ready, of_tile(t, 1, 1))
                for n in range(2):
                    fill(t, T_PMEM + n, [row_b[:, (4 * n + b) * P:(4 * n + b + 1) * P] for b in range(4)])

            def mem_values(t):
                is_drained(t, T_PMEM + 1)
                for n in range(MEM_HEADS):
                    for m in range(MEM_TILES):
                        last = pe.matmul(g[:, 2 + n // 2, (n % 2) * MEM_DIM:(n % 2 + 1) * MEM_DIM], tb[:, 2 * n + m, :],
                                         mem_v[:, m, n * MEM_DIM:(n + 1) * MEM_DIM], start=m == 0, stop=m == 1)
                last.then_inc(mo_ready, 1)
                pe.wait_ge(mo_row, of_tile(t, 1, 1))
                for n in range(2):
                    fill(t, T_OMEM + n, [row_a[:, (4 * n + b) * P:(4 * n + b + 1) * P] for b in range(4)])

            def mem_out(t):
                is_drained(t, T_OMEM + 1)
                gemm(t, 4 * KT, lambda k: ta[:, k, :], (g[:, 0, :], g[:, 1, :]))

            def peer_norm(t):
                pe.wait_ge(hn_ready, of_tile(t, 1, 1))
                for n in range(2):
                    fill(t, T_HFFN + n, [row_a[:, (4 * n + b) * P:(4 * n + b + 1) * P] for b in range(4)])

            def peer_query(t, half):
                is_drained(t, T_HFFN + 1)
                gemm(t, (5 + half) * KT, lambda k: ta[:, k, :], (g[:, 2, :], g[:, 3, :]))
                pe.wait_ge(pq_saved, of_tile(t, 2, half + 1))
                for n in range(2):
                    fill(t, T_QPEER + 2 * half + n, [row_b[:, (4 * n + b) * P:(4 * n + b + 1) * P] for b in range(4)])

            def sub_scores(t, half):
                if first_of(t):
                    pe.wait_ge(loaded["experts"], 64)
                is_drained(t, T_QPEER + 2 * half + 1)
                if half:
                    pe.wait_ge(sub_saved, of_tile(t, 4, 2))
                for n in range(2):
                    for b in range(4):
                        last = pe.matmul(g[:, n, b * P:(b + 1) * P], qp_t[:, 4 * n + b, :],
                                         sub_keysT[:, 8 * half + 4 * n + b, :], start=True, stop=True)
                    last.then_inc(sub_ready, 1)

            def v_group(t, group, first=False, last=False, last_tile=False):
                if first:
                    pe.wait_ge(y_ready, t + 1)
                for j, r in enumerate(BY_PE):
                    pe.wait_ge(landed[r], v_sequence(t, group, last_tile) * 16)
                    pe.wait_ge(diag_ready, of_tile(t, GROUPS * len(BY_PE), j + 1) + group * len(BY_PE))
                    for n in range(2):
                        ins = pe.matmul(acc[:, n * 512:(n + 1) * 512], diag[:, j, :], ring[:, r, n * 512:(n + 1) * 512],
                                        start=first and j == 0, stop=last and j == len(BY_PE) - 1)
                    ins.then_inc(v_used_pe, 1)

            stages = dict(project=project, latents=latents, conv_input=conv_input, queries_keys=queries_keys, head=head,
                          memory=memory, attended=attended, conv_norm=conv_norm, mix_out=mix_out, mem_norm=mem_norm,
                          mem_query=mem_query, mem_scores=mem_scores, mem_values=mem_values, mem_out=mem_out,
                          peer_norm=peer_norm, peer_query=peer_query, sub_scores=sub_scores)

            def run(t, steps, v=None):
                k = 0
                for name, *args in steps:
                    if name == "v rows":
                        if v:
                            v(k)
                        k += 1
                    elif name == "next tile" and args[0] in stages:
                        stages[args[0]](t + 1, *args[1:])
                    elif name in stages:
                        stages[name](t, *args)

            def tile(t, late):
                run(t + 1, EARLY, v=lambda k: v_group(t, k, first=k == 0))
                run(t + 1, late, v=lambda k: v_group(t, k + HALF_GROUPS, last=k == HALF_GROUPS - 1))

            run(0, FIRST)
            run(0, LATE)
            with pe.Fori(0, TILES - 2) as t:
                tile(t, LATE)
            tile(TILES - 2, LATE_LAST)
            v_group(TILES - 1, 0, first=True)
            with pe.Fori(1, HALF_GROUPS) as k:
                v_group(TILES - 1, k)
            with pe.Fori(HALF_GROUPS, GROUPS - 1) as group:
                v_group(TILES - 1, group, last_tile=True)
            v_group(TILES - 1, GROUPS - 1, last=True, last_tile=True)


def kernel(**inputs):
    import numpy as np
    import concourse.bacc as bacc
    from concourse import mybir as mb
    from concourse.bass_utils import run_bass_kernel_spmd

    def columns(v):
        return np.ascontiguousarray(np.asarray(v).reshape(-1, P).T)

    a = {k: np.asarray(v) for k, v in inputs.items()}
    x = a["x"][0]
    arrays = {
        "x": x,
        "xT": np.ascontiguousarray(x.reshape(TILES, P, KT, P).transpose(0, 3, 2, 1)).reshape(TILES * P, KT, P),
        "mem": a["mem"][0],
        "memT": np.ascontiguousarray(a["mem"][0].reshape(N_MEM, KT, P).transpose(2, 1, 0)),
        "mix_gT": columns(a["norm_mix_g"][0]), "mem_gT": columns(a["norm_mem_g"][0]),
        "memkv_gT": columns(a["mem_kv_norm_g"][0]),
        "q_latent_g": a["q_latent_g"], "kv_latent_g": a["kv_latent_g"],
        "norm_ffn_g": a["norm_ffn_g"], "final_norm_g": a["final_norm_g"].reshape(1, D),
        "conv_wT": np.ascontiguousarray(a["conv_w"][0, :, 0, :].reshape(TAPS, CT, P).transpose(2, 1, 0)),
        "conv_p": np.ascontiguousarray(np.stack([a[n][0].reshape(CT, P).T for n in ("conv_b", "conv_ln_g", "conv_ln_b")], 1)),
        "w_in": a["w_in"][0], "w_q_up": a["w_q_up"][0], "w_kv_up": a["w_kv_up"][0], "w_mix_out": a["w_mix_out"][0],
        "w_mem_q": a["w_mem_q"][0], "w_mem_kv": a["w_mem_kv"][0], "w_mem_out": a["w_mem_out"][0],
        "w_peer_query": a["w_peer_query"][0],
        "sub_keysT": np.ascontiguousarray(a["peer_sub_keys"][0].transpose(3, 0, 1, 2)).reshape(P, SETS, KEYS),
        "peer_u": a["peer_u"][0], "peer_v": a["peer_v"][0],
    }
    arrays["ident"] = np.eye(P, dtype=np.float32)
    arrays["iota"] = np.arange(TOPK, dtype=np.float32).reshape(1, TOPK)
    inv = (1.0 / (np.float32(10000.0) ** (np.arange(0, ROPE, 2, dtype=np.float32) / np.float32(ROPE)))).astype(np.float32)
    ang = np.arange(SEQ, dtype=np.float32)[:, None] * inv[None, :]
    arrays["rope"] = np.stack([np.cos(ang), np.sin(ang)], 1).astype(np.float32)
    chunk = np.arange(SEQ) // 64
    arrays["mask"] = np.where(chunk[None, :] <= chunk[:, None], 0.0, -1e30).astype(np.float32)

    nc = bacc.Bacc("TRN2", target_bir_lowering=False, num_devices=1)
    arrays = {n: np.ascontiguousarray(v) for n, v in arrays.items()}
    dram = {n: nc.dram_tensor("in_" + n, v.shape, mb.dt.from_np(v.dtype), kind="ExternalInput").ap()
            for n, v in arrays.items()}
    out = nc.dram_tensor("out", (SEQ, D), mb.dt.float32, kind="ExternalOutput").ap()
    build(nc, dram, out)
    r = run_bass_kernel_spmd(nc, [{"in_" + n: v for n, v in arrays.items()}], core_ids=[0])
    return r.results[0]["out"].reshape(1, SEQ, D)
```

```python
import concourse.bass as bass
from concourse import mybir
from contextlib import ExitStack

P = 128
D = 1024
KT = D // P
SEQ = 512
TILES = SEQ // P
EPS = 1e-6
N_MEM = 256
MEM_TILES = N_MEM // P
HEADS, NOPE, ROPE, VDIM = 8, 64, 32, 64
QK = NOPE + ROPE
HALF = ROPE // 2
Q_RANK, KV_RANK = 256, 128
LATENT = Q_RANK + KV_RANK + ROPE
CONV, TAPS = 512, 31
CT = CONV // P
HIST = TAPS - 1
MEM_HEADS, MEM_DIM = 4, 256
PEER_HEADS, KEYS, TOPK = 8, 128, 16
SETS = 2 * PEER_HEADS
SLOTS = PEER_HEADS * TOPK
RING = 8
GROUPS = SLOTS // RING
WRING = 7
LOWEST = -3.0e38

BY_PE = (0, 2, 4, 6)
BY_DVE = (1, 3, 5, 7)

W_TILE = ([("w_in", k, 0, LATENT) for k in range(KT)] + [("w_in", k, LATENT, 1024) for k in range(KT)]
          + [("w_mix_out", k, 0, 1024) for k in range(KT)] + [("w_mem_q", k, 0, 1024) for k in range(KT)]
          + [("w_mem_out", k, 0, 1024) for k in range(KT)]
          + [("w_peer_query", k, 1024 * n, 1024) for n in range(2) for k in range(KT)])
W_MEMORY = [("w_mem_kv", k, 1024 * n, 1024) for n in range(2) for k in range(KT)]
PER_TILE = len(W_TILE)
W_BEFORE_MEMORY = 2 * KT
assert PER_TILE % WRING == 0

T_LATENT, T_CONV, T_Q, T_K, T_P, T_ATTN = 0, 1, 2, 4, 6, 14
T_HMEM, T_QMEM, T_PMEM, T_OMEM, T_HFFN, T_QPEER, T_TILE = 16, 18, 20, 22, 24, 26, 30
T_MEMORY = 4

HALF_GROUPS = GROUPS // 2
QUARTER = GROUPS // 4
UA, UB, VA, VB = ("u rows", 0), ("u rows", 1), ("v rows", 0), ("v rows", 1)
PARTS = (range(0, RING // 2), range(RING // 2, RING))


def later(*steps):
    return [("next tile",) + s for s in steps]


def first_part(*step):
    return ("part", 0) + step


def second_part(*step):
    return ("part", 1) + step


def product(*step):
    return [first_part(*step), second_part(*step), step]


def choice(half, quarter):
    at = (half, quarter)
    return [("sub_topk",) + at, ("candidates",) + at, ("best",) + at, ("gates",) + at, ("indices",) + at + (0,),
            ("indices",) + at + (1,)]


HEADS_STEPS = [("head", n) for n in range(HEADS)]
CONV_STEPS = [("conv", n) for n in range(6)]
CONV_TAPS = (TAPS - 1) // len(CONV_STEPS)
TAP_BATCH = 4
BATCHES = CT * TAPS // TAP_BATCH


def batches(n):
    return range(n * BATCHES // len(CONV_STEPS), (n + 1) * BATCHES // len(CONV_STEPS))


def pairs(batch):
    return [divmod(i, TAPS) for i in range(batch * TAP_BATCH, (batch + 1) * TAP_BATCH)]


FIRST = ([("inputs",), ("latent_query",)] + product("project") + [("latents",), ("conv_input",), ("up",), ("rotate",)]
         + HEADS_STEPS[:4] + [("memory_input",)] + HEADS_STEPS[4:] + [("memory", 0), ("attended",), ("memory_keys",)]
         + CONV_STEPS + [("memory", 1), first_part("mix_out"),
            ("conv_norm",), second_part("mix_out"), ("mix_out",), ("mem_norm",)] + product("mem_query")
         + [("mem_scores",), ("mem_values",)] + product("mem_out") + [("peer_norm",)] + product("peer_query", 0)
         + [("sub_scores", 0)] + choice(0, 0) + [("publish", 0, 0), ("next_input",), first_part("peer_query", 1)])
LATE_FIRST = ([("sub_topk", 0, 1), UA, ("candidates", 0, 1), ("best", 0, 1), second_part("peer_query", 1), UB,
               ("gates", 0, 1), ("indices", 0, 1, 0), ("indices", 0, 1, 1), ("publish", 0, 1), ("peer_query", 1),
               ("sub_scores", 1),
               UA] + later(("inputs",), ("latent_query",), first_part("project")) + [UB, ("sub_topk", 1, 0),
               ("candidates", 1, 0),
               UA, ("best", 1, 0)] + later(second_part("project")) + [UB, ("gates", 1, 0)] + later(("latents",)) + [
               ("indices", 1, 0, 0),
               UA] + later(("conv_input",)) + [("indices", 1, 0, 1), ("publish", 1, 0), UB, ("sub_topk", 1, 1)]
              + later(("up",), ("conv", 0)) + [
               UA, ("candidates", 1, 1), ("best", 1, 1)] + later(("conv", 1)) + [UB, ("gates", 1, 1)] + [
               ("indices", 1, 1, 0), ("indices", 1, 1, 1), ("publish", 1, 1)] + later(("rotate",)) + [
               UA] + later(("head", 0), ("conv", 2)) + [UB] + later(("head", 1), ("conv", 3)) + [
               UA] + later(("head", 2)) + [UB] + later(("head", 3), ("conv", 4)) + [
               UA] + later(("head", 4)) + [UB] + later(("head", 5)) + [
               UA, ("gelu", 0), ("weigh", 0)] + later(("head", 6)) + [UB] + later(("head", 7), ("attended",)))
LATE = ([UA, second_part("peer_query", 1), ("peer_query", 1), ("weigh", 1), UB] + later(("inputs",)) + [VA,
         ("sub_scores", 1), VB,
         UA, ("sub_topk", 1, 0)] + later(("latent_query",)) + [UB, ("candidates", 1, 0), ("best", 1, 0)]
        + later(first_part("project")) + [VA, ("gates", 1, 0), ("indices", 1, 0, 0), VB,
         UA, ("indices", 1, 0, 1)] + later(second_part("project")) + [UB, ("sub_topk", 1, 1), VA]
        + later(("latents",)) + [("candidates", 1, 1), VB] + later(("conv_input",)) + [
         UA] + later(("up",)) + [("best", 1, 1), UB, ("gates", 1, 1)] + [VA] + later(("conv", 0), ("rotate",)) + [
         ("indices", 1, 1, 0), VB, ("indices", 1, 1, 1),
         UA] + later(("head", 0), ("conv", 1)) + [UB, VA] + later(("head", 1)) + [VB,
         UA] + later(("head", 2), ("conv", 2)) + [UB, VA] + later(("head", 3)) + [VB,
         UA] + later(("head", 4), ("conv", 3)) + [UB, ("publish", 1, 0), VA] + later(("head", 5)) + [VB,
         UA] + later(("head", 6)) + [UB, ("publish", 1, 1)] + later(("head", 7)) + [VA]
        + later(("attended",)) + [VB, ("gelu", 0)] + later(("conv", 4)) + [
         UA, ("weigh", 0), UB, ("finish", 0), ("finish", 1)])
EARLY = [VA, first_part("mix_out"), VB,
         UA, UB, ("conv", 5), ("conv_norm",), VA, second_part("mix_out"), VB,
         UA, ("mix_out",), UB, ("mem_norm",), VA, first_part("mem_query"), VB, second_part("mem_query"),
         UA, ("mem_query",), UB, VA, ("mem_scores",), VB, ("mem_values",),
         UA, first_part("mem_out"), second_part("mem_out"), UB, ("mem_out",), VA, ("peer_norm",), VB,
         UA, first_part("peer_query", 0), second_part("peer_query", 0), UB, ("peer_query", 0), ("sub_scores", 0),
         VA, VB,
         UA, ("sub_topk", 0, 0), UB, ("candidates", 0, 0), ("best", 0, 0), VA, ("gates", 0, 0),
         ("indices", 0, 0, 0), VB,
         ("indices", 0, 0, 1), ("publish", 0, 0),
         UA, ("sub_topk", 0, 1), UB, ("candidates", 0, 1), ("best", 0, 1), ("gates", 0, 1), VA,
         ("indices", 0, 1, 0), ("indices", 0, 1, 1), ("publish", 0, 1), ("next_input",),
         first_part("peer_query", 1), VB, ("gelu", 1)]
LATE_LAST = [s for s in LATE if s[0] != "next tile"]
assert EARLY.count(VA) == LATE.count(VA) == HALF_GROUPS and EARLY.count(UA) + LATE.count(UA) == GROUPS
assert LATE_FIRST.count(UA) == LATE_FIRST.count(UB) == LATE.count(UA)


def of_tile(t, per_tile, n):
    return t * per_tile + n


def build(nc, dram, out):
    f32, i32, u32 = mybir.dt.float32, mybir.dt.int32, mybir.dt.uint32
    ALU, ACT, AX = mybir.AluOpType, mybir.ActivationFunctionType, mybir.AxisListType
    MLA_SCALE, MEM_SCALE = QK ** -0.5, MEM_DIM ** -0.5

    ctx = ExitStack()
    with ctx:
        def sb(name, shape, dt=f32):
            return ctx.enter_context(nc.sbuf_tensor(name, shape, dt))

        def sem(name):
            return ctx.enter_context(nc.semaphore(name))

        ring = sb("ring", [P, RING, D])
        wring = sb("wring", [P, WRING, 1024])
        key_cache = sb("key_cache", [P, HEADS, SEQ])
        value_cache = sb("value_cache", [P, TILES, HEADS * VDIM])
        mem_kT = sb("mem_kT", [P, KT, N_MEM])
        mem_v = sb("mem_v", [P, MEM_TILES, D])
        sub_keysT = sb("sub_keysT", [P, SETS, KEYS])
        w_q_up = sb("w_q_up", [P, 2, HEADS * QK])
        w_kv_up = sb("w_kv_up", [P, HEADS * (NOPE + VDIM)])
        ffn_g = sb("ffn_g", [P, D])
        final_g = sb("final_g", [P, D])
        latent_g = sb("latent_g", [P, Q_RANK + KV_RANK])
        mix_gT = sb("mix_gT", [P, KT])
        mem_gT = sb("mem_gT", [P, KT])
        memkv_gT = sb("memkv_gT", [P, KT])
        conv_wT = sb("conv_wT", [P, CT, TAPS])
        conv_p = sb("conv_p", [P, 3, CT])
        ident = sb("ident", [P, P])
        mean_w = sb("mean_w", [P, P])
        rope = sb("rope", [P, 2, HALF])
        iota = sb("iota", [P, TOPK])
        eps = sb("eps", [P, 1])
        mask = sb("mask", [P, SEQ])
        h = sb("h", [P, D])
        hn = sb("hn", [P, D])
        row_a = sb("row_a", [P, D])
        row_b = sb("row_b", [P, D])
        ta = sb("ta", [P, KT, P])
        tb = sb("tb", [P, KT, P])
        arena = sb("arena", [P, 5728])
        lat_row = sb("lat_row", [P, Q_RANK + KV_RANK])
        lat_t = sb("lat_t", [P, 3, P])
        u_t = sb("u_t", [P, CT, HIST + P])
        conv_acc = sb("conv_acc", [P, CT, P])
        h_kept = sb("h_kept", [P, D])
        y_acc = sb("y_acc", [P, D])
        y_row = sb("y_row", [P, D])
        kfull = sb("kfull", [P, HEADS, QK])
        diag = sb("diag", [P, len(BY_PE), P])
        small = sb("small", [P, 64])
        a_group = sb("a_group", [P, RING])
        a_all = sb("a_all", [P, SLOTS])
        gelu_a = sb("gelu_a", [P, SLOTS])
        gate = sb("gate", [P, SLOTS])
        weight = sb("weight", [P, SLOTS])
        idx = sb("idx", [P, SLOTS], i32)
        idx_group = sb("idx_group", [P, 2, RING], i32)
        top_v = sb("top_v", [P, SETS // 2, TOPK])
        top_i = sb("top_i", [P, SETS // 2, TOPK], u32)
        best_v = sb("best_v", [P, PEER_HEADS // 2, TOPK])
        picked = sb("picked", [P, 2, SLOTS // 2])
        best_p = sb("best_p", [P, PEER_HEADS // 2, TOPK], u32)

        def region(first, size):
            return arena[:, first:first + size]

        probs = region(0, 1024).rearrange("p (b k) -> p b k", k=SEQ)
        q_t = region(1792, 1024).rearrange("p (h t) -> p h t", t=P)
        qk = region(3680, 864).rearrange("p (h d) -> p h d", d=QK)
        junk = region(4704, 1024)
        tap_diag = region(4704, 2 * TAP_BATCH * P).rearrange("p (n d) -> p n d", d=P)
        probs_t = region(3680, 1024).rearrange("p (b j t) -> p b j t", b=2, t=P)
        sig = region(4704, 512)
        u_row = region(5216, 512)
        N_HEAD = PEER_HEADS // 2
        qp_t = region(0, 1024).rearrange("p (s t) -> p s t", t=P)
        onehot = region(0, 1024).rearrange("p (h k a) -> p h k a", h=N_HEAD, k=TOPK)
        scores = region(1024, 1024).rearrange("p (s n) -> p s n", n=KEYS)
        cand = region(2048, 1024).rearrange("p (h a b) -> p h a b", h=N_HEAD, a=TOPK)
        cand_h = region(2048, 1024).rearrange("p (h c) -> p h c", h=N_HEAD)
        top_f = region(3072, 128).rearrange("p (s k) -> p s k", k=TOPK)
        pos_f = region(3200, 128).rearrange("p (c s) -> p c s", c=2)
        pos_u = region(3328, 128).bitcast(u32).rearrange("p (c s) -> p c s", c=2)
        memn_t = ring[:, 0:2, :].rearrange("p a (k m) -> p (a k) m", m=N_MEM)
        mem_k_row = ring[:, 2:4, :]
        mem_row = ring[:, 4:6, :]
        mem_junk = ring[:, 6:8, :]
        ss, root, rinv = small[:, 0:4], small[:, 4:8], small[:, 8:12]
        mx, nmx, lsum, linv = small[:, 16:24], small[:, 24:32], small[:, 32:40], small[:, 40:48]
        f_ss, f_root, f_rinv = small[:, 48:49], small[:, 49:50], small[:, 50:51]
        m_ss, m_root, m_rinv = small[:, 52:54], small[:, 54:56], small[:, 56:58]
        rmix = small[:, 58:59]
        kv2 = small[:, 60:62]
        conv_root = row_b[:, 0:P]
        conv_x = row_b[:, 512:1024].rearrange("p (c t) -> p c t", t=P)

        acc = ctx.enter_context(nc.psum_tensor("acc", [P, D], f32))
        g = ctx.enter_context(nc.psum_tensor("g", [P, 4, 512], f32))
        tp = ctx.enter_context(nc.psum_tensor("tp", [P, 2, 512], f32))
        g01 = g[:, 0:2, :].rearrange("p b n -> p (b n)")
        g23 = g[:, 2:4, :].rearrange("p b n -> p (b n)")
        g12 = g[:, 1:3, :].rearrange("p b n -> p (b n)")

        loaded = {n: sem("loaded_" + n) for n in ("input", "latents", "mixer", "memory", "experts")}
        input_landed = sem("input_landed")
        w_landed = [sem(f"weights_landed_{s}") for s in range(WRING)]
        w_used = sem("weights_used")
        landed = [sem(f"rows_landed_{r}") for r in range(RING)]
        granted = sem("pool_granted")
        dve_granted = sem("dve_granted")
        act_granted = sem("act_granted")
        idx_staged = sem("indices_staged")
        idx_ready = sem("indices_ready")
        u_used = sem("u_rows_used")
        v_used_pe = sem("v_rows_used_by_pe")
        v_used_dve = sem("v_rows_used_by_dve")
        a_copied = sem("a_copied")
        gelu_ready = sem("gelu_ready")
        weight_ready = sem("weight_ready")
        diag_ready = sem("diag_ready")
        y_ready = sem("y_ready")
        y_root_ready = sem("y_root_ready")
        y_normed = sem("y_normed")
        stored = sem("y_row_free")
        h_taken = sem("h_taken")
        filled = sem("transposed_bank_filled")
        drained = sem("transposed_bank_drained")
        dve_step = sem("dve_step")
        act_step = sem("act_step")
        zeroed = sem("caches_zeroed")
        hn_taken = sem("expert_input_taken")
        memT_scaled = sem("memory_scaled")
        mem_root = sem("memory_root")
        mem_rinv_ready = sem("memory_rinv_ready")
        mem_saved = sem("memory_saved")
        x_scaled = sem("x_scaled")
        root_ready = sem("root_ready")
        latent_scale = sem("latent_scale")
        rmix_ready = sem("input_rinv_ready")
        k_rope_copied = sem("k_rope_copied")
        lat_normed = sem("latents_normed")
        sig_ready = sem("sigmoid_ready")
        u_ready = sem("conv_row_ready")
        up_ready = sem("up_ready")
        up_saved = sem("up_saved")
        rope_products = sem("rope_products")
        roped = sem("roped")
        s_ready = sem("attention_scores_ready")
        s_masked = sem("attention_scores_masked")
        p_ready = sem("attention_probs_ready")
        pv_done = sem("attention_values_done")
        attn_ready = sem("attention_row_ready")
        hist_read = sem("conv_history_saved")
        taps_ready = sem("tap_diagonals_ready")
        taps_used = sem("tap_diagonals_used")
        tap_done = sem("tap_done")
        stat_ready = sem("conv_stat_ready")
        centred = sem("conv_centred")
        squared = sem("conv_squared")
        conv_rooted = sem("conv_rooted")
        conv_normed = sem("conv_normed")
        cat_ready = sem("conv_output_ready")
        h_mixed = sem("h_mixed")
        h_row = sem("memory_input_row_ready")
        mq_saved = sem("memory_query_saved")
        ms_ready = sem("memory_scores_ready")
        ms_max = sem("memory_scores_max")
        mp_ready = sem("memory_probs_ready")
        mo_ready = sem("memory_values_ready")
        mo_row = sem("memory_row_ready")
        h_remembered = sem("h_remembered")
        hn_ready = sem("expert_input_ready")
        pq_saved = sem("peer_query_saved")
        sub_ready = sem("sub_scores_ready")
        sub_saved = sem("sub_scores_saved")
        best_shifted = sem("best_shifted")
        best_exp = sem("best_exp")
        picked_ready = sem("picked_ready")

        block = ctx.enter_context(nc.Block())

        def hold(eng, tick, s, value):
            eng.wait_ge(s, value)
            if not isinstance(value, int):
                eng.sem_inc(tick, 1)

        def first_of(t):
            return isinstance(t, int) and t == 0

        def chunk_number(t, n):
            if first_of(t) and n < W_BEFORE_MEMORY:
                return n
            return len(W_MEMORY) + PER_TILE * t + n

        def used_after(t, n):
            return chunk_number(t, n - 1) + 1

        def place(t, n):
            return (n if first_of(t) and n < W_BEFORE_MEMORY else len(W_MEMORY) + n) % WRING

        def landed_value(t, n):
            if first_of(t):
                return 16 * (chunk_number(t, n) // WRING + 1)
            return 16 * (PER_TILE // WRING) * t + 16 * ((len(W_MEMORY) + n) // WRING + 1)

        def bank_number(t, n):
            return n if first_of(t) and n < T_HMEM else of_tile(t, T_TILE, T_MEMORY + n)

        def u_sequence(t, g):
            return of_tile(t, 2 * GROUPS, 1 - HALF_GROUPS) + g * 2

        def u_sequence_start(g):
            return 1 + g

        def v_sequence(t, g, last_tile=False):
            if last_tile:
                return of_tile(t, 2 * GROUPS, HALF_GROUPS + 1 + HALF_GROUPS) + g
            return of_tile(t, 2 * GROUPS, HALF_GROUPS + 2) + g * 2

        def slots_of(half, quarter):
            n = SLOTS // 4
            return slice((2 * half + quarter) * n, (2 * half + quarter + 1) * n)

        def v_count(t, g, by, n):
            return of_tile(t, GROUPS * len(by), len(by) + n) + g * len(by)

        @block.sync
        def _(sp):
            def constants(name, pairs):
                for dst, src in pairs:
                    sp.dma_start(dst, src).then_inc(loaded[name], 16)

            def weight_dma(spec, slot):
                name, k, col, cols = spec
                sp.dma_start(wring[:, slot, 0:cols], dram[name][k * P:(k + 1) * P, col:col + cols]) \
                  .then_inc(w_landed[slot], 16)

            def inputs(t):
                sp.dma_start(h[:, :], dram["x"][bass.ds(t * P, P), :]).then_inc(input_landed, 16)
                sp.dma_start(tb[:, :, :], dram["xT"][bass.ds(t * P, P), :, :]).then_inc(input_landed, 16)
                sp.dma_start(mask[:, :], dram["mask"][bass.ds(t * P, P), :]).then_inc(input_landed, 16)
                sp.dma_start(rope[:, :, :], dram["rope"][bass.ds(t * P, P), :, :]).then_inc(input_landed, 16)

            def tile_weights(t, first, end):
                for n in range(first, end):
                    if not first_of(t) or n >= WRING:
                        sp.wait_ge(w_used, chunk_number(t, n) - WRING + 1)
                    weight_dma(W_TILE[n], place(t, n))

            constants("input", [(mix_gT[:, :], dram["mix_gT"])])
            inputs(0)
            tile_weights(0, 0, WRING)
            constants("latents", [
                (ident[:, :], dram["ident"]),
                (latent_g[:, 0:Q_RANK], dram["q_latent_g"].to_broadcast([P, Q_RANK])),
                (latent_g[:, Q_RANK:], dram["kv_latent_g"].to_broadcast([P, KV_RANK]))])
            tile_weights(0, WRING, W_BEFORE_MEMORY)
            constants("mixer", [
                (w_q_up[:, :, :], dram["w_q_up"].rearrange("(k p) n -> p k n", p=P)),
                (w_kv_up[:, :], dram["w_kv_up"]),
                (conv_wT[:, :, :], dram["conv_wT"]), (conv_p[:, :, :], dram["conv_p"])])
            constants("memory", [
                (memkv_gT[:, :], dram["memkv_gT"]), (mem_gT[:, :], dram["mem_gT"]), (memn_t, dram["memT"]),
                (mem_row, dram["mem"].rearrange("(m p) d -> p m d", p=P))])
            for m, spec in enumerate(W_MEMORY):
                sp.wait_ge(w_used, W_BEFORE_MEMORY + m - WRING + 1)
                weight_dma(spec, (W_BEFORE_MEMORY + m) % WRING)
            constants("experts", [
                (iota[:, :], dram["iota"].to_broadcast([P, TOPK])),
                (ffn_g[:, :], dram["norm_ffn_g"].to_broadcast([P, D])),
                (final_g[:, :], dram["final_norm_g"].to_broadcast([P, D])),
                (sub_keysT[:, :, :], dram["sub_keysT"])])
            second_choice = PER_TILE - KT
            tile_weights(0, W_BEFORE_MEMORY, second_choice)
            with sp.Fori(0, TILES - 1) as t:
                sp.wait_ge(h_taken, of_tile(t, 1, 1))
                inputs(t + 1)
                tile_weights(t, second_choice, PER_TILE)
                tile_weights(t + 1, 0, second_choice)
            tile_weights(TILES - 1, second_choice, PER_TILE)
            sp.wait_ge(stored, 16 * (TILES + 1))

        @block.gpsimd
        def _(pool):
            pool.memset(key_cache[:, :, :], 0.0).then_inc(zeroed, 1)
            pool.memset(value_cache[:, :, :], 0.0).then_inc(zeroed, 1)
            pool.memset(u_t[:, :, :], 0.0).then_inc(zeroed, 1)
            pool.memset(mean_w[:, :], 1.0 / CONV).then_inc(zeroed, 1)
            pool.memset(eps[:, :], EPS).then_inc(zeroed, 1)

            def stage(group, turn, sequence):
                pool.tensor_copy(idx_group[:, turn, :], idx[:, bass.ds(group * RING, RING)]).then_inc(idx_staged, 1)
                hold(pool, granted, idx_staged, sequence)

            def fetch(table, r, turn):
                pool.indirect_dma_start(ring[:, r, :], None, dram[table],
                                        bass.IndirectOffsetOnAxis(ap=idx_group[:, turn, r:r + 1], axis=0)) \
                    .then_inc(landed[r], 16)

            def v_place_free(t, group, r):
                by, used = (BY_PE, v_used_pe) if r in BY_PE else (BY_DVE, v_used_dve)
                hold(pool, granted, used, v_count(t, group, by, by.index(r) + 1))

            def u_place_free(t, group, r):
                hold(pool, granted, u_used, of_tile(t, SLOTS, r + 1) + group * RING)

            def u_group(t, group, turn, v_before):
                stage(group, turn, u_sequence(t, group))
                for r in range(RING):
                    v_place_free(*v_before, r)
                    fetch("peer_u", r, turn)

            def v_group(t, group, turn, u_before):
                stage(group, turn, v_sequence(t, group))
                for r in range(RING):
                    u_place_free(*u_before, r)
                    fetch("peer_v", r, turn)

            def quarters(first, end, ready, group):
                for quarter in range(2):
                    low, high = max(first, quarter * QUARTER), min(end, (quarter + 1) * QUARTER)
                    if low < high:
                        hold(pool, granted, idx_ready, ready + quarter)
                        with pool.Fori(low, high) as s:
                            group(s)

            def first_half(t):
                def group(s):
                    u_group(t, s + HALF_GROUPS, 0, (t, s - 1))
                    v_group(t, s, 1, (t, s + HALF_GROUPS))

                hold(pool, granted, idx_ready, of_tile(t, 4, 3))
                u_place_free(t, HALF_GROUPS - 1, RING - 1)
                u_group(t, HALF_GROUPS, 0, (t, -1))
                v_group(t, 0, 1, (t, HALF_GROUPS))
                quarters(1, HALF_GROUPS, of_tile(t, 4, 3), group)

            for s in range(HALF_GROUPS):
                if s % QUARTER == 0:
                    pool.wait_ge(idx_ready, s // QUARTER + 1)
                stage(s, s % 2, u_sequence_start(s))
                for r in range(RING):
                    if s:
                        u_place_free(0, s - 1, r)
                    fetch("peer_u", r, s % 2)
            with pool.Fori(0, TILES - 1) as t:
                def group(s):
                    u_group(t + 1, s, 0, (t, s + HALF_GROUPS - 1))
                    v_group(t, s + HALF_GROUPS, 1, (t + 1, s))

                first_half(t)
                quarters(0, HALF_GROUPS, of_tile(t, 4, 5), group)
            first_half(TILES - 1)
            with pool.Fori(0, HALF_GROUPS // 2) as j:
                for turn in range(2):
                    g8 = j * 2 + HALF_GROUPS + turn
                    stage(g8, turn, v_sequence(TILES - 1, g8, last_tile=True))
                    for r in range(RING):
                        v_place_free(TILES - 1, g8 - 1, r)
                        fetch("peer_v", r, turn)

        @block.scalar
        def _(act):
            ACT_STEPS = 4
            done = [0, 0]
            at = [0]

            def own(t, n):
                return n + (n > 2) if first_of(t) else of_tile(t, ACT_STEPS, n + 1)

            def settle(t, ins):
                assert not at[0] or done[0] == ACT_STEPS
                done[at[0]] += 1
                ins.then_inc(act_step, 1)
                act.wait_ge(act_step, own(t, done[at[0]]))

            def next_tile():
                assert done[0] == ACT_STEPS, done
                done[0], done[1] = done[1], 0

            def drain(t, n, dst, rows=P, blocks=4):
                act.wait_ge(filled, bank_number(t, n) + 1)
                act.activation(dst, tp[0:rows, n % 2, 0:blocks * P].rearrange("p (b t) -> p b t", t=P), ACT.Copy) \
                   .then_inc(drained, 1)

            act.wait_ge(zeroed, 5)

            def memory(t, half):
                if half == 0:
                    act.wait_ge(loaded["memory"], 64)
                    for m in range(MEM_TILES):
                        last = act.activation(mem_junk[:, m, :], mem_row[:, m, :], ACT.Square,
                                              accum_out=m_ss[:, m:m + 1])
                    last.then_inc(act_step, 1)
                    act.wait_ge(act_step, 3)
                    act.activation(m_root[:, :], m_ss[:, :], ACT.Sqrt, scale=1.0 / D, bias=eps[:, 0:1]) \
                       .then_inc(mem_root, 1)
                    act.wait_ge(mem_rinv_ready, 1)
                act.wait_ge(w_used, W_BEFORE_MEMORY + (half + 1) * KT)
                rows = mem_k_row if half == 0 else mem_v
                for m in range(MEM_TILES):
                    act.activation(rows[:, m, :], ((g01, g23)[half], acc[:, :])[m], ACT.Copy,
                                   scale=m_rinv[:, m:m + 1]).then_inc(mem_saved, 1)

            def memory_keys(t):
                for n in range(4):
                    act.wait_ge(filled, T_HMEM + n + 1)
                    act.activation(mem_kT[:, 4 * (n % 2):4 * (n % 2) + 4, (n // 2) * P:(n // 2 + 1) * P],
                                   tp[:, n % 2, :].rearrange("p (b t) -> p b t", t=P), ACT.Copy).then_inc(drained, 1)

            def inputs(t):
                act.wait_ge(input_landed, of_tile(t, 64, 64))
                settle(t, act.activation(junk, h[:, :], ACT.Square, accum_out=ss[:, 0:1]))
                act.activation(root[:, 0:1], ss[:, 0:1], ACT.Sqrt, scale=1.0 / D, bias=eps[:, 0:1]) \
                   .then_inc(root_ready, 1)

            def latents(t):
                act.wait_ge(rmix_ready, of_tile(t, 1, 1))
                act.wait_ge(w_used, used_after(t, KT))
                act.activation(qk[:, HEADS, NOPE:QK], g[:, 0, Q_RANK + KV_RANK:LATENT], ACT.Copy, scale=rmix) \
                   .then_inc(k_rope_copied, 1)
                act.activation(lat_row[:, 0:Q_RANK], g[:, 0, 0:Q_RANK], ACT.Square, scale=rmix, accum_out=ss[:, 1:2])
                settle(t, act.activation(lat_row[:, Q_RANK:], g[:, 0, Q_RANK:Q_RANK + KV_RANK], ACT.Square,
                                         scale=rmix, accum_out=ss[:, 2:3]))
                act.activation(root[:, 1:2], ss[:, 1:2], ACT.Sqrt, scale=1.0 / Q_RANK, bias=eps[:, 0:1])
                act.activation(root[:, 2:3], ss[:, 2:3], ACT.Sqrt, scale=1.0 / KV_RANK, bias=eps[:, 0:1]) \
                   .then_inc(root_ready, 1)

            def conv_input(t):
                act.wait_ge(w_used, used_after(t, 2 * KT))
                act.activation(sig, g[:, 2, :], ACT.Sigmoid, scale=rmix).then_inc(sig_ready, 1)
                drain(t, T_LATENT, lat_t[:, :, :], blocks=3)
                drain(t, T_CONV, u_t[:, :, HIST:])

            def up(t):
                act.wait_ge(up_ready, of_tile(t, 2, 1))
                act.activation(qk[:, 0:5, :], g[:, 3, 0:5 * QK].rearrange("p (h d) -> p h d", d=QK), ACT.Copy)
                act.activation(qk[:, 5:8, :], g[:, 0, 0:3 * QK].rearrange("p (h d) -> p h d", d=QK), ACT.Copy) \
                   .then_inc(up_saved, 1)
                act.wait_ge(up_ready, of_tile(t, 2, 2))
                kv = g12.rearrange("p (h d) -> p h d", d=NOPE + VDIM)
                act.activation(kfull[:, :, 0:NOPE], kv[:, :, 0:NOPE], ACT.Copy).then_inc(up_saved, 1)
                act.activation(value_cache[:, bass.ds(t, 1), :].rearrange("p a (h d) -> p (a h) d", d=VDIM),
                               kv[:, :, NOPE:], ACT.Copy).then_inc(up_saved, 1)

            def rotate(t):
                if not first_of(t):
                    act.wait_ge(best_shifted, of_tile(t, 4, 0))
                for n in range(2):
                    drain(t, T_Q + n, q_t[0:QK, 4 * n:4 * n + 4, :], rows=QK)
                for n in range(2):
                    hold(act, act_granted, filled, bank_number(t, T_K + n) + 1)
                    act.activation(key_cache[0:QK, 4 * n:4 * n + 4, bass.ds(t * P, P)],
                                   tp[0:QK, n, :].rearrange("p (b t) -> p b t", t=P), ACT.Copy).then_inc(drained, 1)

            def head(t, n):
                act.wait_ge(s_masked, of_tile(t, 2 * HEADS, 2 * n + 2))
                act.activation(probs[:, n % 2, :], probs[:, n % 2, :], ACT.Exp, scale=MLA_SCALE,
                               bias=nmx[:, n:n + 1], accum_out=lsum[:, n:n + 1]).then_inc(p_ready, 1)
                if n >= 2:
                    act.wait_ge(pv_done, of_tile(t, HEADS, n - 1))
                drain(t, T_P + n, probs_t[:, n % 2, :, :])

            def conv(t, n):
                if first_of(t):
                    return
                for b in batches(n):
                    if b >= 2:
                        act.wait_ge(taps_used, of_tile(t - 1, BATCHES, b - 1))
                    for j, (c, k) in enumerate(pairs(b)):
                        last = act.activation(tap_diag[:, b % 2 * TAP_BATCH + j, :], ident[:, :], ACT.Copy,
                                              scale=conv_wT[:, c, k:k + 1])
                    last.then_inc(taps_ready, 1)

            def attended(t):
                drain(t, T_ATTN, ta[:, 0:2, :], blocks=2)
                drain(t, T_ATTN + 1, ta[:, 2:4, :], blocks=2)

            def conv_norm(t):
                act.wait_ge(centred, of_tile(t, 1, 1))
                act.activation(conv_acc[:, :, :], conv_x, ACT.Square).then_inc(squared, 1)
                act.wait_ge(stat_ready, of_tile(t, 2, 2))
                act.activation(conv_root, g[:, 3, P:2 * P], ACT.Sqrt, bias=eps[:, 0:1]).then_inc(conv_rooted, 1)
                act.wait_ge(conv_normed, of_tile(t, 1, 1))
                for c in range(CT):
                    last = act.activation(ta[:, 4 + c, :], conv_x[:, c, :], ACT.Silu, scale=conv_p[:, 1, c:c + 1],
                                          bias=conv_p[:, 2, c:c + 1])
                last.then_inc(cat_ready, 1)

            def norm_root(t, column):
                settle(t, act.activation(row_a[:, :], h[:, :], ACT.Square, accum_out=ss[:, column:column + 1]))
                act.activation(root[:, column:column + 1], ss[:, column:column + 1], ACT.Sqrt, scale=1.0 / D,
                               bias=eps[:, 0:1]).then_inc(root_ready, 1)

            def mem_norm(t):
                act.wait_ge(h_mixed, of_tile(t, 1, 1))
                norm_root(t, 3)
                for n in range(2):
                    act.wait_ge(filled, bank_number(t, T_HMEM + n) + 1)
                    for b in range(4):
                        last = act.activation(ta[:, 4 * n + b, :], tp[:, n, b * P:(b + 1) * P], ACT.Copy,
                                              scale=mem_gT[:, 4 * n + b:4 * n + b + 1])
                    last.then_inc(drained, 1)

            def mem_query(t):
                act.wait_ge(w_used, used_after(t, 4 * KT))
                act.activation(row_b[:, :], g23, ACT.Copy).then_inc(mq_saved, 1)
                for n in range(2):
                    drain(t, T_QMEM + n, tb[:, 4 * n:4 * n + 4, :])

            def mem_scores(t):
                act.wait_ge(ms_max, of_tile(t, 2, 2))
                for n in range(MEM_HEADS):
                    last = act.activation(row_b[:, n * N_MEM:(n + 1) * N_MEM], g01[:, n * N_MEM:(n + 1) * N_MEM],
                                          ACT.Exp, scale=MEM_SCALE, bias=nmx[:, n:n + 1],
                                          accum_out=lsum[:, n:n + 1])
                last.then_inc(mp_ready, 1)

            def mem_values(t):
                for n in range(2):
                    drain(t, T_PMEM + n, tb[:, 4 * n:4 * n + 4, :])
                for n in range(2):
                    drain(t, T_OMEM + n, ta[:, 4 * n:4 * n + 4, :])

            def peer_norm(t):
                act.wait_ge(h_remembered, of_tile(t, 1, 1))
                norm_root(t, 3)
                for n in range(2):
                    drain(t, T_HFFN + n, ta[:, 4 * n:4 * n + 4, :])

            def peer_query(t, half):
                act.wait_ge(w_used, used_after(t, (6 + half) * KT))
                act.activation(row_b[:, :], g23, ACT.Copy).then_inc(pq_saved, 1)
                if half:
                    act.wait_ge(picked_ready, of_tile(t, 8, 4))
                for n in range(2):
                    drain(t, T_QPEER + 2 * half + n, qp_t[:, 4 * n:4 * n + 4, :])

            def sub_scores(t, half):
                for n in range(2):
                    act.wait_ge(sub_ready, of_tile(t, 4, 2 * half + n + 1))
                    act.activation(scores[:, 4 * n:4 * n + 4, :], g[:, n, :].rearrange("p (s n) -> p s n", n=KEYS),
                                   ACT.Copy).then_inc(sub_saved, 1)

            def gates(t, half, quarter):
                act.wait_ge(best_shifted, of_tile(t, 4, 2 * half + quarter + 1))
                part = gate[:, slots_of(half, quarter)]
                act.activation(part, part, ACT.Exp).then_inc(best_exp, 1)

            def gelu(t, half):
                if half and first_of(t):
                    return
                t = t - half
                act.wait_ge(a_copied, of_tile(t, GROUPS, (half + 1) * HALF_GROUPS))
                part = slice(half * SLOTS // 2, (half + 1) * SLOTS // 2)
                act.activation(gelu_a[:, part], a_all[:, part], ACT.Gelu).then_inc(gelu_ready, 1)

            def weigh(t, half):
                if half and first_of(t):
                    return
                t = t - half
                act.wait_ge(weight_ready, of_tile(t, 2, half + 1))
                diagonals(t, half * HALF_GROUPS, 0)

            def diagonals(t, group, part):
                for j, r in enumerate(BY_PE):
                    if r not in PARTS[part]:
                        continue
                    hold(act, act_granted, v_used_pe, v_count(t, group - 1, BY_PE, j + 1))
                    act.activation(diag[:, j, :], ident[:, :], ACT.Copy,
                                   scale=weight[:, bass.ds(group * RING + r, 1)]).then_inc(diag_ready, 1)

            def v_group(t, group, part, last_of_half):
                if part == 0:
                    diagonals(t, group, 1)
                elif not last_of_half:
                    diagonals(t, group + 1, 0)

            def finish(t, part=None):
                if first_of(t) or part == 0:
                    return
                t = t - 1
                act.wait_ge(y_ready, t + 2)
                act.activation(row_a[:, :], y_row[:, :], ACT.Square, accum_out=f_ss).then_inc(y_root_ready, 1)
                act.wait_ge(y_root_ready, of_tile(t, 2, 1))
                act.activation(f_root, f_ss, ACT.Sqrt, scale=1.0 / D, bias=eps[:, 0:1]).then_inc(y_root_ready, 1)
                hold(act, act_granted, y_normed, of_tile(t, 2, 2))
                act.dma_start(out[bass.ds(t * P, P), :], y_row[:, :]).then_inc(stored, 16)

            stages = dict(inputs=inputs, latents=latents, conv_input=conv_input, up=up, rotate=rotate, head=head,
                          memory=memory, memory_keys=memory_keys, conv=conv, attended=attended,
                          conv_norm=conv_norm, mem_norm=mem_norm,
                          mem_query=mem_query, mem_scores=mem_scores, mem_values=mem_values, peer_norm=peer_norm,
                          peer_query=peer_query, sub_scores=sub_scores, gates=gates, gelu=gelu, weigh=weigh,
                          finish=finish)

            def run(t, steps, u=None, v=None):
                groups = {"u rows": u, "v rows": v}
                passed = dict.fromkeys(groups, 0)
                for name, *args in steps:
                    at[0] = name == "next tile"
                    if name in groups:
                        if groups[name]:
                            groups[name](passed[name], args[0])
                        passed[name] += args[0]
                    elif at[0] and args[0] in stages:
                        stages[args[0]](t + 1, *args[1:])
                    elif name in stages:
                        stages[name](t, *args)

            def tile(t, late):
                run(t + 1, EARLY, v=lambda k, part: v_group(t, k, part, k == HALF_GROUPS - 1))
                run(t + 1, late, v=lambda k, part: v_group(t, HALF_GROUPS + k, part, k == HALF_GROUPS - 1))
                next_tile()

            run(0, FIRST)
            run(0, LATE_FIRST)
            next_tile()
            with act.Fori(0, TILES - 2) as t:
                tile(t, LATE)
            tile(TILES - 2, LATE_LAST)
            for half in range(2):
                if half:
                    gelu(TILES, 1)
                    weigh(TILES, 1)
                with act.Fori(half * HALF_GROUPS, (half + 1) * HALF_GROUPS - 1) as group:
                    for part in range(2):
                        v_group(TILES - 1, group, part, False)
                v_group(TILES - 1, (half + 1) * HALF_GROUPS - 1, 0, True)
            finish(TILES)

        @block.vector
        def _(dve):
            DVE_STEPS = 153
            BASE = 1
            done = [0, 0]
            at = [0]

            def step_of(t, n):
                return of_tile(t, DVE_STEPS, BASE + n)

            def note(ins):
                assert not at[0] or done[0] == DVE_STEPS, done
                done[at[0]] += 1
                ins.then_inc(dve_step, 1)

            def next_tile():
                assert done[0] == DVE_STEPS, done
                done[0], done[1] = done[1], 0

            def settle(t):
                dve.wait_ge(dve_step, step_of(t, done[at[0]]))

            def settle_held(t):
                hold(dve, dve_granted, dve_step, step_of(t, done[at[0]]))

            dve.wait_ge(zeroed, 5)
            dve.memset(a_group[:, :], 0.0).then_inc(dve_step, 1)
            dve.sem_inc(y_ready, 1)
            dve.sem_inc(stored, 16)
            dve.sem_inc(v_used_pe, len(BY_PE))
            dve.sem_inc(v_used_dve, len(BY_DVE))
            dve.wait_ge(dve_step, 1)
            dve.wait_ge(loaded["input"], 16)

            def memory_input(t):
                dve.wait_ge(loaded["memory"], 64)
                dve.tensor_tensor(memn_t, memn_t, memkv_gT[:, :].unsqueeze(2).to_broadcast([P, KT, N_MEM]),
                                  ALU.mult).then_inc(memT_scaled, 1)

            def memory(t, half):
                if half == 0:
                    dve.wait_ge(mem_root, 1)
                    dve.reciprocal(m_rinv[:, :], m_root[:, :]).then_inc(mem_rinv_ready, 1)

            def inputs(t):
                dve.wait_ge(input_landed, of_tile(t, 64, 64))
                dve.tensor_tensor(tb[:, :, :], tb[:, :, :], mix_gT[:, :].unsqueeze(2).to_broadcast([P, KT, P]),
                                  ALU.mult).then_inc(x_scaled, 1)
                dve.wait_ge(root_ready, of_tile(t, 4, 1))
                dve.reciprocal(rmix, root[:, 0:1]).then_inc(rmix_ready, 1)

            def latents(t):
                if first_of(t):
                    dve.wait_ge(loaded["latents"], 16 * 3)
                dve.wait_ge(rmix_ready, of_tile(t, 1, 1))
                dve.wait_ge(root_ready, of_tile(t, 4, 2))
                dve.reciprocal(rinv[:, 1:3], root[:, 1:3]).then_inc(latent_scale, 1)
                dve.wait_ge(latent_scale, of_tile(t, 2, 1))
                dve.tensor_scalar(kv2, rinv[:, 1:3], rmix, None, ALU.mult).then_inc(latent_scale, 1)
                dve.wait_ge(latent_scale, of_tile(t, 2, 2))
                dve.scalar_tensor_tensor(lat_row[:, 0:Q_RANK], g[:, 0, 0:Q_RANK], kv2[:, 0:1], latent_g[:, 0:Q_RANK],
                                         ALU.mult, ALU.mult)
                dve.scalar_tensor_tensor(lat_row[:, Q_RANK:], g[:, 0, Q_RANK:Q_RANK + KV_RANK], kv2[:, 1:2],
                                         latent_g[:, Q_RANK:], ALU.mult, ALU.mult).then_inc(lat_normed, 1)

            def conv_input(t):
                dve.wait_ge(sig_ready, of_tile(t, 1, 1))
                dve.scalar_tensor_tensor(u_row, g[:, 1, :], rmix, sig, ALU.mult, ALU.mult).then_inc(u_ready, 1)

            def rotate(t):
                dve.wait_ge(up_saved, of_tile(t, 3, 1))
                dve.wait_ge(k_rope_copied, of_tile(t, 1, 1))
                n9 = [P, HEADS + 1, HALF]
                cos, sin = (rope[:, c:c + 1, :].to_broadcast(n9) for c in range(2))
                x1, x2 = qk[:, :, NOPE:NOPE + HALF], qk[:, :, NOPE + HALF:QK]
                w = (HEADS + 1) * HALF
                t1, t2, t3, t4 = (row_b[:, c * w:(c + 1) * w].rearrange("p (h d) -> p h d", d=HALF) for c in range(4))
                dve.tensor_tensor(t1, x1, cos, ALU.mult)
                dve.tensor_tensor(t2, x2, sin, ALU.mult)
                dve.tensor_tensor(t3, x1, sin, ALU.mult)
                dve.tensor_tensor(t4, x2, cos, ALU.mult).then_inc(rope_products, 1)
                dve.wait_ge(rope_products, of_tile(t, 1, 1))
                dve.tensor_tensor(x1, t1, t2, ALU.subtract)
                dve.tensor_tensor(x2, t3, t4, ALU.add).then_inc(roped, 1)
                dve.wait_ge(roped, of_tile(t, 2, 1))
                dve.tensor_copy(kfull[:, :, NOPE:QK], qk[:, HEADS:HEADS + 1, NOPE:QK].to_broadcast([P, HEADS, ROPE])) \
                   .then_inc(roped, 1)

            def head(t, n):
                dve.wait_ge(s_ready, of_tile(t, HEADS, n + 1))
                if n >= 2:
                    dve.wait_ge(filled, bank_number(t, T_P + n - 2) + 1)
                elif n == 0 and not first_of(t):
                    dve.wait_ge(picked_ready, of_tile(t, 8, 0))
                dve.tensor_tensor(probs[:, n % 2, :], g[:, n % 2, :], mask[:, :], ALU.add).then_inc(s_masked, 1)
                dve.wait_ge(s_masked, of_tile(t, 2 * HEADS, 2 * n + 1))
                note(dve.tensor_reduce(mx[:, n:n + 1], probs[:, n % 2, :], AX.X, ALU.max))
                settle(t)
                dve.tensor_scalar(nmx[:, n:n + 1], mx[:, n:n + 1], -MLA_SCALE, None, ALU.mult).then_inc(s_masked, 1)

            def conv(t, n):
                if first_of(t):
                    if n == 0:
                        dve.wait_ge(loaded["mixer"], 16 * 4)
                        dve.wait_ge(drained, bank_number(t, T_CONV) + 1)
                        for c in range(CT):
                            ins = dve.tensor_scalar(conv_acc[:, c, :], u_t[:, c, 0:P], conv_wT[:, c, 0:1],
                                                    conv_p[:, 0, c:c + 1], ALU.mult, ALU.add)
                        ins.then_inc(tap_done, 1)
                    for k in range(1 + CONV_TAPS * n, 1 + CONV_TAPS * (n + 1)):
                        dve.wait_ge(tap_done, k)
                        for c in range(CT):
                            ins = dve.scalar_tensor_tensor(conv_acc[:, c, :], u_t[:, c, k:k + P],
                                                           conv_wT[:, c, k:k + 1], conv_acc[:, c, :],
                                                           ALU.mult, ALU.add)
                        ins.then_inc(tap_done, 1)
                elif n == len(CONV_STEPS) - 1:
                    dve.wait_ge(taps_used, of_tile(t - 1, BATCHES, BATCHES))
                    dve.tensor_tensor(conv_acc[:, :, :], g[:, 3, :].rearrange("p (c t) -> p c t", t=P),
                                      conv_p[:, 0, :].unsqueeze(2).to_broadcast([P, CT, P]), ALU.add)
                if n == len(CONV_STEPS) - 1:
                    dve.tensor_copy(u_t[:, :, 0:HIST], u_t[:, :, P:P + HIST]).then_inc(hist_read, 1)

            def attended(t):
                dve.wait_ge(p_ready, of_tile(t, HEADS, HEADS))
                note(dve.reciprocal(linv, lsum))
                settle(t)
                dve.wait_ge(pv_done, of_tile(t, HEADS, HEADS))
                dve.tensor_tensor(row_b[:, 0:512].rearrange("p (h d) -> p h d", d=VDIM),
                                  g[:, 2, :].rearrange("p (h d) -> p h d", d=VDIM),
                                  linv.unsqueeze(2).to_broadcast([P, HEADS, VDIM]), ALU.mult).then_inc(attn_ready, 1)

            def conv_norm(t):
                all4 = [P, CT, P]
                dve.wait_ge(stat_ready, of_tile(t, 2, 1))
                dve.tensor_tensor(conv_x, conv_acc[:, :, :], g[:, 3:4, 0:P].to_broadcast(all4), ALU.subtract) \
                   .then_inc(centred, 1)
                dve.wait_ge(conv_rooted, of_tile(t, 1, 1))
                note(dve.reciprocal(conv_root, conv_root))
                settle(t)
                dve.tensor_tensor(conv_x, conv_x, row_b[:, 0:P].unsqueeze(1).to_broadcast(all4), ALU.mult) \
                   .then_inc(conv_normed, 1)

            def mix_out(t):
                dve.wait_ge(w_used, used_after(t, 3 * KT))
                dve.tensor_tensor(h[:, :], h[:, :], g01, ALU.add).then_inc(h_mixed, 1)

            def mem_norm(t):
                dve.wait_ge(root_ready, of_tile(t, 4, 3))
                note(dve.reciprocal(rinv[:, 3:4], root[:, 3:4]))
                settle(t)
                dve.tensor_scalar(row_a[:, :], h[:, :], rinv[:, 3:4], None, ALU.mult).then_inc(h_row, 1)

            def mem_scores(t):
                dve.wait_ge(ms_ready, of_tile(t, 1, 1))
                dve.tensor_reduce(mx[:, 0:4], g01.rearrange("p (h m) -> p h m", m=N_MEM), AX.X, ALU.max) \
                   .then_inc(ms_max, 1)
                dve.wait_ge(ms_max, of_tile(t, 2, 1))
                dve.tensor_scalar(nmx[:, 0:4], mx[:, 0:4], -MEM_SCALE, None, ALU.mult).then_inc(ms_max, 1)

            def mem_values(t):
                dve.wait_ge(mp_ready, of_tile(t, 1, 1))
                note(dve.reciprocal(linv[:, 0:4], lsum[:, 0:4]))
                settle(t)
                dve.wait_ge(mo_ready, of_tile(t, 1, 1))
                dve.tensor_tensor(row_a[:, :].rearrange("p (h d) -> p h d", d=MEM_DIM),
                                  g23.rearrange("p (h d) -> p h d", d=MEM_DIM),
                                  linv[:, 0:4].unsqueeze(2).to_broadcast([P, MEM_HEADS, MEM_DIM]), ALU.mult) \
                   .then_inc(mo_row, 1)

            def mem_out(t):
                dve.wait_ge(w_used, used_after(t, 5 * KT))
                dve.tensor_tensor(h[:, :], h[:, :], g01, ALU.add).then_inc(h_remembered, 1)

            def peer_norm(t):
                if first_of(t):
                    dve.wait_ge(loaded["experts"], 64)
                dve.wait_ge(root_ready, of_tile(t, 4, 4))
                note(dve.reciprocal(rinv[:, 3:4], root[:, 3:4]))
                settle(t)
                dve.scalar_tensor_tensor(row_a[:, :], h[:, :], rinv[:, 3:4], ffn_g[:, :], ALU.mult, ALU.mult) \
                   .then_inc(hn_ready, 1)
                dve.tensor_copy(h_kept[:, :], h[:, :]).then_inc(h_taken, 1)

            def next_input(t):
                dve.wait_ge(hn_ready, of_tile(t, 1, 1))
                dve.tensor_copy(hn[:, :], row_a[:, :]).then_inc(hn_taken, 1)
                hold(dve, dve_granted, hn_taken, of_tile(t, 1, 1))

            def best_16(t, values, indices, source, many):
                for s in many:
                    note(dve.max(values[:, s, 0:8], source[:, s, :]))
                settle_held(t)
                for s in many:
                    dve.max_index(indices[:, s, 0:8], values[:, s, 0:8], source[:, s, :])
                    note(dve.match_replace(source[:, s, :], values[:, s, 0:8], source[:, s, :], LOWEST))
                settle_held(t)
                for s in many:
                    note(dve.max(values[:, s, 8:16], source[:, s, :]))
                settle_held(t)
                for s in many:
                    note(dve.max_index(indices[:, s, 8:16], values[:, s, 8:16], source[:, s, :]))

            N_CHOICE = N_HEAD // 2

            def heads_of(quarter):
                return slice(quarter * N_CHOICE, (quarter + 1) * N_CHOICE)

            def sub_topk(t, half, quarter):
                hold(dve, dve_granted, sub_saved, of_tile(t, 4, 2 * half + quarter + 1))
                best_16(t, top_v, top_i, scores, range(4 * quarter, 4 * quarter + 4))

            def candidates(t, half, quarter):
                settle(t)
                n4 = [P, N_CHOICE, TOPK, TOPK]
                sets = slice(4 * quarter, 4 * quarter + 4)
                halves = top_v[:, sets, :].rearrange("p (h c) k -> p c h k", c=2)
                note(dve.tensor_tensor(cand[:, heads_of(quarter)], halves[:, 0, :, :].unsqueeze(3).to_broadcast(n4),
                                       halves[:, 1, :, :].unsqueeze(2).to_broadcast(n4), ALU.add))
                note(dve.tensor_copy(top_f[:, sets, :], top_i[:, sets, :]))
                settle_held(t)

            def best(t, half, quarter):
                heads = heads_of(quarter)
                best_16(t, best_v, best_p, cand_h, range(heads.start, heads.stop))

            def gates(t, half, quarter):
                settle(t)
                n3 = [P, N_CHOICE, TOPK]
                heads = heads_of(quarter)
                here = slice(heads.start * TOPK, heads.stop * TOPK)
                gate3 = gate[:, slots_of(half, quarter)].rearrange("p (h k) -> p h k", k=TOPK)
                dve.tensor_tensor(gate3, best_v[:, heads, :], best_v[:, heads, 0:1].to_broadcast(n3), ALU.subtract) \
                   .then_inc(best_shifted, 1)
                flat = best_p[:, heads, :].rearrange("p h k -> p (h k)")
                dve.tensor_scalar(pos_u[:, 0, here], flat, 4, None, ALU.logical_shift_right)
                note(dve.tensor_scalar(pos_u[:, 1, here], flat, 15, None, ALU.bitwise_and))
                settle(t)
                note(dve.tensor_copy(pos_f[:, :, here], pos_u[:, :, here]))
                dve.wait_ge(best_exp, of_tile(t, 4, 2 * half + quarter + 1))
                note(dve.tensor_reduce(mx[:, 0:N_CHOICE], gate3, AX.X, ALU.add))
                settle(t)
                note(dve.reciprocal(linv[:, 0:N_CHOICE], mx[:, 0:N_CHOICE]))
                settle(t)
                note(dve.tensor_tensor(gate3, gate3, linv[:, 0:N_CHOICE].unsqueeze(2).to_broadcast(n3), ALU.mult))

            def indices(t, half, quarter, c):
                n4 = [P, N_CHOICE, TOPK, TOPK]
                heads = heads_of(quarter)
                here = slice(heads.start * TOPK, heads.stop * TOPK)
                tops = top_f[:, 4 * quarter:4 * quarter + 4, :].rearrange("p (h c) k -> p c h k", c=2)
                places = iota[:, :].unsqueeze(1).unsqueeze(1).to_broadcast(n4)
                pos = pos_f[:, c, here].rearrange("p (h k) -> p h k", k=TOPK).unsqueeze(3).to_broadcast(n4)
                mask4 = onehot[:, heads]
                done_before = 4 * half + 2 * quarter + c
                settle(t)
                if done_before:
                    dve.wait_ge(picked_ready, of_tile(t, 8, done_before))
                note(dve.tensor_tensor(mask4, pos, places, ALU.is_equal))
                settle(t)
                note(dve.tensor_tensor(mask4, mask4, tops[:, c, :, :].unsqueeze(2).to_broadcast(n4), ALU.mult))
                settle(t)
                dve.tensor_reduce(picked[:, c, here].rearrange("p (h k) -> p h k", k=TOPK), mask4, AX.X, ALU.add) \
                   .then_inc(picked_ready, 1)

            def publish(t, half, quarter):
                heads = heads_of(quarter)
                here = slice(heads.start * TOPK, heads.stop * TOPK)
                dve.wait_ge(picked_ready, of_tile(t, 8, 4 * half + 2 * quarter + 2))
                if not first_of(t):
                    dve.wait_ge(idx_staged, v_sequence(t - 1, (2 * half + quarter + 1) * QUARTER - 1))
                dve.scalar_tensor_tensor(idx[:, slots_of(half, quarter)], picked[:, 0, here], float(KEYS),
                                         picked[:, 1, here], ALU.mult, ALU.add).then_inc(idx_ready, 1)

            def u_group(t, group, part, sequence=None):
                for r in PARTS[part]:
                    dve.wait_ge(landed[r], (u_sequence(t, group) if sequence is None else sequence) * 16)
                    dve.tensor_tensor_reduce(out=ring[:, r, :], in0=ring[:, r, :], in1=hn[:, :], scale=1.0, scalar=0.0,
                                             op0=ALU.mult, op1=ALU.add, accum_out=a_group[:, r:r + 1]) \
                       .then_inc(u_used, 1)
                if part == 0:
                    return
                hold(dve, dve_granted, u_used, of_tile(t, SLOTS, RING) + group * RING)
                dve.tensor_copy(a_all[:, bass.ds(group * RING, RING)], a_group[:, :]).then_inc(a_copied, 1)
                hold(dve, dve_granted, a_copied, of_tile(t, GROUPS, 1) + group)

            def weigh(t, half):
                if half:
                    if first_of(t):
                        return
                    t = t - 1
                dve.wait_ge(gelu_ready, of_tile(t, 2, half + 1))
                part = slice(half * SLOTS // 2, (half + 1) * SLOTS // 2)
                dve.tensor_tensor(weight[:, part], gelu_a[:, part], gate[:, part], ALU.mult).then_inc(weight_ready, 1)
                hold(dve, dve_granted, weight_ready, of_tile(t, 2, half + 1))

            def v_group(t, group, part, first=False, last_tile=False):
                for j, r in enumerate(BY_DVE):
                    if r not in PARTS[part]:
                        continue
                    dve.wait_ge(landed[r], v_sequence(t, group, last_tile) * 16)
                    before = h_kept if first and j == 0 else y_acc
                    if first and j == 0:
                        dve.wait_ge(h_taken, of_tile(t, 1, 1))
                    dve.scalar_tensor_tensor(y_acc[:, :], ring[:, r, :], weight[:, bass.ds(group * RING + r, 1)],
                                             before[:, :], ALU.mult, ALU.add).then_inc(v_used_dve, 1)
                    hold(dve, dve_granted, v_used_dve, v_count(t, group, BY_DVE, j + 1))

            def finish(t, part):
                if first_of(t):
                    return
                t = t - 1
                if part == 0:
                    dve.wait_ge(v_used_pe, v_count(t, GROUPS, BY_PE, 0))
                    dve.wait_ge(stored, of_tile(t, 16, 16))
                    dve.tensor_tensor(y_row[:, :], acc[:, :], y_acc[:, :], ALU.add).then_inc(y_ready, 1)
                    return
                dve.wait_ge(y_root_ready, of_tile(t, 2, 2))
                dve.reciprocal(f_rinv, f_root).then_inc(y_normed, 1)
                dve.wait_ge(y_normed, of_tile(t, 2, 1))
                dve.scalar_tensor_tensor(y_row[:, :], y_row[:, :], f_rinv, final_g[:, :], ALU.mult, ALU.mult) \
                   .then_inc(y_normed, 1)

            stages = dict(inputs=inputs, latents=latents, conv_input=conv_input, rotate=rotate, head=head,
                          memory_input=memory_input, memory=memory, conv=conv, attended=attended,
                          conv_norm=conv_norm, mix_out=mix_out,
                          mem_norm=mem_norm, mem_scores=mem_scores, mem_values=mem_values, mem_out=mem_out,
                          peer_norm=peer_norm, next_input=next_input, sub_topk=sub_topk, candidates=candidates,
                          best=best, gates=gates, indices=indices, publish=publish, weigh=weigh,
                          finish=finish)

            def run(t, steps, u=None, v=None):
                groups = {"u rows": u, "v rows": v}
                passed = dict.fromkeys(groups, 0)
                for name, *args in steps:
                    at[0] = name == "next tile"
                    if name in groups:
                        if groups[name]:
                            groups[name](passed[name], args[0])
                        passed[name] += args[0]
                    elif at[0] and args[0] in stages:
                        stages[args[0]](t + 1, *args[1:])
                    elif name in stages:
                        stages[name](t, *args)

            def tile(t, late):
                run(t + 1, EARLY, u=lambda k, part: u_group(t, k + HALF_GROUPS + 1, part),
                    v=lambda k, part: v_group(t, k, part, first=k == 0))
                run(t + 1, late, u=lambda k, part: u_group(t + 1, k, part),
                    v=lambda k, part: v_group(t, k + HALF_GROUPS, part))
                next_tile()

            run(0, FIRST)
            run(0, LATE_FIRST, u=lambda k, part: u_group(0, k, part, u_sequence_start(k) if k < HALF_GROUPS else None))
            next_tile()
            with dve.Fori(0, TILES - 2) as t:
                tile(t, LATE)
            tile(TILES - 2, LATE_LAST)
            for part in range(2):
                v_group(TILES - 1, 0, part, first=True)
            with dve.Fori(1, HALF_GROUPS) as k:
                for part in range(2):
                    u_group(TILES - 1, k + HALF_GROUPS, part)
                for part in range(2):
                    v_group(TILES - 1, k, part)
            weigh(TILES, 1)
            with dve.Fori(HALF_GROUPS, GROUPS) as group:
                for part in range(2):
                    v_group(TILES - 1, group, part, last_tile=True)
            finish(TILES, 0)
            finish(TILES, 1)

        @block.tensor
        def _(pe):
            def fill(t, n, blocks, rows=P, number=None):
                number = bank_number(t, n) if number is None else number
                if not isinstance(number, int) or number >= 2:
                    pe.wait_ge(drained, number - 1)
                for b, src in enumerate(blocks):
                    last = pe.transpose(tp[0:rows, n % 2, b * P:(b + 1) * P], src, ident[:, :])
                last.then_inc(filled, 1)

            def is_drained(t, n):
                pe.wait_ge(drained, bank_number(t, n) + 1)

            def use(t, n, lhs, outs):
                pe.wait_ge(w_landed[place(t, n)], landed_value(t, n))
                for o, col, cols, start, stop in outs:
                    last = pe.matmul(o, lhs, wring[:, place(t, n), col:col + cols], start=start, stop=stop)
                last.then_inc(w_used, 1)

            def gemm(t, first, lhs_of, banks, part):
                for k in range(part * KT // 2, (part + 1) * KT // 2):
                    use(t, first + k, lhs_of(k), [(banks[n], 512 * n, 512, k == 0, k == KT - 1) for n in range(2)])

            pe.wait_ge(zeroed, 5)

            def memory(t, half):
                if half == 0:
                    pe.wait_ge(memT_scaled, 1)
                    pe.wait_ge(s_masked, 2 * HEADS)
                else:
                    pe.wait_ge(attn_ready, 1)
                    pe.wait_ge(mem_saved, 2)
                for k in range(KT):
                    c = W_BEFORE_MEMORY + half * KT + k
                    pe.wait_ge(w_landed[c % WRING], 16 * (c // WRING + 1))
                    for m in range(MEM_TILES):
                        for b in range(2):
                            bank = acc[:, b * 512:(b + 1) * 512] if m else g[:, 2 * half + b, :]
                            last = pe.matmul(bank, memn_t[:, k, m * P:(m + 1) * P],
                                             wring[:, c % WRING, b * 512:(b + 1) * 512], start=k == 0, stop=k == KT - 1)
                    last.then_inc(w_used, 1)

            def memory_keys(t):
                pe.wait_ge(mem_saved, 2)
                for q in range(4):
                    fill(0, q, [mem_k_row[:, q // 2, (4 * (q % 2) + b) * P:(4 * (q % 2) + b + 1) * P]
                                for b in range(4)], number=T_HMEM + q)

            def latent_query(t):
                pe.wait_ge(x_scaled, of_tile(t, 1, 1))
                if not first_of(t):
                    pe.wait_ge(sub_saved, of_tile(t, 4, 0))
                for k in range(KT):
                    use(t, k, tb[:, k, :], [(g[:, 0, 0:LATENT], 0, LATENT, k == 0, k == KT - 1)])

            def project(t, part=None):
                if part is not None:
                    gemm(t, KT, lambda k: tb[:, k, :], (g[:, 1, :], g[:, 2, :]), part)

            def latents(t):
                pe.wait_ge(lat_normed, of_tile(t, 1, 1))
                if first_of(t):
                    pe.wait_ge(loaded["latents"], 16 * 3)
                fill(t, T_LATENT, [lat_row[:, b * P:(b + 1) * P] for b in range(3)])

            def conv_input(t):
                pe.wait_ge(u_ready, of_tile(t, 1, 1))
                if not isinstance(t, int):
                    pe.wait_ge(hist_read, t)
                fill(t, T_CONV, [u_row[:, b * P:(b + 1) * P] for b in range(4)])

            def up(t):
                if first_of(t):
                    pe.wait_ge(loaded["mixer"], 16 * 4)
                is_drained(t, T_LATENT)
                pe.wait_ge(k_rope_copied, of_tile(t, 1, 1))
                for k in range(2):
                    pe.matmul(g[:, 3, 0:5 * QK], lat_t[:, k, :], w_q_up[:, k, 0:5 * QK], start=k == 0, stop=k == 1)
                    last = pe.matmul(g[:, 0, 0:3 * QK], lat_t[:, k, :], w_q_up[:, k, 5 * QK:], start=k == 0,
                                     stop=k == 1)
                last.then_inc(up_ready, 1)
                for b in range(2):
                    last = pe.matmul(g[:, 1 + b, :], lat_t[:, 2, :], w_kv_up[:, b * 512:(b + 1) * 512],
                                     start=True, stop=True)
                last.then_inc(up_ready, 1)

            def rotate(t):
                pe.wait_ge(roped, of_tile(t, 2, 1))
                for n in range(2):
                    fill(t, T_Q + n, [qk[:, 4 * n + b, :] for b in range(4)], rows=QK)
                pe.wait_ge(roped, of_tile(t, 2, 2))
                pe.wait_ge(up_saved, of_tile(t, 3, 3))
                for n in range(2):
                    fill(t, T_K + n, [kfull[:, 4 * n + b, :] for b in range(4)], rows=QK)

            def scores_of(t, n):
                if n == 0:
                    is_drained(t, T_K + 1)
                else:
                    if n >= 2:
                        pe.wait_ge(s_masked, of_tile(t, 2 * HEADS, 2 * (n - 2) + 1))
                pe.matmul(g[:, n % 2, :], q_t[0:QK, n, :], key_cache[0:QK, n, :], start=True, stop=True) \
                  .then_inc(s_ready, 1)

            def values_of(t, n):
                is_drained(t, T_P + n)
                for j in range(TILES):
                    last = pe.matmul(g[:, 2, n * VDIM:(n + 1) * VDIM], probs_t[:, n % 2, j, :],
                                     value_cache[:, j, n * VDIM:(n + 1) * VDIM], start=j == 0, stop=j == TILES - 1)
                last.then_inc(pv_done, 1)

            def head(t, n):
                if n == 0:
                    scores_of(t, 0)
                if n + 1 < HEADS:
                    scores_of(t, n + 1)
                pe.wait_ge(p_ready, of_tile(t, HEADS, n + 1))
                fill(t, T_P + n, [probs[:, n % 2, j * P:(j + 1) * P] for j in range(TILES)])
                if n:
                    values_of(t, n - 1)
                if n == HEADS - 1:
                    values_of(t, n)

            def conv(t, n):
                if first_of(t):
                    return
                if n == 0:
                    is_drained(t, T_CONV)
                    pe.wait_ge(up_saved, of_tile(t, 3, 1))
                for b in batches(n):
                    pe.wait_ge(taps_ready, of_tile(t - 1, BATCHES, b + 1))
                    for j, (c, k) in enumerate(pairs(b)):
                        last = pe.matmul(g[:, 3, c * P:(c + 1) * P], tap_diag[:, b % 2 * TAP_BATCH + j, :],
                                         u_t[:, c, k:k + P], start=k == 0, stop=k == TAPS - 1)
                    last.then_inc(taps_used, 1)

            def attended(t):
                pe.wait_ge(attn_ready, of_tile(t, 1, 1))
                for n in range(2):
                    fill(t, T_ATTN + n, [row_b[:, (2 * n + b) * P:(2 * n + b + 1) * P] for b in range(2)])

            def conv_norm(t):
                pe.wait_ge(hist_read, of_tile(t, 1, 1))
                if first_of(t):
                    pe.wait_ge(mem_saved, 2 * MEM_TILES)
                for c in range(CT):
                    last = pe.matmul(g[:, 3, 0:P], mean_w[:, :], conv_acc[:, c, :], start=c == 0, stop=c == CT - 1)
                last.then_inc(stat_ready, 1)
                pe.wait_ge(squared, of_tile(t, 1, 1))
                for c in range(CT):
                    last = pe.matmul(g[:, 3, P:2 * P], mean_w[:, :], conv_acc[:, c, :], start=c == 0, stop=c == CT - 1)
                last.then_inc(stat_ready, 1)

            def mix_out(t, part=None):
                if part == 0:
                    is_drained(t, T_ATTN + 1)
                    pe.wait_ge(s_masked, of_tile(t, 2 * HEADS, 2 * HEADS))
                if part == 1:
                    pe.wait_ge(cat_ready, of_tile(t, 1, 1))
                if part is not None:
                    gemm(t, 2 * KT, lambda k: ta[:, k, :], (g[:, 0, :], g[:, 1, :]), part)

            def mem_norm(t):
                pe.wait_ge(h_row, of_tile(t, 1, 1))
                for n in range(2):
                    fill(t, T_HMEM + n, [row_a[:, (4 * n + b) * P:(4 * n + b + 1) * P] for b in range(4)])

            def mem_query(t, part=None):
                if part is not None:
                    is_drained(t, T_HMEM + 1)
                    gemm(t, 3 * KT, lambda k: ta[:, k, :], (g[:, 2, :], g[:, 3, :]), part)
                    return
                pe.wait_ge(mq_saved, of_tile(t, 1, 1))
                for n in range(2):
                    fill(t, T_QMEM + n, [row_b[:, (4 * n + b) * P:(4 * n + b + 1) * P] for b in range(4)])

            def mem_scores(t):
                is_drained(t, T_QMEM + 1)
                for n in range(MEM_HEADS):
                    for k in range(2):
                        last = pe.matmul(g[:, n // 2, (n % 2) * N_MEM:(n % 2 + 1) * N_MEM], tb[:, 2 * n + k, :],
                                         mem_kT[:, 2 * n + k, :], start=k == 0, stop=k == 1)
                last.then_inc(ms_ready, 1)

            def mem_values(t):
                pe.wait_ge(mp_ready, of_tile(t, 1, 1))
                for n in range(2):
                    fill(t, T_PMEM + n, [row_b[:, (4 * n + b) * P:(4 * n + b + 1) * P] for b in range(4)])

                is_drained(t, T_PMEM + 1)
                for n in range(MEM_HEADS):
                    for m in range(MEM_TILES):
                        last = pe.matmul(g[:, 2 + n // 2, (n % 2) * MEM_DIM:(n % 2 + 1) * MEM_DIM], tb[:, 2 * n + m, :],
                                         mem_v[:, m, n * MEM_DIM:(n + 1) * MEM_DIM], start=m == 0, stop=m == 1)
                last.then_inc(mo_ready, 1)
                pe.wait_ge(mo_row, of_tile(t, 1, 1))
                for n in range(2):
                    fill(t, T_OMEM + n, [row_a[:, (4 * n + b) * P:(4 * n + b + 1) * P] for b in range(4)])

            def mem_out(t, part=None):
                if part is not None:
                    is_drained(t, T_OMEM + 1)
                    gemm(t, 4 * KT, lambda k: ta[:, k, :], (g[:, 0, :], g[:, 1, :]), part)

            def peer_norm(t):
                pe.wait_ge(hn_ready, of_tile(t, 1, 1))
                for n in range(2):
                    fill(t, T_HFFN + n, [row_a[:, (4 * n + b) * P:(4 * n + b + 1) * P] for b in range(4)])

            def peer_query(t, half, part=None):
                if part is not None:
                    is_drained(t, T_HFFN + 1)
                    if half:
                        pe.wait_ge(pq_saved, of_tile(t, 2, 1))
                    gemm(t, (5 + half) * KT, lambda k: ta[:, k, :], (g[:, 2, :], g[:, 3, :]), part)
                    return
                pe.wait_ge(pq_saved, of_tile(t, 2, half + 1))
                for n in range(2):
                    fill(t, T_QPEER + 2 * half + n, [row_b[:, (4 * n + b) * P:(4 * n + b + 1) * P] for b in range(4)])

            def sub_scores(t, half):
                if first_of(t):
                    pe.wait_ge(loaded["experts"], 64)
                is_drained(t, T_QPEER + 2 * half + 1)
                if half:
                    pe.wait_ge(sub_saved, of_tile(t, 4, 2))
                for n in range(2):
                    for b in range(4):
                        last = pe.matmul(g[:, n, b * P:(b + 1) * P], qp_t[:, 4 * n + b, :],
                                         sub_keysT[:, 8 * half + 4 * n + b, :], start=True, stop=True)
                    last.then_inc(sub_ready, 1)

            def v_group(t, group, part, first=False, last=False, last_tile=False):
                if first and part == 0:
                    pe.wait_ge(y_ready, t + 1)
                for j, r in enumerate(BY_PE):
                    if r not in PARTS[part]:
                        continue
                    pe.wait_ge(landed[r], v_sequence(t, group, last_tile) * 16)
                    pe.wait_ge(diag_ready, of_tile(t, GROUPS * len(BY_PE), j + 1) + group * len(BY_PE))
                    for n in range(2):
                        ins = pe.matmul(acc[:, n * 512:(n + 1) * 512], diag[:, j, :], ring[:, r, n * 512:(n + 1) * 512],
                                        start=first and j == 0, stop=last and j == len(BY_PE) - 1)
                    ins.then_inc(v_used_pe, 1)

            stages = dict(latent_query=latent_query, project=project, latents=latents, conv_input=conv_input, up=up,
                          rotate=rotate, head=head, memory=memory, memory_keys=memory_keys, conv=conv, attended=attended,
                          conv_norm=conv_norm,
                          mix_out=mix_out, mem_norm=mem_norm, mem_query=mem_query, mem_scores=mem_scores,
                          mem_values=mem_values, mem_out=mem_out, peer_norm=peer_norm, peer_query=peer_query,
                          sub_scores=sub_scores)

            def step(t, name, *args):
                if name == "part":
                    stages[args[1]](t, *args[2:], part=args[0])
                elif name in stages:
                    stages[name](t, *args)

            def run(t, steps, v=None):
                k = 0
                for name, *args in steps:
                    if name == "v rows":
                        if v:
                            v(k, args[0])
                        k += args[0]
                    elif name == "next tile":
                        step(t + 1, *args)
                    else:
                        step(t, name, *args)

            def tile(t, late):
                run(t + 1, EARLY, v=lambda k, part: v_group(t, k, part, first=k == 0))
                run(t + 1, late, v=lambda k, part: v_group(t, k + HALF_GROUPS, part, last=k == HALF_GROUPS - 1))

            run(0, FIRST)
            run(0, LATE_FIRST)
            with pe.Fori(0, TILES - 2) as t:
                tile(t, LATE)
            tile(TILES - 2, LATE_LAST)
            for part in range(2):
                v_group(TILES - 1, 0, part, first=True)
            with pe.Fori(1, HALF_GROUPS) as k:
                for part in range(2):
                    v_group(TILES - 1, k, part)
            with pe.Fori(HALF_GROUPS, GROUPS - 1) as group:
                for part in range(2):
                    v_group(TILES - 1, group, part, last_tile=True)
            for part in range(2):
                v_group(TILES - 1, GROUPS - 1, part, last=True, last_tile=True)


def kernel(**inputs):
    import numpy as np
    import concourse.bacc as bacc
    from concourse import mybir as mb
    from concourse.bass_utils import run_bass_kernel_spmd

    def columns(v):
        return np.ascontiguousarray(np.asarray(v).reshape(-1, P).T)

    a = {k: np.asarray(v) for k, v in inputs.items()}
    x = a["x"][0]
    arrays = {
        "x": x,
        "xT": np.ascontiguousarray(x.reshape(TILES, P, KT, P).transpose(0, 3, 2, 1)).reshape(TILES * P, KT, P),
        "mem": a["mem"][0],
        "memT": np.ascontiguousarray(a["mem"][0].reshape(N_MEM, KT, P).transpose(2, 1, 0)),
        "mix_gT": columns(a["norm_mix_g"][0]), "mem_gT": columns(a["norm_mem_g"][0]),
        "memkv_gT": columns(a["mem_kv_norm_g"][0]),
        "q_latent_g": a["q_latent_g"], "kv_latent_g": a["kv_latent_g"],
        "norm_ffn_g": a["norm_ffn_g"], "final_norm_g": a["final_norm_g"].reshape(1, D),
        "conv_wT": np.ascontiguousarray(a["conv_w"][0, :, 0, :].reshape(TAPS, CT, P).transpose(2, 1, 0)),
        "conv_p": np.stack([a[n][0].reshape(CT, P).T for n in ("conv_b", "conv_ln_g", "conv_ln_b")], 1),
        "w_in": a["w_in"][0], "w_q_up": a["w_q_up"][0], "w_kv_up": a["w_kv_up"][0], "w_mix_out": a["w_mix_out"][0],
        "w_mem_q": a["w_mem_q"][0], "w_mem_kv": a["w_mem_kv"][0], "w_mem_out": a["w_mem_out"][0],
        "w_peer_query": a["w_peer_query"][0],
        "sub_keysT": np.ascontiguousarray(a["peer_sub_keys"][0].transpose(3, 0, 1, 2)).reshape(P, SETS, KEYS),
        "peer_u": a["peer_u"][0], "peer_v": a["peer_v"][0],
    }
    arrays["ident"] = np.eye(P, dtype=np.float32)
    arrays["iota"] = np.arange(TOPK, dtype=np.float32).reshape(1, TOPK)
    inv = (1.0 / (np.float32(10000.0) ** (np.arange(0, ROPE, 2, dtype=np.float32) / np.float32(ROPE)))).astype(np.float32)
    ang = np.arange(SEQ, dtype=np.float32)[:, None] * inv[None, :]
    arrays["rope"] = np.stack([np.cos(ang), np.sin(ang)], 1).astype(np.float32)
    chunk = np.arange(SEQ) // 64
    arrays["mask"] = np.where(chunk[None, :] <= chunk[:, None], 0.0, -1e30).astype(np.float32)

    nc = bacc.Bacc("TRN2", target_bir_lowering=False, num_devices=1)
    arrays = {n: np.ascontiguousarray(v) for n, v in arrays.items()}
    dram = {n: nc.dram_tensor("in_" + n, v.shape, mb.dt.from_np(v.dtype), kind="ExternalInput").ap()
            for n, v in arrays.items()}
    out = nc.dram_tensor("out", (SEQ, D), mb.dt.float32, kind="ExternalOutput").ap()
    build(nc, dram, out)
    r = run_bass_kernel_spmd(nc, [{"in_" + n: v for n, v in arrays.items()}], core_ids=[0])
    return r.results[0]["out"].reshape(1, SEQ, D)
```
